# Optimizing a Trainium2 kernel written in Bass

```python
import math
import jax
import jax.numpy as jnp
from jax import lax
import numpy as np
import jax, jax.numpy as jnp

D_MODEL = 1024
BATCH = 1
SEQ = 256
DEPTH = 1

D_MIX = D_MODEL
SB_HEADS = 8
SB_HEAD_DIM = 64
SB_WIDTH = SB_HEADS * SB_HEAD_DIM
POOL_WINDOWS = (2, 4, 8, 16)
POOL_GROUPS = len(POOL_WINDOWS)
POOL_WIDTH = D_MIX - SB_WIDTH
POOL_GROUP_DIM = POOL_WIDTH // POOL_GROUPS
IN_PROJ_COLS = 3 * SB_WIDTH + POOL_WIDTH
Q_BLOCK = 128
N_MEM = 256
MEM_HEADS = 4
MEM_HEAD_DIM = D_MODEL // MEM_HEADS
N_EXPERTS = 32
TOP_K = 4
D_FF = D_MODEL
SWIGLU_LIMIT = 7.0
SWIGLU_ALPHA = 1.702
MOE_BLOCK = 128
RMS_EPS = 1e-5


def rmsnorm(x, g):
    xf = x.astype(jnp.float32)
    y = xf * lax.rsqrt(jnp.mean(xf * xf, axis=-1, keepdims=True) + RMS_EPS)
    return (y * g.astype(jnp.float32)).astype(x.dtype)

def stick_breaking_attention(q, k, v):
    seq = q.shape[2]
    scale = 1.0 / math.sqrt(q.shape[-1])
    outs = []
    for i in range(seq // Q_BLOCK):
        t0 = i * Q_BLOCK
        kv_len = t0 + Q_BLOCK
        qb = q[:, :, t0:kv_len]
        kb = k[:, :, :kv_len]
        vb = v[:, :, :kv_len]
        z = jnp.einsum('bhqd,bhkd->bhqk', qb, kb).astype(jnp.float32) * scale
        t_pos = t0 + jnp.arange(Q_BLOCK)
        s_pos = jnp.arange(kv_len)
        mask = s_pos[None, :] < t_pos[:, None]
        log_stay = jnp.where(mask, jax.nn.log_sigmoid(-z), 0.0)
        rev = lax.cumsum(log_stay, axis=3, reverse=True)
        after = jnp.concatenate([rev[..., 1:], jnp.zeros_like(rev[..., :1])], axis=-1)
        w = jnp.where(mask, jnp.exp(jax.nn.log_sigmoid(z) + after), 0.0)
        outs.append(jnp.einsum('bhqk,bhkd->bhqd', w.astype(vb.dtype), vb))
    return jnp.concatenate(outs, axis=2)

def multiscale_pool(u):
    seq = u.shape[1]
    uf = u.astype(jnp.float32)
    csum = jnp.cumsum(uf, axis=1)
    outs = []
    for g, win in enumerate(POOL_WINDOWS):
        cg = csum[:, :, g]
        shifted = jnp.pad(cg, ((0, 0), (win, 0), (0, 0)))[:, :seq]
        count = jnp.minimum(jnp.arange(seq) + 1, win).astype(jnp.float32)
        outs.append((cg - shifted) / count[None, :, None] - uf[:, :, g])
    return jnp.stack(outs, axis=2).astype(u.dtype)

def memory_cross_attention(h, m, w_q, w_kv, w_o):
    b, s, d = h.shape
    q = (h @ w_q).reshape(b, s, MEM_HEADS, MEM_HEAD_DIM)
    kv = m @ w_kv
    k = kv[..., :d].reshape(b, -1, MEM_HEADS, MEM_HEAD_DIM)
    v = kv[..., d:].reshape(b, -1, MEM_HEADS, MEM_HEAD_DIM)
    scores = jnp.einsum('bshd,bmhd->bhsm', q, k).astype(jnp.float32) / math.sqrt(MEM_HEAD_DIM)
    p = jax.nn.softmax(scores, axis=-1).astype(v.dtype)
    o = jnp.einsum('bhsm,bmhd->bshd', p, v).reshape(b, s, d)
    return o @ w_o

def moe_ffn(h, w_router, b_router, w1, b1, w2, b2):
    b, s, d = h.shape
    n_tok = b * s
    hf = h.reshape(n_tok, d)
    logits = (hf @ w_router + b_router).astype(jnp.float32)
    top_val, top_idx = lax.top_k(logits, TOP_K)
    gates = jax.nn.softmax(top_val, axis=-1)
    nk = n_tok * TOP_K
    flat_e = top_idx.reshape(nk)
    flat_tok = (jnp.arange(nk, dtype=jnp.int32) // TOP_K)
    flat_g = gates.reshape(nk)
    order = jnp.argsort(flat_e)
    sorted_e = flat_e[order]
    counts = jnp.bincount(flat_e, length=N_EXPERTS)
    padded = (counts + MOE_BLOCK - 1) // MOE_BLOCK * MOE_BLOCK
    start = jnp.cumsum(counts) - counts
    pend = jnp.cumsum(padded)
    pstart = pend - padded
    dest = pstart[sorted_e] + jnp.arange(nk) - start[sorted_e]
    n_rows = (nk + MOE_BLOCK - 1) // MOE_BLOCK * MOE_BLOCK + N_EXPERTS * MOE_BLOCK
    n_blk = n_rows // MOE_BLOCK
    row_tok = jnp.zeros((n_rows,), jnp.int32).at[dest].set(flat_tok[order])
    row_g = jnp.zeros((n_rows,), h.dtype).at[dest].set(flat_g[order].astype(h.dtype))
    blk_e = jnp.minimum(jnp.searchsorted(pend, jnp.arange(n_blk) * MOE_BLOCK, side='right'),
                        N_EXPERTS - 1)

    def expert_block(args):
        e, tok, g = args
        xb = hf[tok]
        gu = xb @ w1[e] + b1[e]
        gate = jnp.minimum(gu[:, :D_FF], SWIGLU_LIMIT)
        up = jnp.clip(gu[:, D_FF:], -SWIGLU_LIMIT, SWIGLU_LIMIT)
        act = (up + 1.0) * gate * jax.nn.sigmoid(SWIGLU_ALPHA * gate)
        return (act @ w2[e] + b2[e]) * g[:, None]

    y = lax.map(expert_block, (blk_e, row_tok.reshape(n_blk, MOE_BLOCK),
                               row_g.reshape(n_blk, MOE_BLOCK)))
    out = jnp.zeros((n_tok, d), h.dtype).at[row_tok].add(y.reshape(n_rows, d))
    return out.reshape(b, s, d)

def first_inputs(seed: int = 0) -> dict:
    key = jax.random.key(seed)
    ks = jax.random.split(key, 24)
    f32 = jnp.float32
    nrm = lambda k, shape, fan_in: jax.random.normal(k, shape, f32) * (fan_in ** -0.5)
    gain = lambda k, shape: 1.0 + 0.05 * jax.random.normal(k, shape, f32)
    L = DEPTH
    return {
        "x": jax.random.normal(ks[0], (BATCH, SEQ, D_MODEL), f32),
        "mem": jax.random.normal(ks[1], (BATCH, N_MEM, D_MODEL), f32),
        "g_mix": gain(ks[2], (L, D_MODEL)),
        "w_in": nrm(ks[3], (L, D_MODEL, IN_PROJ_COLS), D_MODEL),
        "g_sb_out": gain(ks[4], (L, SB_WIDTH)),
        "g_pool_out": gain(ks[5], (L, POOL_WIDTH)),
        "w_pool": nrm(ks[6], (L, POOL_GROUPS, POOL_GROUP_DIM, POOL_GROUP_DIM), POOL_GROUP_DIM),
        "pool_scale": 1.0 + 0.1 * jax.random.normal(ks[7], (L, POOL_WIDTH), f32),
        "w_out": nrm(ks[8], (L, D_MIX, D_MODEL), D_MIX),
        "g_mem_q": gain(ks[9], (L, D_MODEL)),
        "g_mem_kv": gain(ks[10], (L, D_MODEL)),
        "w_mem_q": nrm(ks[11], (L, D_MODEL, D_MODEL), D_MODEL),
        "w_mem_kv": nrm(ks[12], (L, D_MODEL, 2 * D_MODEL), D_MODEL),
        "w_mem_o": nrm(ks[13], (L, D_MODEL, D_MODEL), D_MODEL),
        "g_ffn": gain(ks[14], (L, D_MODEL)),
        "w_router": nrm(ks[15], (L, D_MODEL, N_EXPERTS), D_MODEL),
        "b_router": 0.01 * jax.random.normal(ks[16], (L, N_EXPERTS), f32),
        "w_expert_in": nrm(ks[17], (L, N_EXPERTS, D_MODEL, 2 * D_FF), D_MODEL),
        "b_expert_in": 0.01 * jax.random.normal(ks[18], (L, N_EXPERTS, 2 * D_FF), f32),
        "w_expert_out": nrm(ks[19], (L, N_EXPERTS, D_FF, D_MODEL), D_FF),
        "b_expert_out": 0.01 * jax.random.normal(ks[20], (L, N_EXPERTS, D_MODEL), f32),
        "g_final": gain(ks[21], (D_MODEL,)),
    }

def first_block(x, mem, g_mix, w_in, g_sb_out, g_pool_out, w_pool, pool_scale, w_out,
              g_mem_q, g_mem_kv, w_mem_q, w_mem_kv, w_mem_o, g_ffn, w_router, b_router,
              w_expert_in, b_expert_in, w_expert_out, b_expert_out, g_final):
    b, s, d = x.shape
    for l in range(DEPTH):
        h = rmsnorm(x, g_mix[l])
        proj = h @ w_in[l]
        q = proj[..., :SB_WIDTH].reshape(b, s, SB_HEADS, SB_HEAD_DIM).transpose(0, 2, 1, 3)
        k = proj[..., SB_WIDTH:2 * SB_WIDTH].reshape(b, s, SB_HEADS, SB_HEAD_DIM).transpose(0, 2, 1, 3)
        v = proj[..., 2 * SB_WIDTH:3 * SB_WIDTH].reshape(b, s, SB_HEADS, SB_HEAD_DIM).transpose(0, 2, 1, 3)
        u = proj[..., 3 * SB_WIDTH:].reshape(b, s, POOL_GROUPS, POOL_GROUP_DIM)
        sb = stick_breaking_attention(q, k, v).transpose(0, 2, 1, 3).reshape(b, s, SB_WIDTH)
        pooled = multiscale_pool(u)
        pooled = jnp.einsum('bsgc,gce->bsge', pooled, w_pool[l]).reshape(b, s, POOL_WIDTH) * pool_scale[l]
        mixed = jnp.concatenate([rmsnorm(sb, g_sb_out[l]), rmsnorm(pooled, g_pool_out[l])], axis=-1)
        x = x + mixed @ w_out[l]
        x = x + memory_cross_attention(rmsnorm(x, g_mem_q[l]), rmsnorm(mem, g_mem_kv[l]),
                                       w_mem_q[l], w_mem_kv[l], w_mem_o[l])
        x = x + moe_ffn(rmsnorm(x, g_ffn[l]), w_router[l], b_router[l], w_expert_in[l],
                        b_expert_in[l], w_expert_out[l], b_expert_out[l])
    return rmsnorm(x, g_final)


PLE_DIM = 256
RMS_EPS_2 = 1e-6
A_HEAD_DIM = 64
A_HEADS = D_MODEL // 128
A_WIDTH = A_HEADS * A_HEAD_DIM
MOBA_BLOCK = 256
MOBA_TOPK = 3
Q_CHUNK = 16
REL_BUCKETS = 32
REL_MAX_EXACT = REL_BUCKETS // 2
REL_MAX_DIST = 128
B_HEAD_DIM = 64
B_HEADS = D_MODEL // 128
B_WIDTH = B_HEADS * B_HEAD_DIM
DECAY_RANK = 64
ICLR_RANK = 64
GN_EPS = 64e-5
A_COLS = 4 * A_WIDTH
RW_COLS = 4 * B_WIDTH + DECAY_RANK + ICLR_RANK
IN_COLS = A_COLS + RW_COLS + 2 * D_MODEL


def _rms_norm(x, g):
    xf = x.astype(jnp.float32)
    y = xf * lax.rsqrt(jnp.mean(xf * xf, axis=-1, keepdims=True) + RMS_EPS_2)
    return y * g.astype(jnp.float32)

def _t5_bucket(dist):
    n = jnp.maximum(dist, 0)
    nf = jnp.maximum(n, 1).astype(jnp.float32)
    large = REL_MAX_EXACT + (jnp.log(nf / REL_MAX_EXACT) / math.log(REL_MAX_DIST / REL_MAX_EXACT)
                             * (REL_BUCKETS - REL_MAX_EXACT)).astype(jnp.int32)
    large = jnp.minimum(large, REL_BUCKETS - 1)
    return jnp.where(n < REL_MAX_EXACT, n, large)

def _moba_attention(q, k, v, rel_bias):
    bsz, seq, nh, hd = q.shape
    n_blk = -(-seq // MOBA_BLOCK)
    pad = n_blk * MOBA_BLOCK - seq
    topk = min(MOBA_TOPK, n_blk)
    qh = jnp.swapaxes(q, 1, 2).astype(jnp.float32) * (hd ** -0.5)
    kh = jnp.pad(jnp.swapaxes(k, 1, 2).astype(jnp.float32), ((0, 0), (0, 0), (0, pad), (0, 0)))
    vh = jnp.pad(jnp.swapaxes(v, 1, 2).astype(jnp.float32), ((0, 0), (0, 0), (0, pad), (0, 0)))
    k_blk = kh.reshape(bsz, nh, n_blk, MOBA_BLOCK, hd)
    v_blk = vh.reshape(bsz, nh, n_blk, MOBA_BLOCK, hd)
    k_mean = jnp.mean(k_blk, axis=3)
    gate = jnp.einsum('bhsd,bhnd->bhsn', qh, k_mean)
    q_blk = jnp.arange(seq) // MOBA_BLOCK
    past = jnp.arange(n_blk)[None, :] < q_blk[:, None]
    gate = jnp.where(past[None, None], gate, -jnp.inf)
    _, sel = lax.top_k(gate, topk)
    bias_h = rel_bias.T.astype(jnp.float32)
    b_idx = jnp.arange(bsz)[:, None, None, None]
    h_idx = jnp.arange(nh)[None, :, None, None]
    offs = jnp.arange(MOBA_BLOCK)

    def chunk(c):
        t0 = c * Q_CHUNK
        pos = t0 + jnp.arange(Q_CHUNK)
        qb = t0 // MOBA_BLOCK
        qc = lax.dynamic_slice_in_dim(qh, t0, Q_CHUNK, axis=2)
        sc = lax.dynamic_slice_in_dim(sel, t0, Q_CHUNK, axis=2)
        ks = k_blk[b_idx, h_idx, sc]
        vs = v_blk[b_idx, h_idx, sc]
        key_pos = sc[..., None] * MOBA_BLOCK + offs
        dist = pos[None, None, :, None, None] - key_pos
        l_sel = jnp.einsum('bhqd,bhqkjd->bhqkj', qc, ks) + bias_h[h_idx[..., None], _t5_bucket(dist)]
        valid = (sc < qb)[..., None]
        l_sel = jnp.where(valid, l_sel, -jnp.inf).reshape(bsz, nh, Q_CHUNK, topk * MOBA_BLOCK)
        ko = lax.dynamic_index_in_dim(k_blk, qb, axis=2, keepdims=False)
        vo = lax.dynamic_index_in_dim(v_blk, qb, axis=2, keepdims=False)
        dist_o = pos[:, None] - (qb * MOBA_BLOCK + offs)[None, :]
        l_own = jnp.einsum('bhqd,bhjd->bhqj', qc, ko) + bias_h[:, _t5_bucket(dist_o)][None]
        l_own = jnp.where((dist_o >= 0)[None, None], l_own, -jnp.inf)
        probs = jax.nn.softmax(jnp.concatenate([l_sel, l_own], axis=-1), axis=-1)
        p_sel = probs[..., :topk * MOBA_BLOCK].reshape(bsz, nh, Q_CHUNK, topk, MOBA_BLOCK)
        p_own = probs[..., topk * MOBA_BLOCK:]
        return (jnp.einsum('bhqkj,bhqkjd->bhqd', p_sel, vs)
                + jnp.einsum('bhqj,bhjd->bhqd', p_own, vo))

    outs = lax.map(chunk, jnp.arange(seq // Q_CHUNK))
    return outs.transpose(1, 0, 3, 2, 4).reshape(bsz, seq, nh * hd)

def _rwkv7_time_mix(cols, mu, w0, w_up, a0, a_up, k_k, k_a, r_k, ln_w, ln_b):
    bsz, seq, _ = cols.shape
    cols = cols.astype(jnp.float32)
    prev = jnp.pad(cols, ((0, 0), (1, 0), (0, 0)))[:, :-1]
    cols = cols + (prev - cols) * mu.astype(jnp.float32)
    o = np.cumsum([0, B_WIDTH, B_WIDTH, B_WIDTH, B_WIDTH, DECAY_RANK])
    r, k, v, z = (cols[..., o[j]:o[j + 1]] for j in range(4))
    wd = cols[..., o[4]:o[5]]
    ad = cols[..., o[5]:]
    w_log = -jax.nn.softplus(-(w0 + jnp.tanh(wd) @ w_up)) - 0.5
    decay = jnp.exp(-jnp.exp(w_log))
    a = jax.nn.sigmoid(a0 + ad @ a_up)
    heads = lambda t: t.reshape(bsz, seq, B_HEADS, B_HEAD_DIM)
    kk = heads(k * k_k)
    kk = kk / jnp.maximum(jnp.linalg.norm(kk, axis=-1, keepdims=True), 1e-12)
    k = k * (1.0 + (a - 1.0) * k_a)
    rh, kh, vh, ah = heads(r), heads(k), heads(v), heads(a)
    xs = tuple(jnp.moveaxis(t, 1, 0) for t in (rh, heads(decay), kh, vh, -kk, kk * ah))

    def step(state, inp):
        r_t, w_t, k_t, v_t, a_t, b_t = inp
        sa = jnp.einsum('bhvk,bhk->bhv', state, a_t)
        state = (state * w_t[:, :, None, :] + sa[..., None] * b_t[:, :, None, :]
                 + v_t[..., None] * k_t[:, :, None, :])
        return state, jnp.einsum('bhvk,bhk->bhv', state, r_t)

    s0 = jnp.zeros((bsz, B_HEADS, B_HEAD_DIM, B_HEAD_DIM), jnp.float32)
    _, y = lax.scan(step, s0, xs)
    y = jnp.moveaxis(y, 0, 1)
    mean = jnp.mean(y, axis=-1, keepdims=True)
    var = jnp.mean(jnp.square(y - mean), axis=-1, keepdims=True)
    y = ((y - mean) * lax.rsqrt(var + GN_EPS)).reshape(bsz, seq, B_WIDTH) * ln_w + ln_b
    bonus = jnp.sum(rh * kh * r_k, axis=-1, keepdims=True) * vh
    y = y + bonus.reshape(bsz, seq, B_WIDTH)
    return y, z

def second_inputs(seed: int = 0) -> dict:
    key = jax.random.key(seed)
    ks = jax.random.split(key, 22)
    n = lambda k, s, sc: jax.random.normal(k, s, jnp.float32) * sc
    L = DEPTH
    return {
        "x": n(ks[0], (BATCH, SEQ, D_MODEL), 1.0),
        "p": n(ks[1], (DEPTH, BATCH, SEQ, PLE_DIM), 1.0),
        "g_pre": 1.0 + n(ks[2], (L, D_MODEL), 0.05),
        "w_in": n(ks[3], (L, D_MODEL, IN_COLS), D_MODEL ** -0.5),
        "rel_bias": n(ks[4], (REL_BUCKETS, A_HEADS), 0.5),
        "mu_shift": jax.random.uniform(ks[5], (L, RW_COLS), jnp.float32, 0.0, 1.0),
        "w0": jax.random.uniform(ks[6], (L, B_WIDTH), jnp.float32, -4.0, 1.0),
        "w_up": n(ks[7], (L, DECAY_RANK, B_WIDTH), 0.5 * DECAY_RANK ** -0.5),
        "a0": n(ks[8], (L, B_WIDTH), 0.5),
        "a_up": n(ks[9], (L, ICLR_RANK, B_WIDTH), 0.5 * ICLR_RANK ** -0.5),
        "k_k": 0.85 + n(ks[10], (L, B_WIDTH), 0.05),
        "k_a": 1.0 + n(ks[11], (L, B_WIDTH), 0.05),
        "r_k": n(ks[12], (L, B_HEADS, B_HEAD_DIM), 0.1),
        "ln_x_w": 1.0 + n(ks[13], (L, B_WIDTH), 0.05),
        "ln_x_b": n(ks[14], (L, B_WIDTH), 0.02),
        "p_a": n(ks[15], (L, A_WIDTH, D_MODEL), A_WIDTH ** -0.5),
        "p_b": n(ks[16], (L, B_WIDTH, D_MODEL), B_WIDTH ** -0.5),
        "w_out": n(ks[17], (L, D_MODEL, D_MODEL), D_MODEL ** -0.5),
        "g_post": 1.0 + n(ks[18], (L, D_MODEL), 0.05),
        "w_ple_up": n(ks[19], (L, PLE_DIM, D_MODEL), PLE_DIM ** -0.5),
        "w_ple_gate": n(ks[20], (L, D_MODEL, D_MODEL), D_MODEL ** -0.5),
    }

def second_block(x, p, g_pre, w_in, rel_bias, mu_shift, w0, w_up, a0, a_up, k_k, k_a, r_k,
              ln_x_w, ln_x_b, p_a, p_b, w_out, g_post, w_ple_up, w_ple_gate):
    bsz, seq, _ = x.shape
    h = x.astype(jnp.float32)
    for i in range(DEPTH):
        u = _rms_norm(h, g_pre[i]).astype(w_in.dtype)
        cols = u @ w_in[i]
        a_cols = cols[..., :A_COLS]
        b_cols = cols[..., A_COLS:A_COLS + RW_COLS]
        gate_a = cols[..., A_COLS + RW_COLS:A_COLS + RW_COLS + D_MODEL].astype(jnp.float32)
        gate_b = cols[..., A_COLS + RW_COLS + D_MODEL:].astype(jnp.float32)
        qa, ka, va, za = (a_cols[..., j * A_WIDTH:(j + 1) * A_WIDTH].reshape(bsz, seq, A_HEADS, A_HEAD_DIM)
                          for j in range(4))
        y_a = _moba_attention(qa, ka, va, rel_bias) * jax.nn.silu(za.reshape(bsz, seq, A_WIDTH).astype(jnp.float32))
        y_b, z_b = _rwkv7_time_mix(b_cols, mu_shift[i], w0[i], w_up[i], a0[i], a_up[i], k_k[i], k_a[i],
                                   r_k[i], ln_x_w[i], ln_x_b[i])
        y_b = y_b * jax.nn.silu(z_b)
        merged = (jax.nn.sigmoid(gate_a) * (y_a.astype(p_a.dtype) @ p_a[i])
                  + jax.nn.sigmoid(gate_b) * (y_b.astype(p_b.dtype) @ p_b[i]))
        y = merged.astype(w_out.dtype) @ w_out[i]
        h = h + _rms_norm(y, g_post[i])
        e = p[i] @ w_ple_up[i]
        h = h + jax.nn.sigmoid((h.astype(w_ple_gate.dtype) @ w_ple_gate[i]).astype(jnp.float32)) * e
    return h.astype(x.dtype)


def setup_inputs(seed=0):
    out = dict(first_inputs(seed))
    for name, value in second_inputs(seed + 1).items():
        if name != "x":
            out[name + "_2"] = value
    return out


def reference(
    x, mem, g_mix, w_in, g_sb_out, g_pool_out, w_pool, pool_scale, w_out, g_mem_q, g_mem_kv,
    w_mem_q, w_mem_kv, w_mem_o, g_ffn, w_router, b_router, w_expert_in, b_expert_in,
    w_expert_out, b_expert_out, g_final, p_2, g_pre_2, w_in_2, rel_bias_2, mu_shift_2, w0_2,
    w_up_2, a0_2, a_up_2, k_k_2, k_a_2, r_k_2, ln_x_w_2, ln_x_b_2, p_a_2, p_b_2, w_out_2,
    g_post_2, w_ple_up_2, w_ple_gate_2,
):
    x = first_block(
        x, mem, g_mix, w_in, g_sb_out, g_pool_out, w_pool, pool_scale, w_out, g_mem_q, g_mem_kv,
        w_mem_q, w_mem_kv, w_mem_o, g_ffn, w_router, b_router, w_expert_in, b_expert_in,
        w_expert_out, b_expert_out, g_final,
    )
    return second_block(
        x, p_2, g_pre_2, w_in_2, rel_bias_2, mu_shift_2, w0_2, w_up_2, a0_2, a_up_2, k_k_2,
        k_a_2, r_k_2, ln_x_w_2, ln_x_b_2, p_a_2, p_b_2, w_out_2, g_post_2, w_ple_up_2,
        w_ple_gate_2,
    )


_drawn_inputs = setup_inputs


def setup_inputs(seed=0):
    import zlib

    import numpy as np

    out = dict(_drawn_inputs(seed))
    spreads = {}
    factors = {'b_expert_in': 7.978, 'b_expert_out': 8.0, 'k_k_2': 3.45, 'ln_x_b_2': 4.35}
    for name, (base, spread) in spreads.items():
        noise = np.random.default_rng([zlib.crc32(name.encode()), seed]).standard_normal(out[name].shape)
        drawn = base * np.exp(spread * noise) if base else spread * noise
        out[name] = jnp.asarray(drawn.astype(out[name].dtype))
    for name, factor in factors.items():
        out[name] = (out[name] * factor).astype(out[name].dtype)
    return out
```

```python
import math
from contextlib import ExitStack

import numpy as np
import concourse.bass as bass
from concourse import mybir

D = 1024
S = 256
KT = D // 128
TH = S // 128
SLOTS = 12
SLOT = 2048
N_EXP = 32
CAP = 64
N_BLK = S // CAP
NEG = -1.0e30
HEADS = 8
HD = 64
L = 64
NCH = S // L
NSET = 4 * NCH
DECAY = math.exp(-0.5)

PARAMS = [("g_mix", 8), ("g_sb_out", 4), ("g_pool_out", 4), ("g_mem_q", 8), ("g_mem_kv", 8), ("g_ffn", 8),
          ("g_pre_2", 8), ("mu_shift_2", 17), ("w0_2", 4), ("a0_2", 4), ("k_k_2", 4), ("k_a_2", 4),
          ("r_k_2", 4), ("ln_x_w_2", 4), ("ln_x_b_2", 4)]
P_AT, _at = {}, 0
for _n, _r in PARAMS:
    P_AT[_n] = _at
    _at += _r
P_ROWS = _at

CONSTS = [("ident", 128), ("tri_ge", 128), ("tri_lt", 128), ("ones", 128), ("head_ones", 128), ("iota", 128),
          ("causal", 128), ("neg_diag", 128), ("iota32", 32), ("up_strict", 64), ("up_incl", 64),
          ("up_diag", 64), ("up_off", 64), ("low_diag", 64), ("eye64", 64), ("bias_sel", 512), ("inv_count", 1024), ("chunk_reset", 1024)]
C_AT, _at = {}, 0
for _n, _r in CONSTS:
    C_AT[_n] = (_at, _at + _r)
    _at += _r
C_COLS = _at
LATE = C_AT["iota32"][0]


def constants():
    c = np.zeros((128, C_COLS), np.float32)

    def put(name, value):
        c[:value.shape[0], C_AT[name][0]:C_AT[name][1]] = value

    p = np.arange(128)
    put("ident", np.eye(128))
    put("tri_ge", p[:, None] >= p[None, :])
    put("tri_lt", p[:, None] < p[None, :])
    put("ones", np.ones((128, 128)))
    put("head_ones", p[:, None] // HD == p[None, :] // HD)
    put("iota", np.tile(p % CAP, (128, 1)))
    put("causal", p[:, None] < p[None, :])
    put("neg_diag", np.where(p[:, None] < p[None, :], 0.0, NEG))
    put("iota32", np.tile(np.arange(32), (128, 1)))
    r, q = p[:, None] % L, np.arange(L)[None, :]
    put("up_strict", r < q)
    put("up_incl", r <= q)
    near = r // 16 == q // 16
    put("up_diag", (r < q) & near)
    put("up_off", (r < q) & ~near)
    put("low_diag", (r > q) & near)
    put("eye64", r == q)
    dist = 255 - np.arange(512)
    n = np.maximum(dist, 0)
    large = 16 + (np.log(np.maximum(n, 1).astype(np.float32) / np.float32(16)) / np.float32(math.log(8.0))
                  * np.float32(16)).astype(np.int32)
    bucket = np.where(n < 16, n, np.minimum(large, 31))
    sel = np.zeros((33, 512))
    sel[:32] = (np.arange(32)[:, None] == bucket[None, :]) & (dist >= 0)[None, :]
    sel[32] = np.where(dist >= 0, 0.0, NEG)
    put("bias_sel", sel)
    cnt = np.stack([1.0 / np.minimum(np.arange(S) + 1, w) for w in (2, 4, 8, 16)])
    put("inv_count", np.tile(cnt.reshape(1, -1), (128, 1)))
    put("chunk_reset", np.tile((np.arange(1024) % L != 0)[None, :], (128, 1)))
    return c


def two_blocks(nc, a, out):
    f32, i32, u32 = mybir.dt.float32, mybir.dt.int32, mybir.dt.uint32
    ALU, ACT = mybir.AluOpType, mybir.ActivationFunctionType
    AX = mybir.AxisListType.X
    ctx = ExitStack()
    with ctx:
        def sb(name, shape, dt=f32):
            return ctx.enter_context(nc.sbuf_tensor(name, shape, dt))

        ring = sb("ring", [128, SLOTS * SLOT])
        big = sb("big", [128, 10 * 2048])
        cst = sb("cst", [128, C_COLS])
        par_rows = sb("par_rows", [128, 128])
        par = sb("par", [128, 128])
        w_pool = sb("w_pool_sb", [128, 512])
        scale_bc = sb("scale_bc", [128, 512])
        w_router = sb("w_router_sb", [128, KT, N_EXP])
        b_router = sb("b_router_sb", [1, N_EXP])
        stat = sb("stat", [128, 96])
        eps = sb("eps", [128, 4])
        mstat = sb("mstat", [128, 64])
        dec_end = sb("dec_end", [128, NSET])
        lora_w = sb("lora_w", [128, 512])
        rbias = sb("rbias", [33, HEADS])
        lg = sb("lg", [128, TH, N_EXP])
        top8 = sb("top8", [128, TH, 8])
        idx8 = sb("idx8", [128, TH, 8], u32)
        idxf = sb("idxf", [128, TH, 8])
        hot = sb("hot", [128, TH, 4, N_EXP])
        mask = sb("mask", [128, TH, N_EXP])
        gate = sb("gate", [128, TH, N_EXP + 1])
        slot_of = sb("slot_of", [128, TH, N_EXP + 1])
        ov_slot = sb("ov_slot", [128, TH])
        flag = sb("flag", [1, 1], i32)

        def buf(n, lo=0, hi=2048):
            return big[:, 2048 * n + lo:2048 * n + hi]

        def slot(n, lo=0, hi=SLOT):
            return ring[:, SLOT * n + lo:SLOT * n + hi]

        def C(name):
            return cst[:, C_AT[name][0]:C_AT[name][1]]

        def P(name, k=0):
            return par[:, P_AT[name] + k:P_AT[name] + k + 1]

        def Pn(name, n, inner):
            return par[:, P_AT[name]:P_AT[name] + n].unsqueeze(2).to_broadcast([128, n, inner])

        def tk(ap, t):
            return ap.rearrange("p (k t) -> p k t", t=t)

        ident, ones = C("ident"), C("ones")
        X, HN = tk(buf(0), D), tk(buf(1), D)
        HT = tk(buf(2), S)
        qkT = tk(buf(3), S)
        v_rows = tk(buf(4, 0, 1024), 512)
        u_T = tk(buf(4, 1024), S)
        pooled = tk(buf(2, 0, 1024), S)
        win = [buf(2, 1024 + 256 * n, 1280 + 256 * n) for n in range(3)]
        Z = tk(big[:, 5 * 2048:5 * 2048 + 3072], 384)
        SP = tk(big[:, 5 * 2048 + 3072:8 * 2048], 384)
        mem_rows, memT = tk(buf(5), D), tk(buf(6), S)
        mkT, mv_rows = tk(buf(8), S), tk(buf(9), D)
        mqT = tk(buf(3), S)
        prob = tk(buf(5), S)
        probT = tk(buf(6), S)
        oT = tk(buf(7), S)
        xT_e = tk(buf(3, 0, 512), CAP)
        actT = buf(3, 512, 1024).rearrange("p (b h c) -> p b h c", b=4, h=2)
        y_e, gpT = buf(3, 1024, 1536), buf(3, 1536, 1792)
        g7, u7 = buf(4, 0, 512), buf(4, 512, 1024)
        sig, gu = buf(4, 1024, 1536), buf(4, 1536, 2048)
        act_e = buf(5, 0, 512)
        pick = tk(buf(5, 512, 640), CAP)
        gpick = tk(buf(5, 640, 896), 128)
        b2_all, gT = buf(6, 0, 1024), buf(6, 1024, 1280)
        b1_rows = C("inv_count")
        frow = buf(6, 1280, 1792)
        g_final, g_post = buf(8, 0, 1024), buf(8, 1024, 2048)
        bias = buf(9).rearrange("p (h b s) -> p h b s", h=HEADS, b=2)
        arr = [slot(s, lo, lo + 1024) for s in (8, 9, 10, 11, 0, 1, 2, 3) for lo in (0, 1024)]
        rwT = tk(big[:, 3 * 2048:5 * 2048], S)
        diff = tk(big[:, 5 * 2048:7 * 2048], S)
        qk2 = tk(buf(5), S)
        v2, za = tk(buf(6, 0, 1024), 512), tk(buf(6, 1024), S)
        lora, lora_d, lora_t = buf(7, 0, 256), buf(7, 256, 512), buf(7, 512, 768)
        z_sig = buf(7, 1024)
        p_rows, pT = tk(buf(8, 0, 512), 256), tk(buf(8, 512, 1024), S)
        gate_a, gate_b = tk(buf(1), S), tk(buf(2), S)
        prob2, prob2T = tk(ring[:, 0:3072], 384), tk(ring[:, 3072:6144], 384)
        ya = za
        rT, rw_k, rw_v, rw_z = buf(3, 0, 1024), buf(3, 1024), buf(4, 0, 1024), buf(4, 1024)
        sg, cum, dec, dec_inv, dec_prev, rate, kk, kk_sq = arr[:8]
        k2, kk_inv = arr[14:16]
        bon_in = buf(1, 0, 1024)
        bonus = cum
        aT, bT, kTl = dec_prev, rate, dec_inv
        v_tok, b_tok, k_tok, b0, a0, akT, rbT, rkT = arr[8:16]
        offT, E1, F1, t3, t4, t5, t6 = sg, dec, kk, kk_sq, buf(5, 0, 1024), buf(5, 1024), rw_k
        t7, invT = rate, dec_inv
        SOLVE_STEPS = [(b0, a0, 0, t3, None), (a0, b0, 0, t4, None), (t3, E1, 1, E1, E1), (t4, F1, 2, F1, F1),
                       (t4, t3, 2, t5, None), (t3, t4, 2, t6, None), (t5, E1, 5, E1, E1), (t6, F1, 6, F1, F1),
                       (t6, t5, 6, t3, None), (t5, t6, 6, t4, None), (t3, E1, 9, E1, E1), (t4, F1, 10, F1, F1),
                       (F1, offT, 12, t5, None), (offT, F1, 12, t6, None), (t6, E1, 14, t7, E1),
                       (t5, t6, 14, t3, None), (t3, t7, 16, invT, t7)]
        SOLVE = [x[:3] for x in SOLVE_STEPS]
        SOLVED = [x[3:] for x in SOLVE_STEPS]
        rec_rhs, rec_sa = tk(buf(7, 0, 256), HD), tk(buf(7, 256, 512), HD)
        state = tk(buf(7, 512, 768), HD), tk(buf(7, 768, 1024), HD)
        yT, ysq, ystd = sg, dec, kk
        yb = tk(yT, S)
        merged = tk(buf(5), S)
        pg_sig = tk(buf(5), D)

        PS = ctx.enter_context(nc.psum_tensor("PS", [128, 8, 512], f32))

        def banks(lo, n, t):
            return PS[:, lo:lo + n, :].rearrange("p b (k t) -> p (b k) t", t=t)

        def sem(name):
            return ctx.enter_context(nc.semaphore(name))

        s_x_loaded = sem("s_x_loaded")
        s_mem_loaded = sem("s_mem_loaded")
        s_ring_used = sem("s_ring_used")
        s_b1_loaded = sem("s_b1_loaded")
        s_flag_ready = sem("s_flag_ready")
        s_ov_sc = sem("s_ov_sc")
        s_ov_loaded = sem("s_ov_loaded")
        s_out_ready = sem("s_out_ready")
        s_out_written = sem("s_out_written")
        s_norm_tr = sem("s_norm_tr")
        s_const_loaded = sem("s_const_loaded")
        s_param_loaded = sem("s_param_loaded")
        s_params_T = sem("s_params_T")
        s_norm_rows = sem("s_norm_rows")
        s_params_cols = sem("s_params_cols")
        s_norm_T = sem("s_norm_T")
        s_kv_evac = sem("s_kv_evac")
        s_win_evac = sem("s_win_evac")
        s_z_done = sem("s_z_done")
        s_sp_ready = sem("s_sp_ready")
        s_rev_done = sem("s_rev_done")
        s_w_ready = sem("s_w_ready")
        s_sb_done = sem("s_sb_done")
        s_pooled_ready = sem("s_pooled_ready")
        s_small_loaded = sem("s_small_loaded")
        s_pool_done = sem("s_pool_done")
        s_memq_evac = sem("s_memq_evac")
        s_score_done = sem("s_score_done")
        s_p_ready = sem("s_p_ready")
        s_tr_p = sem("s_tr_p")
        s_pT_evac = sem("s_pT_evac")
        s_o_done = sem("s_o_done")
        s_oT_evac = sem("s_oT_evac")
        s_logits_done = sem("s_logits_done")
        s_late_loaded = sem("s_late_loaded")
        s_rbias_ready = sem("s_rbias_ready")
        s_frow_done = sem("s_frow_done")
        s_mask_ready = sem("s_mask_ready")
        s_rank_done = sem("s_rank_done")
        s_gates_ready = sem("s_gates_ready")
        s_gT_done = sem("s_gT_done")
        s_gT_evac = sem("s_gT_evac")
        s_b2_loaded = sem("s_b2_loaded")
        s_pe_ready = sem("s_pe_ready")
        s_gathered = sem("s_gathered")
        s_frow_evac = sem("s_frow_evac")
        s_xT_ready = sem("s_xT_ready")
        s_gu_free = sem("s_gu_free")
        s_gp_ready = sem("s_gp_ready")
        s_gpt_done = sem("s_gpt_done")
        s_act_ready = sem("s_act_ready")
        s_gpt_evac = sem("s_gpt_evac")
        s_actT_done = sem("s_actT_done")
        s_actT_evac = sem("s_actT_evac")
        s_y_evac = sem("s_y_evac")
        s_scattered = sem("s_scattered")
        s_ov_up = sem("s_ov_up")
        s_ov_down = sem("s_ov_down")
        s_lora_evac = sem("s_lora_evac")
        s_rw_evac = sem("s_rw_evac")
        s_a_evac = sem("s_a_evac")
        s_tanh_ready = sem("s_tanh_ready")
        s_wl_done = sem("s_wl_done")
        s_kk_sq = sem("s_kk_sq")
        s_kk_sum = sem("s_kk_sum")
        s_bon_in = sem("s_bon_in")
        s_bon_sum = sem("s_bon_sum")
        s_wl_sig = sem("s_wl_sig")
        s_bon_ready = sem("s_bon_ready")
        s_gate_evac = sem("s_gate_evac")
        s_moba_s = sem("s_moba_s")
        s_moba_p = sem("s_moba_p")
        s_moba_tr = sem("s_moba_tr")
        s_moba_pT = sem("s_moba_pT")
        s_moba_o = sem("s_moba_o")
        s_wkv_T = sem("s_wkv_T")
        s_ya_ready = sem("s_ya_ready")
        s_rows_done = sem("s_rows_done")
        s_rows_evac = sem("s_rows_evac")
        s_mat_evac = sem("s_mat_evac")
        s_mat_done = sem("s_mat_done")
        s_sol_ready = sem("s_sol_ready")
        s_sol_evac = sem("s_sol_evac")
        s_sol_done = sem("s_sol_done")
        s_rec_state = sem("s_rec_state")
        s_rec_x = sem("s_rec_x")
        s_rec_xe = sem("s_rec_xe")
        s_rec_sa = sem("s_rec_sa")
        s_rec_sae = sem("s_rec_sae")
        s_rec_s = sem("s_rec_s")
        s_y_psum = sem("s_y_psum")
        s_yT_evac = sem("s_yT_evac")
        s_gn_mean = sem("s_gn_mean")
        s_gn_sq = sem("s_gn_sq")
        s_gn_var = sem("s_gn_var")
        s_yb_ready = sem("s_yb_ready")
        s_merged_ready = sem("s_merged_ready")
        s_p_loaded = sem("s_p_loaded")
        s_ple_pT = sem("s_ple_pT")
        s_ple_pTe = sem("s_ple_pTe")
        s_h2_ready = sem("s_h2_ready")
        s_norm_sq = sem("s_norm_sq")
        s_norm_std = sem("s_norm_std")
        s_norm_rstd = sem("s_norm_rstd")
        s_eps_set = sem("s_eps_set")
        s_z_copied = sem("s_z_copied")
        s_z_abs = sem("s_z_abs")
        s_z_ln = sem("s_z_ln")
        s_arg_ready = sem("s_arg_ready")
        s_mix_sq = sem("s_mix_sq")
        s_pool_scaled = sem("s_pool_scaled")
        s_mix_std = sem("s_mix_std")
        s_mix_rstd = sem("s_mix_rstd")
        s_x_new = sem("s_x_new")
        s_score_max = sem("s_score_max")
        s_p_exp = sem("s_p_exp")
        s_g_loaded = sem("s_g_loaded")
        s_top_ready = sem("s_top_ready")
        s_top_exp = sem("s_top_exp")
        s_bias_written = sem("s_bias_written")
        s_bias_read = sem("s_bias_read")
        s_sig_in = sem("s_sig_in")
        s_sig_out = sem("s_sig_out")
        s_lora_mix = sem("s_lora_mix")
        s_rw_mix = sem("s_rw_mix")
        s_za_sig = sem("s_za_sig")
        s_kk_sqrt = sem("s_kk_sqrt")
        s_wkv_cum = sem("s_wkv_cum")
        s_wkv_exp = sem("s_wkv_exp")
        s_moba_max = sem("s_moba_max")
        s_moba_exp = sem("s_moba_exp")
        s_zb_sig = sem("s_zb_sig")
        s_gn_std = sem("s_gn_std")
        s_pg_sig = sem("s_pg_sig")
        s_pool_chain = sem("s_pool_chain")
        s_dve_chain = sem("s_dve_chain")
        s_gu_made = sem("s_gu_made")
        s_ov_base = sem("s_ov_base")
        s_slot_loaded = [sem(f"s_slot_loaded{i}") for i in range(SLOTS)]

        def rows_of(w, k, n=1):
            return w[k * 128:(k + n) * 128, :].rearrange("(a p) n -> p a n", p=128)

        w_in, w_kv = a["w_in"][0], a["w_mem_kv"][0]
        PRE = ([rows_of(w_kv, k) for k in range(8)] + [rows_of(w_in, k) for k in range(8)]
               + [rows_of(a[n][0], k, 2) for n in ("w_out", "w_mem_q", "w_mem_o") for k in (0, 2, 4, 6)])
        w1, w2, b1 = a["w_expert_in"][0], a["w_expert_out"][0], a["b_expert_in"][0]
        wi2 = a["w_in_2"][0]
        A0, R0, G0 = 0, 4 * 512, 4 * 512 + 2176
        POST = ([wi2[:, R0 + 2048:G0].rearrange("(a p) n -> p a n", p=128)]
                + [rows_of(wi2[:, R0:R0 + 2048], k) for k in range(8)]
                + [rows_of(wi2[:, A0:A0 + 2048], k) for k in range(8)]
                + [rows_of(wi2[:, G0:G0 + 2048], k) for k in range(8)]
                + [rows_of(a[n][0], k, 2) for n in ("p_a_2", "p_b_2") for k in (0, 2)]
                + [rows_of(a["w_out_2"][0], k, 2) for k in (0, 2, 4, 6)]
                + [rows_of(a["w_ple_up_2"][0], 0, 2)]
                + [rows_of(a["w_ple_gate_2"][0], k, 2) for k in (0, 2, 4, 6)])
        NPRE, PER = len(PRE), 12
        MOE_END = NPRE + PER * N_EXP
        FIRST = NPRE % SLOTS
        assert PER == SLOTS and FIRST == 4
        POST_SLOTS = (4, 5, 6, 7)

        def moe_slot(j):
            return (FIRST + j) % SLOTS

        def loads_before(sl):
            return len(range(sl, MOE_END, SLOTS))

        def view(sl, ap):
            return tk(slot(sl, 0, ap.shape[1] * ap.shape[2]), ap.shape[2])

        def bias_view(start):
            return bass.AP(bias_dram.tensor, start, [[512, 128], [128 * 513, HEADS], [1, 128]])

        bias_dram = nc.dram_tensor("bias_rows", [HEADS, 128, 513], f32, kind="Internal").ap()

        block = ctx.enter_context(nc.Block())

        @block.sync
        def _(sp):
            for h in range(TH):
                sp.dma_start(X[:, h, :], a["x"][0, 128 * h:128 * h + 128, :]).then_inc(s_x_loaded, 16)
            for h in range(TH):
                sp.dma_start(mem_rows[:, h, :], a["mem"][0, 128 * h:128 * h + 128, :]).then_inc(s_mem_loaded, 16)
            for n, w in enumerate(PRE):
                if n >= SLOTS:
                    sp.wait_ge(s_ring_used, n - SLOTS + 1)
                sp.dma_start(view(n % SLOTS, w), w).then_inc(s_slot_loaded[n % SLOTS], 16)
            with sp.Fori(0, N_EXP) as e:
                for j in range(PER):
                    sp.wait_ge(s_ring_used, e * PER + NPRE + j - SLOTS + 1)
                    if j < 8:
                        sp.dma_start(slot(moe_slot(j)), w1[bass.ds(e, 1), 128 * j:128 * j + 128, :]
                                     .rearrange("a p n -> p (a n)")).then_inc(s_slot_loaded[moe_slot(j)], 16)
                    else:
                        sp.dma_start(tk(slot(moe_slot(j)), D),
                                     w2[bass.ds(e, 1), 256 * (j - 8):256 * (j - 8) + 256, :]
                                     .rearrange("a (k p) n -> p (a k) n", p=128)).then_inc(s_slot_loaded[moe_slot(j)], 16)
                    if j == 8:
                        sp.dma_start(b1_rows[0:33:32, :], b1[bass.ds(e, 1), :].rearrange("a (b n) -> (a b) n", b=2))\
                          .then_inc(s_b1_loaded, 16)
            sp.wait_ge(s_flag_ready, 1)
            over = sp.value_load(flag[0:1, 0:1], min_val=0, max_val=1)
            with sp.If(over > 0):
                sp.wait_ge(s_ring_used, MOE_END)
                with sp.Fori(0, N_EXP) as e:
                    sp.wait_ge(s_ov_sc, e * (N_BLK - 1) + 1)
                    for j in range(8):
                        sp.dma_start(slot(moe_slot(j)), w1[bass.ds(e, 1), 128 * j:128 * j + 128, :]
                                     .rearrange("a p n -> p (a n)")).then_inc(s_ov_loaded, 16)
                    for j in range(8, PER):
                        sp.dma_start(tk(slot(moe_slot(j)), D),
                                     w2[bass.ds(e, 1), 256 * (j - 8):256 * (j - 8) + 256, :]
                                     .rearrange("a (k p) n -> p (a k) n", p=128)).then_inc(s_ov_loaded, 16)
                    sp.dma_start(b1_rows[0:33:32, :], b1[bass.ds(e, 1), :].rearrange("a (b n) -> (a b) n", b=2))\
                      .then_inc(s_ov_loaded, 16)
                sp.wait_ge(s_ov_sc, N_EXP * (N_BLK - 1) + 1)
            for n, w in enumerate(POST):
                sl = POST_SLOTS[n % 4]
                if n < 4:
                    sp.wait_ge(s_ring_used, MOE_END - PER + n + 1)
                else:
                    sp.wait_ge(s_ring_used, MOE_END + n - 4 + 1)
                sp.dma_start(view(sl, w), w).then_inc(s_slot_loaded[sl], 16)
            for h in range(TH):
                sp.wait_ge(s_out_ready, h + 1)
                sp.dma_start(out[0, 128 * h:128 * h + 128, :], HN[:, h, :]).then_inc(s_out_written, 16)
            sp.wait_ge(s_out_written, 16 * TH)

        @block.tensor
        def _(pe):
            mm, transpose = nc.tensor.matmul, nc.tensor.transpose

            def pre_chunk(n):
                pe.wait_ge(s_slot_loaded[n % SLOTS], 16 * (n // SLOTS + 1))
                return view(n % SLOTS, PRE[n])

            def post_chunk(n):
                sl = POST_SLOTS[n % 4]
                pe.wait_ge(s_slot_loaded[sl], 16 * (loads_before(sl) + n // 4 + 1))
                return view(sl, POST[n])

            def transpose_rows(rows, bank):
                ps = banks(bank, 4, S)
                for k in range(KT):
                    for h in range(TH):
                        t = transpose(ps[:, k, 128 * h:128 * h + 128], rows[:, h, 128 * k:128 * k + 128], ident)
                    if k % 4 == 3:
                        t.then_inc(s_norm_tr, 1)

            def project_T(ps, w, x, first, last):
                for j in range(ps.shape[1]):
                    t = mm(ps[:, j, :], w[:, 128 * j:128 * j + 128], x, start=first and j % 2 == 0,
                           stop=last and j % 2 == 1)
                return t

            def project_rows(bank, xT, k, w, first, last, n=2):
                for h in range(TH):
                    for c in range(n):
                        t = mm(PS[:, bank + n * h + c, :], xT[:, k, 128 * h:128 * h + 128],
                               w[:, 512 * c:512 * c + 512], start=first, stop=last)
                return t

            def rows_from_pairs(n0, chunk, bank, xT):
                for n in range(4):
                    w = chunk(n0 + n)
                    for i in range(2):
                        t = project_rows(bank, xT, 2 * n + i, w[:, i, :], n + i == 0, n + i == 4)
                    t.then_inc(s_ring_used, 1)

            pe.wait_ge(s_const_loaded, 16)
            pe.wait_ge(s_param_loaded, 16)
            transpose(PS[:, 7, 0:128], par_rows[:, :], ident).then_inc(s_params_T, 1)
            pe.wait_ge(s_norm_rows, 2)
            transpose_rows(mem_rows, 0)
            pe.wait_ge(s_norm_rows, 4)
            pe.wait_ge(s_params_cols, 1)
            transpose_rows(HN, 4)

            pe.wait_ge(s_norm_T, 4)
            for k in range(KT):
                w = pre_chunk(k)[:, 0, :]
                project_T(banks(0, 4, S), w, memT[:, k, :], k == 0, k == KT - 1)
                project_rows(4, memT, k, w[:, D:], k == 0, k == KT - 1).then_inc(s_ring_used, 1)

            pe.wait_ge(s_kv_evac, 2)
            for k in range(KT):
                w = pre_chunk(8 + k)[:, 0, :]
                project_T(banks(0, 4, S), w, HT[:, k, :], k == 0, k == KT - 1)
                project_rows(4, HT, k, w[:, 1024:1536], k == 0, k == KT - 1, n=1)
                project_T(banks(6, 2, S), w[:, 1536:2048], HT[:, k, :], k == 0, k == KT - 1)\
                    .then_inc(s_ring_used, 1)

            pe.wait_ge(s_win_evac, 4)
            for h in range(HEADS):
                j, r = h // 2, HD * (h % 2)
                q, k = qkT[r:r + HD, j, :], qkT[r:r + HD, 4 + j, :]
                mm(PS[:, h, 0:256], k[:, 0:128], q, start=True, stop=False)
                t = mm(PS[:, h, 256:384], k[:, 128:256], q[:, 128:256], start=False, stop=True)
            t.then_inc(s_z_done, 1)
            pe.wait_ge(s_sp_ready, 1)
            for h in range(HEADS):
                mm(PS[:, h, 0:256], C("tri_ge"), SP[:, h, 0:256], start=True, stop=False)
                mm(PS[:, h, 128:256], ones, SP[:, h, 256:384], start=False, stop=False)
                t = mm(PS[:, h, 256:384], C("tri_ge"), SP[:, h, 256:384], start=False, stop=True)
            t.then_inc(s_rev_done, 1)
            pe.wait_ge(s_w_ready, 1)
            for h in range(HEADS):
                c = slice(HD * h, HD * h + HD)
                mm(PS[:, 0, c], SP[:, h, 0:128], v_rows[:, 0, c], start=h == 0, stop=h == HEADS - 1)
                mm(PS[:, 1, c], SP[:, h, 128:256], v_rows[:, 0, c], start=h == 0, stop=False)
                t = mm(PS[:, 1, c], SP[:, h, 256:384], v_rows[:, 1, c], start=False, stop=h == HEADS - 1)
            t.then_inc(s_sb_done, 1)
            pe.wait_ge(s_pooled_ready, 4)
            pe.wait_ge(s_small_loaded, 16 * 6)
            for h in range(TH):
                for g in range(4):
                    c = slice(128 * g, 128 * g + 128)
                    t = mm(PS[:, 2 + h, c], pooled[:, g, 128 * h:128 * h + 128], w_pool[:, c], start=g == 0, stop=g == 3)
            t.then_inc(s_pool_done, 1)
            pe.wait_ge(s_norm_rows, 6)
            transpose_rows(HN, 4)
            pe.wait_ge(s_norm_T, 6)
            rows_from_pairs(16, pre_chunk, 0, HT)

            pe.wait_ge(s_norm_rows, 8)
            transpose_rows(HN, 4)
            pe.wait_ge(s_norm_T, 8)
            for n in range(4):
                w = pre_chunk(20 + n)
                for i in range(2):
                    t = project_T(banks(0, 4, S), w[:, i, :], HT[:, 2 * n + i, :], n + i == 0, n + i == 4)
                t.then_inc(s_ring_used, 1)
            pe.wait_ge(s_memq_evac, 2)
            for h in range(4):
                for th in range(TH):
                    for d in range(2):
                        t = mm(PS[:, 4 + h, 256 * th:256 * th + 256], mqT[:, 2 * h + d, 128 * th:128 * th + 128],
                               mkT[:, 2 * h + d, :], start=th + d == 0, stop=th + d == 2)
            t.then_inc(s_score_done, 1)
            pe.wait_ge(s_p_ready, 1)
            for h in range(4):
                for m in range(2):
                    for th in range(TH):
                        t = transpose(banks(0, 4, S)[:, 2 * h + m, 128 * th:128 * th + 128],
                                      prob[:, 2 * h + th, 128 * m:128 * m + 128], ident)
            t.then_inc(s_tr_p, 1)
            pe.wait_ge(s_pT_evac, 2)
            for j in range(KT):
                for m in range(2):
                    t = mm(banks(4, 4, S)[:, j, :], mv_rows[:, m, 128 * j:128 * j + 128], probT[:, 2 * (j // 2) + m, :],
                           start=j % 2 == 0 and m == 0, stop=j % 2 == 1 and m == 1)
            t.then_inc(s_o_done, 1)
            pe.wait_ge(s_oT_evac, 2)
            rows_from_pairs(24, pre_chunk, 0, oT)

            pe.wait_ge(s_norm_rows, 10)
            transpose_rows(HN, 4)
            pe.wait_ge(s_norm_T, 10)
            for h in range(TH):
                c = slice(N_EXP * h, N_EXP * h + N_EXP)
                mm(PS[:, 0, c], ones[0:1, :], b_router[0:1, :], start=h == 0, stop=False)
                for k in range(KT):
                    t = mm(PS[:, 0, c], HT[:, k, 128 * h:128 * h + 128], w_router[:, k, :], start=False,
                           stop=h == 1 and k == KT - 1)
            t.then_inc(s_logits_done, 1)
            pe.wait_ge(s_late_loaded, 16)
            pe.wait_ge(s_rbias_ready, 16)
            mm(PS[0:HEADS, 3, :], rbias[0:33, :], C("bias_sel")[0:33, :], start=True, stop=True).then_inc(s_frow_done, 1)
            pe.wait_ge(s_mask_ready, 1)
            mm(PS[:, 1, 0:32], C("tri_lt"), mask[:, 0, :], start=True, stop=False)
            mm(PS[:, 1, 32:64], ones, mask[:, 0, :], start=False, stop=False)
            mm(PS[:, 1, 32:64], C("tri_lt"), mask[:, 1, :], start=False, stop=False)
            mm(PS[:, 1, 64:96], ones, mask[:, 0, :], start=False, stop=False)
            mm(PS[:, 1, 64:96], ones, mask[:, 1, :], start=False, stop=True).then_inc(s_rank_done, 1)
            pe.wait_ge(s_gates_ready, 1)
            for h in range(TH):
                t = transpose(PS[0:N_EXP, 2, 128 * h:128 * h + 128], gate[:, h, 0:N_EXP], ident)
            t.then_inc(s_gT_done, 1)
            pe.wait_ge(s_gT_evac, 1)
            pe.wait_ge(s_b2_loaded, 16)
            for h in range(TH):
                for c in range(2):
                    mm(PS[:, 4 + 2 * h + c, :], gT[0:N_EXP, 128 * h:128 * h + 128],
                       b2_all[0:N_EXP, 512 * c:512 * c + 512], start=True, stop=True)

            def gather():
                for k in range(KT):
                    for h in range(TH):
                        t = mm(banks(0, 1, CAP)[:, k, :], HN[:, h, 128 * k:128 * k + 128], pick[:, h, :],
                               start=k + h == 0, stop=k + h == KT)
                return t

            def up_bias():
                for c in range(2):
                    for b in range(2):
                        mm(PS[CAP * c:CAP * c + CAP, 2 + b, :], ones[32 * b:32 * b + 1, 0:CAP],
                           b1_rows[32 * b:32 * b + 1, 512 * c:512 * c + 512], start=True, stop=False)

            def up(k):
                w = slot(moe_slot(k))
                for b in range(2):
                    for c in range(2):
                        t = mm(PS[CAP * c:CAP * c + CAP, 2 + b, :], xT_e[:, k, :],
                               w[:, D * b + 512 * c:D * b + 512 * c + 512], start=False, stop=k == KT - 1)
                return t

            def turn_gpick():
                for h in range(TH):
                    t = transpose(PS[:, 1, 128 * h:128 * h + 128], gpick[:, h, :], ident)
                return t

            def turn_act():
                for b in range(4):
                    t = transpose(PS[:, 1, 128 * b:128 * b + 128], act_e[:, 128 * b:128 * b + 128], ident)
                return t

            def down(n):
                w = tk(slot(moe_slot(8 + n)), D)
                for i in range(2):
                    k = 2 * n + i
                    for c in range(2):
                        t = mm(PS[CAP * c:CAP * c + CAP, 0, :], actT[:, k % 4, k // 4, :],
                               w[:, i, 512 * c:512 * c + 512], start=k == 0, stop=k == KT - 1)
                return t

            def scatter():
                for h in range(TH):
                    for c in range(2):
                        t = mm(PS[:, 4 + 2 * h + c, :], gpT[CAP * c:CAP * c + CAP, 128 * h:128 * h + 128],
                               y_e[CAP * c:CAP * c + CAP, :], start=False, stop=True, skip_group_check=True)
                return t

            pe.wait_ge(s_pe_ready, 1)
            gather().then_inc(s_gathered, 1)
            pe.wait_ge(s_frow_evac, 1)
            with pe.Fori(0, N_EXP) as e:
                pe.wait_ge(s_xT_ready, e + 1)
                pe.wait_ge(s_gu_free, e + 1)
                pe.wait_ge(s_b1_loaded, (e + 1) * 16)
                up_bias()
                for k in range(KT):
                    pe.wait_ge(s_slot_loaded[moe_slot(k)], (e + ((NPRE + k) // SLOTS + 1)) * 16)
                    up(k).then_inc(s_ring_used, 1)
                pe.wait_ge(s_gp_ready, e + 1)
                turn_gpick().then_inc(s_gpt_done, 1)
                pe.wait_ge(s_pe_ready, e + 2)
                gather().then_inc(s_gathered, 1)
                pe.wait_ge(s_act_ready, e + 1)
                pe.wait_ge(s_gpt_evac, e + 1)
                turn_act().then_inc(s_actT_done, 1)
                pe.wait_ge(s_actT_evac, e + 1)
                pe.wait_ge(s_xT_ready, e + 2)
                for n in range(4):
                    pe.wait_ge(s_slot_loaded[moe_slot(8 + n)], (e + ((NPRE + 8 + n) // SLOTS + 1)) * 16)
                    down(n).then_inc(s_ring_used, 1)
                pe.wait_ge(s_y_evac, e + 1)
                scatter().then_inc(s_scattered, 1)

            pe.wait_ge(s_flag_ready, 1)
            over = pe.value_load(flag[0:1, 0:1], min_val=0, max_val=1)
            with pe.If(over > 0):
                NB = N_BLK - 1
                pe.wait_ge(s_gu_free, N_EXP + 1)
                with pe.Fori(0, N_EXP) as e:
                    pe.wait_ge(s_ov_loaded, (e + 1) * (16 * (PER + 1)))
                    for b in range(NB):
                        pe.wait_ge(s_pe_ready, e * NB + (N_EXP + 1 + b + 1))
                        gather().then_inc(s_gathered, 1)
                        turn_gpick().then_inc(s_gpt_done, 1)
                        pe.wait_ge(s_xT_ready, e * NB + (N_EXP + 1 + b + 1))
                        up_bias()
                        for k in range(KT):
                            t = up(k)
                        t.then_inc(s_ov_up, 1)
                        pe.wait_ge(s_gpt_evac, e * NB + (N_EXP + b + 1))
                        pe.wait_ge(s_act_ready, e * NB + (N_EXP + b + 1))
                        turn_act().then_inc(s_actT_done, 1)
                        pe.wait_ge(s_actT_evac, e * NB + (N_EXP + b + 1))
                        for n in range(4):
                            t = down(n)
                        t.then_inc(s_ov_down, 1)
                        pe.wait_ge(s_y_evac, e * NB + (N_EXP + b + 1))
                        scatter().then_inc(s_ov_sc, 1)
            pe.wait_ge(s_norm_rows, 14)
            transpose_rows(HN, 0)
            pe.wait_ge(s_norm_T, 12)
            n = 0
            w = post_chunk(n)
            for k in range(KT):
                t = mm(PS[:, 4, 0:256], w[:, k, :], HT[:, k, :], start=k == 0, stop=k == KT - 1)
            t.then_inc(s_ring_used, 1)
            n += 1
            pe.wait_ge(s_lora_evac, 1)
            for k in range(KT):
                w = post_chunk(n + k)[:, 0, :]
                project_T(banks(0, 8, S), w, HT[:, k, :], k == 0, k == KT - 1).then_inc(s_ring_used, 1)
            n += KT
            pe.wait_ge(s_rw_evac, 2)
            for k in range(KT):
                w = post_chunk(n + k)[:, 0, :]
                project_T(banks(0, 4, S), w, HT[:, k, :], k == 0, k == KT - 1)
                project_rows(4, HT, k, w[:, 1024:1536], k == 0, k == KT - 1, n=1)
                project_T(banks(6, 2, S), w[:, 1536:2048], HT[:, k, :], k == 0, k == KT - 1)\
                    .then_inc(s_ring_used, 1)
            n += KT
            pe.wait_ge(s_a_evac, 4)
            pe.wait_ge(s_tanh_ready, 1)
            for j in range(4):
                mm(banks(0, 2, S)[:, j, :], lora_w[0:64, 128 * j:128 * j + 128], lora_t[0:64, :],
                   start=j % 2 == 0, stop=j % 2 == 1)
            for j in range(4):
                t = mm(banks(2, 2, S)[:, j, :], lora_w[64:128, 128 * j:128 * j + 128], lora[64:128, :],
                       start=j % 2 == 0, stop=j % 2 == 1)
            t.then_inc(s_wl_done, 1)
            pe.wait_ge(s_kk_sq, 1)
            for b in range(2):
                t = mm(PS[:, 4 + b, :], C("head_ones"), kk_sq[:, 512 * b:512 * b + 512], start=True, stop=True)
            t.then_inc(s_kk_sum, 1)
            pe.wait_ge(s_bon_in, 1)
            for b in range(2):
                t = mm(PS[:, 6 + b, :], C("head_ones"), bon_in[:, 512 * b:512 * b + 512], start=True, stop=True)
            t.then_inc(s_bon_sum, 1)
            pe.wait_ge(s_wl_sig, 8)
            pe.wait_ge(s_bon_ready, 1)
            for k in range(KT):
                w = post_chunk(n + k)[:, 0, :]
                project_T(banks(0, 8, S), w, HT[:, k, :], k == 0, k == KT - 1).then_inc(s_ring_used, 1)
            n += KT
            pe.wait_ge(s_gate_evac, 2)
            for h in range(HEADS):
                j, r = h // 2, HD * (h % 2)
                q, k = qk2[r:r + HD, j, :], qk2[r:r + HD, 4 + j, :]
                mm(PS[:, h, 0:128], q[:, 0:128], k[:, 0:128], start=True, stop=False)
                t = mm(PS[:, h, 128:384], q[:, 128:256], k, start=False, stop=True)
            t.then_inc(s_moba_s, 1)
            pe.wait_ge(s_moba_p, 1)
            for h in range(HEADS):
                for b in range(3):
                    t = transpose(PS[:, h, 128 * b:128 * b + 128], prob2[:, h, 128 * b:128 * b + 128], ident)
            t.then_inc(s_moba_tr, 1)
            pe.wait_ge(s_moba_pT, 2)
            for h in range(HEADS):
                j, r, c = h // 2, HD * (h % 2), slice(HD * h, HD * h + HD)
                mm(banks(0, 2, S)[r:r + HD, j, :], v2[:, 0, c], prob2T[:, h, 0:256], start=j % 2 == 0, stop=False)
                t = mm(banks(0, 2, S)[r:r + HD, j, 128:256], v2[:, 1, c], prob2T[:, h, 256:384], start=False,
                       stop=j % 2 == 1)
            t.then_inc(s_moba_o, 1)

            def pair_product(bank, lhs, rhs):
                ps = banks(bank, 2, L)
                for n in range(NSET):
                    for r in (0, HD):
                        t = mm(ps[r:r + HD, n, :], lhs(n, r), rhs(n, r), start=True, stop=True)
                return t

            def of(x):
                v = tk(x, L)
                return lambda n, r: v[r:r + HD, n, :]

            def eye(n, r):
                return ident[r:r + HD, r:r + HD]

            pe.wait_ge(s_wkv_T, 1)
            pe.wait_ge(s_ya_ready, 1)
            for i, (src, bank) in enumerate(((rw_v, 2), (bT, 4), (kTl, 6))):
                pair_product(bank, of(src), eye).then_inc(s_rows_done, 1)
            for i, (x, y) in enumerate(((bT, aT), (aT, bT), (kTl, aT), (bT, rT), (kTl, rT))):
                if i:
                    pe.wait_ge(s_rows_evac, min(i, 3))
                if i == 4:
                    pe.wait_ge(s_mat_evac, 2)
                pair_product((0, 2, 4, 6, 0)[i], of(x), of(y)).then_inc(s_mat_done, 1)
            pe.wait_ge(s_sol_ready, 1)
            for i, (x, y, need) in enumerate(SOLVE):
                if need:
                    pe.wait_ge(s_sol_evac, need)
                pair_product(2 * (i % 4), of(x), of(y)).then_inc(s_sol_done, 1)
            pe.wait_ge(s_sol_evac, len(SOLVE))
            oY = banks(4, 2, S)
            for c in range(NCH):
                for r in (0, HD):
                    for j in range(4):
                        n = j * NCH + c
                        if c:
                            if r + j == 0:
                                pe.wait_ge(s_rec_state, c)
                            mm(PS[r:r + HD, 0, L * j:L * j + L], tk(aT, L)[r:r + HD, n, :], state[c % 2][r:r + HD, j, :],
                               start=j == 0, stop=False)
                        t = mm(PS[r:r + HD, 0, L * j:L * j + L], of(akT)(n, r), of(v_tok)(n, r), start=c == 0 and j == 0,
                               stop=j == 3)
                t.then_inc(s_rec_x, 1)
                pe.wait_ge(s_rec_xe, c + 1)
                for r in (0, HD):
                    for j in range(4):
                        t = mm(PS[r:r + HD, 1, L * j:L * j + L], of(invT)(j * NCH + c, r), rec_rhs[r:r + HD, j, :],
                               start=j == 0, stop=j == 3)
                t.then_inc(s_rec_sa, 1)
                pe.wait_ge(s_rec_sae, c + 1)
                if c < NCH - 1:
                    for r in (0, HD):
                        for j in range(4):
                            n = j * NCH + c
                            mm(PS[r:r + HD, 2, L * j:L * j + L], of(b_tok)(n, r), rec_sa[r:r + HD, j, :], start=j == 0,
                               stop=False)
                            t = mm(PS[r:r + HD, 2, L * j:L * j + L], of(k_tok)(n, r), of(v_tok)(n, r), start=False,
                                   stop=j == 3)
                    t.then_inc(s_rec_s, 1)
                for r in (0, HD):
                    for j in range(4):
                        n = j * NCH + c
                        o = oY[r:r + HD, j, L * c:L * c + L]
                        mm(o, rec_sa[r:r + HD, j, :], of(rbT)(n, r), start=c == 0 and j % 2 == 0, stop=False)
                        if c:
                            mm(o, state[c % 2][r:r + HD, j, :], tk(rT, L)[r:r + HD, n, :], start=False, stop=False)
                        t = mm(o, of(v_tok)(n, r), of(rkT)(n, r), start=False, stop=c == NCH - 1 and j % 2 == 1)
                t.then_inc(s_y_psum, 1)
            pe.wait_ge(s_yT_evac, 1)
            for b in range(2):
                t = mm(PS[:, 6 + b, :], C("head_ones"), yT[:, 512 * b:512 * b + 512], start=True, stop=True)
            t.then_inc(s_gn_mean, 1)
            pe.wait_ge(s_gn_sq, 1)
            for b in range(2):
                t = mm(PS[:, 4 + b, :], C("head_ones"), ysq[:, 512 * b:512 * b + 512], start=True, stop=True)
            t.then_inc(s_gn_var, 1)
            n = 25
            for i in range(2):
                if i:
                    pe.wait_ge(s_yb_ready, 1)
                for c in range(2):
                    w = post_chunk(n + c)
                    for q in range(2):
                        k = 2 * c + q
                        t = project_T(banks(4 * i, 4, S), w[:, q, :], (ya, yb)[i][:, k, :], k == 0, k == 3)
                    t.then_inc(s_ring_used, 1)
                n += 2
            pe.wait_ge(s_merged_ready, 1)
            rows_from_pairs(n, post_chunk, 0, merged)
            n += 4
            pe.wait_ge(s_p_loaded, 16)
            for k in range(2):
                for h in range(TH):
                    t = transpose(banks(4, 1, S)[:, k, 128 * h:128 * h + 128], p_rows[:, h, 128 * k:128 * k + 128], ident)
            t.then_inc(s_ple_pT, 1)
            pe.wait_ge(s_ple_pTe, 1)
            w = post_chunk(n)
            for k in range(2):
                t = project_rows(4, pT, k, w[:, k, :], k == 0, k == 1)
            t.then_inc(s_ring_used, 1)
            n += 1
            pe.wait_ge(s_h2_ready, 2)
            transpose_rows(X, 0)
            pe.wait_ge(s_norm_T, 14)
            rows_from_pairs(n, post_chunk, 0, HT)

        @block.scalar
        def _(act):
            fn = nc.scalar.activation

            def stats(n, halves, width, eps_col):
                for h, (rows, scratch) in enumerate(halves):
                    fn(scratch, rows, ACT.Square, accum_out=stat[:, 2 * n + h:2 * n + h + 1]).then_inc(s_norm_sq, 1)
                act.wait_ge(s_norm_sq, 2 * n + 2)
                fn(stat[:, 16 + 2 * n:18 + 2 * n], stat[:, 2 * n:2 * n + 2], ACT.Sqrt, scale=1.0 / width,
                   bias=eps[:, eps_col:eps_col + 1]).then_inc(s_norm_std, 1)

            def scale_half(n, dst, src):
                act.wait_ge(s_norm_rstd, n + 1)
                fn(dst, src, ACT.Copy, scale=stat[:, 32 + 2 * n + 1:32 + 2 * n + 2]).then_inc(s_norm_rows, 1)

            def evac_T(m, bank, dst, gain):
                act.wait_ge(s_norm_tr, 2 * m)
                for k in range(4, KT):
                    t = fn(dst[:, k, :], banks(bank, 4, S)[:, k, :], ACT.Copy, scale=P(gain, k) if gain else 1.0)
                t.then_inc(s_norm_T, 1)

            act.dma_start(cst[:, 0:LATE], a["consts"][:, 0:LATE]).then_inc(s_const_loaded, 16)
            act.dma_start(par_rows[:, :], a["params"]).then_inc(s_param_loaded, 16)
            act.dma_start(cst[:, LATE:], a["consts"][:, LATE:]).then_inc(s_late_loaded, 16)
            act.dma_start(w_pool[:, :].rearrange("p (g e) -> p g e", g=4), a["w_pool"][0].rearrange("g c e -> c g e"))\
               .then_inc(s_small_loaded, 16)
            act.dma_start(scale_bc[:, :], a["pool_scale"][0].partition_broadcast(128)).then_inc(s_small_loaded, 16)
            act.dma_start(w_router[:, :, :], a["w_router"][0].rearrange("(k p) e -> p k e", p=128)).then_inc(s_small_loaded, 16)
            act.dma_start(b_router[:, :], a["b_router"]).then_inc(s_small_loaded, 16)
            act.dma_start(lora_w[0:64, :], a["w_up_2"][0]).then_inc(s_small_loaded, 16)
            act.dma_start(lora_w[64:128, :], a["a_up_2"][0]).then_inc(s_small_loaded, 16)

            act.wait_ge(s_eps_set, 1)
            act.wait_ge(s_mem_loaded, 32)
            stats(0, [(mem_rows[:, h, :], HN[:, h, :]) for h in range(TH)], D, 0)
            scale_half(0, mem_rows[:, 1, :], mem_rows[:, 1, :])
            act.wait_ge(s_x_loaded, 32)
            stats(1, [(X[:, h, :], HN[:, h, :]) for h in range(TH)], D, 0)
            scale_half(1, HN[:, 1, :], X[:, 1, :])
            act.wait_ge(s_params_cols, 1)
            evac_T(1, 0, memT, "g_mem_kv")
            evac_T(2, 4, HT, "g_mix")
            act.wait_ge(s_ring_used, 8)
            fn(mkT, banks(0, 4, S), ACT.Copy).then_inc(s_kv_evac, 1)
            act.wait_ge(s_ring_used, 16)
            fn(qkT[:, 0:4, :], banks(0, 2, S), ACT.Copy, scale=HD ** -0.5).then_inc(s_win_evac, 1)
            fn(qkT[:, 4:8, :], banks(2, 2, S), ACT.Copy).then_inc(s_win_evac, 1)
            act.wait_ge(s_z_copied, 1)
            fn(SP, Z, ACT.Abs).then_inc(s_z_abs, 1)
            act.wait_ge(s_z_abs, 1)
            fn(SP, SP, ACT.Exp, scale=-1.0).then_inc(s_z_abs, 1)
            act.wait_ge(s_z_abs, 2)
            fn(SP, SP, ACT.Ln, bias=1.0).then_inc(s_z_ln, 1)
            act.wait_ge(s_arg_ready, 1)
            fn(SP, Z, ACT.Exp).then_inc(s_w_ready, 1)
            act.wait_ge(s_sb_done, 1)
            for h in range(TH):
                fn(buf(7, 512 * h, 512 * h + 512), PS[:, h, :], ACT.Square, accum_out=stat[:, 48 + h:49 + h]).then_inc(s_mix_sq, 1)
            act.wait_ge(s_pool_scaled, 2)
            for h in range(TH):
                fn(buf(7, 1024 + 512 * h, 1536 + 512 * h), HN[:, h, 512:], ACT.Square,
                   accum_out=stat[:, 50 + h:51 + h]).then_inc(s_mix_sq, 1)
            act.wait_ge(s_mix_sq, 4)
            fn(stat[:, 52:56], stat[:, 48:52], ACT.Sqrt, scale=1.0 / 512, bias=eps[:, 0:1]).then_inc(s_mix_std, 1)
            act.wait_ge(s_mix_rstd, 1)
            for h in range(TH):
                t = fn(HN[:, h, 0:512], PS[:, h, :], ACT.Copy, scale=stat[:, 56 + h:57 + h])
            t.then_inc(s_norm_rows, 1)
            evac_T(3, 4, HT, "g_sb_out")
            for h in range(TH):
                act.wait_ge(s_x_new, h + 1)
                if h == 0:
                    act.wait_ge(s_norm_tr, 6)
                fn(HN[:, h, :], X[:, h, :], ACT.Square, accum_out=stat[:, 6 + h:7 + h]).then_inc(s_norm_sq, 1)
            act.wait_ge(s_norm_sq, 6)
            fn(stat[:, 22:24], stat[:, 6:8], ACT.Sqrt, scale=1.0 / D, bias=eps[:, 0:1]).then_inc(s_norm_std, 1)
            act.wait_ge(s_norm_rstd, 3)
            fn(HN[:, 1, :], X[:, 1, :], ACT.Copy, scale=stat[:, 39:40]).then_inc(s_norm_rows, 1)
            evac_T(4, 4, HT, "g_mem_q")
            act.wait_ge(s_ring_used, 24)
            fn(mqT[:, 0:4, :], banks(0, 2, S), ACT.Copy, scale=256 ** -0.5).then_inc(s_memq_evac, 1)
            act.wait_ge(s_score_max, 1)
            for i in range(8):
                fn(prob[:, i, :], banks(4, 4, S)[:, i, :], ACT.Exp, bias=mstat[:, 8 + i:9 + i],
                   accum_out=mstat[:, 16 + i:17 + i]).then_inc(s_p_exp, 1)
            act.wait_ge(s_tr_p, 1)
            fn(probT[:, 0:4, :], banks(0, 2, S), ACT.Copy).then_inc(s_pT_evac, 1)
            act.wait_ge(s_o_done, 1)
            fn(oT[:, 0:4, :], banks(4, 2, S), ACT.Copy).then_inc(s_oT_evac, 1)
            for h in range(TH):
                act.wait_ge(s_x_new, 2 + h + 1)
                if h == 0:
                    act.wait_ge(s_norm_tr, 8)
                fn(HN[:, h, :], X[:, h, :], ACT.Square, accum_out=stat[:, 8 + h:9 + h]).then_inc(s_norm_sq, 1)
            act.dma_start(b2_all[0:N_EXP, :], a["b_expert_out"][0]).then_inc(s_b2_loaded, 16)
            act.dma_start(g_final, a["g_final"].partition_broadcast(128)).then_inc(s_g_loaded, 16)
            act.dma_start(g_post, a["g_post_2"][0].partition_broadcast(128)).then_inc(s_g_loaded, 16)
            act.wait_ge(s_norm_sq, 8)
            fn(stat[:, 24:26], stat[:, 8:10], ACT.Sqrt, scale=1.0 / D, bias=eps[:, 0:1]).then_inc(s_norm_std, 1)
            act.wait_ge(s_norm_rstd, 4)
            fn(HN[:, 1, :], X[:, 1, :], ACT.Copy, scale=stat[:, 41:42]).then_inc(s_norm_rows, 1)
            evac_T(5, 4, HT, "g_ffn")
            act.wait_ge(s_top_ready, 1)
            for h in range(TH):
                t = fn(lg[:, h, :], lg[:, h, :], ACT.Exp, bias=stat[:, 60 + h:61 + h])
            t.then_inc(s_top_exp, 1)
            act.wait_ge(s_frow_done, 1)
            fn(frow[0:HEADS, :], PS[0:HEADS, 3, :], ACT.Copy).then_inc(s_frow_evac, 1)
            act.wait_ge(s_frow_evac, 1)
            act.dma_start(bias_dram[:, :, 0:512], frow[0:HEADS, :].unsqueeze(1).to_broadcast([HEADS, 128, 512])).then_inc(s_bias_written, 16)
            act.wait_ge(s_bias_written, 16)
            for b in range(2):
                src = bias_view(255 - 128 * b)
                act.dma_start(bias[:, :, b, :], src).then_inc(s_bias_read, 16)

            def silu_gate():
                return fn(sig, g7, ACT.Sigmoid, scale=1.702)

            def copy_gpT():
                return fn(gpT, PS[:, 1, 0:256], ACT.Copy)

            def copy_actT():
                return fn(actT, PS[:, 1, :].rearrange("p (b h c) -> p b h c", b=4, h=2), ACT.Copy)

            def copy_y():
                return fn(y_e, PS[:, 0, :], ACT.Copy)

            with act.Fori(0, N_EXP) as e:
                act.wait_ge(s_sig_in, e + 1)
                silu_gate().then_inc(s_sig_out, 1)
                act.wait_ge(s_gpt_done, e + 1)
                copy_gpT().then_inc(s_gpt_evac, 1)
                act.wait_ge(s_actT_done, e + 1)
                copy_actT().then_inc(s_actT_evac, 1)
                act.wait_ge(s_ring_used, e * PER + (NPRE + PER))
                copy_y().then_inc(s_y_evac, 1)
            act.wait_ge(s_flag_ready, 1)
            over = act.value_load(flag[0:1, 0:1], min_val=0, max_val=1)
            with act.If(over > 0):
                NB = N_BLK - 1
                with act.Fori(0, N_EXP * NB) as n:
                    act.wait_ge(s_gpt_done, n + (N_EXP + 1))
                    copy_gpT().then_inc(s_gpt_evac, 1)
                    act.wait_ge(s_sig_in, n + (N_EXP + 1))
                    silu_gate().then_inc(s_sig_out, 1)
                    act.wait_ge(s_actT_done, n + (N_EXP + 1))
                    copy_actT().then_inc(s_actT_evac, 1)
                    act.wait_ge(s_ov_down, n + 1)
                    copy_y().then_inc(s_y_evac, 1)

            for n in (5, 6):
                for h in range(TH):
                    if n == 5:
                        act.wait_ge(s_x_new, 4 + h + 1)
                    else:
                        act.wait_ge(s_norm_rows, 11 + h)
                    fn(HN[:, h, :], X[:, h, :], ACT.Square, accum_out=stat[:, 2 * n + h - 0:2 * n + h + 1])\
                        .then_inc(s_norm_sq, 1)
                act.wait_ge(s_norm_sq, 2 * n)
                fn(stat[:, 16 + 2 * n:18 + 2 * n], stat[:, 2 * n:2 * n + 2], ACT.Sqrt, scale=1.0 / D,
                   bias=eps[:, n - 5:n - 4]).then_inc(s_norm_std, 1)
            act.wait_ge(s_norm_rstd, 6)
            fn(HN[:, 1, :], X[:, 1, :], ACT.Copy, scale=stat[:, 45:46]).then_inc(s_norm_rows, 1)
            act.dma_start(p_rows, a["p_2"][0, 0].rearrange("(h p) n -> p h n", p=128)).then_inc(s_p_loaded, 16)
            evac_T(6, 0, HT, "g_pre_2")
            act.wait_ge(s_lora_mix, 1)
            fn(lora_t[0:64, :], lora[0:64, :], ACT.Tanh).then_inc(s_tanh_ready, 1)
            act.wait_ge(s_ring_used, MOE_END + 9)
            fn(rwT[:, 0:8, :], banks(0, 4, S), ACT.Copy).then_inc(s_rw_evac, 1)
            act.wait_ge(s_ring_used, MOE_END + 17)
            act.wait_ge(s_rw_mix, 1)
            fn(qk2[:, 0:4, :], banks(0, 2, S), ACT.Copy, scale=HD ** -0.5).then_inc(s_a_evac, 1)
            fn(qk2[:, 4:8, :], banks(2, 2, S), ACT.Copy).then_inc(s_a_evac, 1)
            act.wait_ge(s_wl_done, 1)
            for j in range(4):
                fn(tk(sg, S)[:, j, :], banks(0, 2, S)[:, j, :], ACT.Sigmoid, bias=P("w0_2", j)).then_inc(s_wl_sig, 1)
            for j in range(4):
                fn(tk(rate, S)[:, j, :], banks(2, 2, S)[:, j, :], ACT.Sigmoid, bias=P("a0_2", j)).then_inc(s_wl_sig, 1)
            act.wait_ge(s_a_evac, 4)
            fn(z_sig, buf(6, 1024), ACT.Sigmoid).then_inc(s_za_sig, 1)
            act.wait_ge(s_kk_sum, 1)
            fn(kk_inv, PS[:, 4:6, :].rearrange("p b n -> p (b n)"), ACT.Sqrt).then_inc(s_kk_sqrt, 1)
            act.wait_ge(s_wkv_cum, 1)
            fn(dec, cum, ACT.Exp, scale=-DECAY).then_inc(s_wkv_exp, 1)
            fn(dec_inv, cum, ACT.Exp, scale=DECAY).then_inc(s_wkv_exp, 1)
            fn(dec_prev, sg, ACT.Exp, scale=-DECAY).then_inc(s_wkv_exp, 1)
            act.wait_ge(s_ring_used, MOE_END + 25)
            fn(gate_a, banks(0, 4, S), ACT.Sigmoid).then_inc(s_gate_evac, 1)
            fn(gate_b, banks(4, 4, S), ACT.Sigmoid).then_inc(s_gate_evac, 1)
            act.wait_ge(s_moba_max, 1)
            for h in range(HEADS):
                for i, c in enumerate((slice(0, 128), slice(128, 384))):
                    fn(prob2[:, h, c], prob2[:, h, c], ACT.Exp, bias=mstat[:, 16 + 8 * i + h:17 + 8 * i + h],
                       accum_out=mstat[:, 32 + 8 * i + h:33 + 8 * i + h]).then_inc(s_moba_exp, 1)
            act.wait_ge(s_moba_tr, 1)
            fn(prob2T[:, 0:4, :], PS[:, 0:4, 0:384], ACT.Copy).then_inc(s_moba_pT, 1)
            act.wait_ge(s_ya_ready, 1)
            fn(z_sig, buf(4, 1024), ACT.Sigmoid).then_inc(s_zb_sig, 1)
            act.wait_ge(s_gn_var, 1)
            fn(ystd, PS[:, 4:6, :].rearrange("p b n -> p (b n)"), ACT.Sqrt, scale=1.0 / HD, bias=eps[:, 2:3])\
                .then_inc(s_gn_std, 1)
            act.wait_ge(s_ring_used, MOE_END + 33)
            for h in range(TH):
                fn(HN[:, h, :], PS[:, 2 * h:2 * h + 2, :].rearrange("p b n -> p (b n)"), ACT.Square,
                   accum_out=stat[:, 14 + h:15 + h]).then_inc(s_norm_sq, 1)
            act.wait_ge(s_norm_sq, 14)
            fn(stat[:, 30:32], stat[:, 14:16], ACT.Sqrt, scale=1.0 / D, bias=eps[:, 1:2]).then_inc(s_norm_std, 1)
            evac_T(7, 0, HT, None)
            act.wait_ge(s_ring_used, MOE_END + len(POST))
            for h in range(TH):
                fn(pg_sig[:, h, :], PS[:, 2 * h:2 * h + 2, :].rearrange("p b n -> p (b n)"), ACT.Sigmoid)\
                    .then_inc(s_pg_sig, 1)

        @block.gpsimd
        def _(pool):
            done = [0]

            def step(ins):
                done[0] += 1
                ins.then_inc(s_pool_chain, 1)
                pool.wait_ge(s_pool_chain, done[0])

            nc.gpsimd.memset(eps[:, 0:1], 1e-5)
            nc.gpsimd.memset(eps[:, 1:2], 1e-6)
            nc.gpsimd.memset(eps[:, 2:3], 64e-5).then_inc(s_eps_set, 1)
            nc.gpsimd.memset(eps[:, 3:4], 0.0).then_inc(s_gu_free, 1)
            nc.gpsimd.memset(gate[:, :, N_EXP:], 0.0).then_inc(s_ov_sc, 1)
            nc.gpsimd.memset(slot_of[:, :, N_EXP:], -1.0)
            step(nc.gpsimd.memset(rbias[:, :], 1.0))
            pool.dma_start(rbias[0:32, :], a["rel_bias_2"]).then_inc(s_rbias_ready, 16)
            pool.wait_ge(s_win_evac, 4)
            pool.wait_ge(s_late_loaded, 16)
            for g in range(4):
                src = u_T[:, g, :]
                for n in range(g + 1):
                    w, dst = 1 << n, win[n % 2]
                    nc.gpsimd.tensor_copy(dst[:, 0:w], src[:, 0:w])
                    step(nc.gpsimd.tensor_tensor(dst[:, w:], src[:, w:], src[:, 0:S - w], ALU.add))
                    src = dst
                step(nc.gpsimd.tensor_tensor(win[2], src, C("inv_count")[:, S * g:S * g + S], ALU.mult))
                nc.gpsimd.tensor_tensor(pooled[:, g, :], win[2], u_T[:, g, :], ALU.subtract).then_inc(s_pooled_ready, 1)
                pool.wait_ge(s_pooled_ready, g + 1)

        @block.vector
        def _(dve):
            v = nc.vector
            done = [0]

            def step(ins):
                done[0] += 1
                ins.then_inc(s_dve_chain, 1)
                dve.wait_ge(s_dve_chain, done[0])

            def rstd(n):
                dve.wait_ge(s_norm_std, n + 1)
                v.reciprocal(stat[:, 32 + 2 * n:34 + 2 * n], stat[:, 16 + 2 * n:18 + 2 * n]).then_inc(s_norm_rstd, 1)
                dve.wait_ge(s_norm_rstd, n + 1)

            def scale_half(n, dst, src):
                v.tensor_scalar(dst, src, stat[:, 32 + 2 * n:33 + 2 * n], None, ALU.mult).then_inc(s_norm_rows, 1)

            def evac_T(m, bank, dst, gain):
                dve.wait_ge(s_norm_tr, 2 * m - 1)
                if gain:
                    t = v.tensor_tensor(dst[:, 0:4, :], banks(bank, 2, S), Pn(gain, 4, S), ALU.mult)
                else:
                    t = v.tensor_copy(dst[:, 0:4, :], banks(bank, 2, S))
                t.then_inc(s_norm_T, 1)

            def half(bank, h):
                return PS[:, bank + 2 * h:bank + 2 * h + 2, :].rearrange("p b n -> p (b n)")

            def add_residual(bank):
                for h in range(TH):
                    v.tensor_tensor(X[:, h, :], half(bank, h), X[:, h, :], ALU.add).then_inc(s_x_new, 1)

            rstd(0)
            scale_half(0, mem_rows[:, 0, :], mem_rows[:, 0, :])
            dve.wait_ge(s_params_T, 1)
            v.tensor_copy(par[:, :], PS[:, 7, 0:128]).then_inc(s_params_cols, 1)
            rstd(1)
            scale_half(1, HN[:, 0, :], X[:, 0, :])
            dve.wait_ge(s_params_cols, 1)
            evac_T(1, 0, memT, "g_mem_kv")
            evac_T(2, 4, HT, "g_mix")
            dve.wait_ge(s_ring_used, 8)
            v.tensor_copy(tk(buf(9), 512), PS[:, 4:8, :]).then_inc(s_kv_evac, 1)
            dve.wait_ge(s_ring_used, 16)
            v.tensor_copy(v_rows, PS[:, 4:6, :]).then_inc(s_win_evac, 1)
            v.tensor_copy(u_T, banks(6, 2, S)).then_inc(s_win_evac, 1)
            causal = C("causal").unsqueeze(1).to_broadcast([128, HEADS, 128])
            neg = C("neg_diag").unsqueeze(1).to_broadcast([128, HEADS, 128])
            diag = (slice(0, 128), slice(256, 384))
            dve.wait_ge(s_z_done, 1)
            v.tensor_copy(Z, PS[:, :, 0:384]).then_inc(s_z_copied, 1)
            dve.wait_ge(s_z_copied, 1)
            dve.wait_ge(s_z_ln, 1)
            step(v.scalar_tensor_tensor(SP, Z, 0.0, SP, ALU.max, ALU.add))
            for c in diag:
                t = v.tensor_tensor(SP[:, :, c], SP[:, :, c], causal, ALU.mult)
            t.then_inc(s_sp_ready, 1)
            for c in diag:
                t = v.tensor_tensor(Z[:, :, c], Z[:, :, c], neg, ALU.add)
            step(t)
            dve.wait_ge(s_rev_done, 1)
            v.tensor_tensor(Z, Z, PS[:, :, 0:384], ALU.subtract).then_inc(s_arg_ready, 1)
            dve.wait_ge(s_pool_done, 1)
            dve.wait_ge(s_small_loaded, 16 * 6)
            for h in range(TH):
                v.tensor_tensor(HN[:, h, 512:], PS[:, 2 + h, :], scale_bc[:, :], ALU.mult).then_inc(s_pool_scaled, 1)
            dve.wait_ge(s_mix_std, 1)
            v.reciprocal(stat[:, 56:60], stat[:, 52:56]).then_inc(s_mix_rstd, 1)
            dve.wait_ge(s_mix_rstd, 1)
            for h in range(TH):
                t = v.tensor_scalar(HN[:, h, 512:], HN[:, h, 512:], stat[:, 58 + h:59 + h], None, ALU.mult)
            t.then_inc(s_norm_rows, 1)
            evac_T(3, 4, HT, "g_sb_out")
            dve.wait_ge(s_ring_used, 20)
            add_residual(0)
            dve.wait_ge(s_norm_std, 3)
            v.reciprocal(stat[:, 38:40], stat[:, 22:24]).then_inc(s_norm_rstd, 1)
            dve.wait_ge(s_norm_rstd, 3)
            v.tensor_scalar(HN[:, 0, :], X[:, 0, :], stat[:, 38:39], None, ALU.mult).then_inc(s_norm_rows, 1)
            evac_T(4, 4, HT, "g_mem_q")
            dve.wait_ge(s_ring_used, 24)
            v.tensor_scalar(mqT[:, 4:8, :], banks(2, 2, S), 256 ** -0.5, None, ALU.mult).then_inc(s_memq_evac, 1)
            dve.wait_ge(s_score_done, 1)
            step(v.reduce_max(mstat[:, 0:8], banks(4, 4, S), AX))
            v.tensor_scalar(mstat[:, 8:16], mstat[:, 0:8], -1.0, None, ALU.mult).then_inc(s_score_max, 1)
            dve.wait_ge(s_p_exp, 8)
            step(v.reciprocal(mstat[:, 24:32], mstat[:, 16:24]))
            v.tensor_tensor(prob, prob, mstat[:, 24:32].unsqueeze(2).to_broadcast([128, 8, S]), ALU.mult)\
                .then_inc(s_p_ready, 1)
            dve.wait_ge(s_tr_p, 1)
            v.tensor_copy(probT[:, 4:8, :], banks(2, 2, S)).then_inc(s_pT_evac, 1)
            dve.wait_ge(s_o_done, 1)
            v.tensor_copy(oT[:, 4:8, :], banks(6, 2, S)).then_inc(s_oT_evac, 1)
            dve.wait_ge(s_ring_used, 28)
            add_residual(0)
            dve.wait_ge(s_norm_std, 4)
            v.reciprocal(stat[:, 40:42], stat[:, 24:26]).then_inc(s_norm_rstd, 1)
            dve.wait_ge(s_norm_rstd, 4)
            v.tensor_scalar(HN[:, 0, :], X[:, 0, :], stat[:, 40:41], None, ALU.mult).then_inc(s_norm_rows, 1)
            evac_T(5, 4, HT, "g_ffn")
            dve.wait_ge(s_logits_done, 1)
            step(v.tensor_copy(lg[:, :, :], PS[:, 0, 0:64].rearrange("p (h e) -> p h e", h=TH)))
            for h in range(TH):
                t = v.max(top8[:, h, :], lg[:, h, :])
            step(t)
            for h in range(TH):
                v.tensor_scalar(stat[:, 60 + h:61 + h], top8[:, h, 0:1], -1.0, None, ALU.mult)
                t = v.max_index(idx8[:, h, :], top8[:, h, :], lg[:, h, :])
            t.then_inc(s_top_ready, 1)
            dve.wait_ge(s_top_ready, 1)
            step(v.tensor_copy(idxf[:, :, :], idx8[:, :, :]))
            for h in range(TH):
                t = v.tensor_tensor(hot[:, h, :, :], C("iota32").unsqueeze(1).to_broadcast([128, 4, N_EXP]),
                                    idxf[:, h, 0:4].unsqueeze(2).to_broadcast([128, 4, N_EXP]), ALU.is_equal)
            step(t)
            v.tensor_reduce(mask[:, :, :], hot[:, :, :, :].rearrange("p h k e -> p h e k"), AX, ALU.add)\
                .then_inc(s_mask_ready, 1)
            dve.wait_ge(s_top_exp, 1)
            dve.wait_ge(s_mask_ready, 1)
            step(v.tensor_tensor(lg[:, :, :], lg[:, :, :], mask[:, :, :], ALU.mult))
            step(v.tensor_reduce(stat[:, 62:64], lg[:, :, :], AX, ALU.add))
            step(v.reciprocal(stat[:, 64:66], stat[:, 62:64]))
            v.tensor_tensor(gate[:, :, 0:N_EXP], lg[:, :, :], stat[:, 64:66].unsqueeze(2).to_broadcast([128, TH, N_EXP]),
                            ALU.mult).then_inc(s_gates_ready, 1)
            dve.wait_ge(s_rank_done, 1)
            step(v.scalar_tensor_tensor(slot_of[:, :, 0:N_EXP], PS[:, 1, 0:64].rearrange("p (h e) -> p h e", h=TH), 1.0,
                                        mask[:, :, :], ALU.add, ALU.mult))
            step(v.tensor_scalar(slot_of[:, :, 0:N_EXP], slot_of[:, :, 0:N_EXP], -1.0, None, ALU.add))
            dve.wait_ge(s_ov_sc, 1)

            def set_pick(col):
                for h in range(TH):
                    t = v.tensor_scalar(pick[:, h, :], C("iota")[:, 0:CAP], col(h), None, ALU.is_equal)
                return t

            def set_gpick(col, e):
                for h in range(TH):
                    t = v.tensor_scalar(gpick[:, h, :], C("iota"), col(h), gate[:, h, bass.ds(e, 1)], ALU.is_equal,
                                        ALU.mult)
                return t

            def copy_xT():
                return v.tensor_tensor(xT_e, banks(0, 1, CAP), Pn("g_ffn", KT, CAP), ALU.mult)

            def clip_gate():
                return v.tensor_scalar(g7, PS[:, 2, :], 7.0, None, ALU.min)

            def clip_up():
                return v.tensor_scalar(u7, PS[:, 3, :], 7.0, -7.0, ALU.min, ALU.max)

            def up_gate():
                return v.scalar_tensor_tensor(gu, u7, 1.0, g7, ALU.add, ALU.mult)

            def activate():
                return v.tensor_tensor(act_e, gu, sig, ALU.mult)

            set_pick(lambda h: slot_of[:, h, 0:1]).then_inc(s_pe_ready, 1)
            step(v.reduce_max(stat[0:1, 66:67], PS[0:1, 1, 64:96], AX))
            v.tensor_scalar(flag[0:1, 0:1], stat[0:1, 66:67], float(CAP), None, ALU.is_gt).then_inc(s_flag_ready, 1)
            dve.wait_ge(s_gates_ready, 1)
            for h in range(TH):
                t = v.tensor_scalar(gpick[:, h, :], C("iota"), slot_of[:, h, 0:1], gate[:, h, 0:1], ALU.is_equal, ALU.mult)
            t.then_inc(s_gp_ready, 1)
            dve.wait_ge(s_gT_done, 1)
            v.tensor_copy(gT[0:N_EXP, :], PS[0:N_EXP, 2, 0:256]).then_inc(s_gT_evac, 1)
            dve.wait_ge(s_gathered, 1)
            copy_xT().then_inc(s_xT_ready, 1)

            with dve.Fori(0, N_EXP) as e:
                dve.wait_ge(s_gathered, e + 1)
                set_pick(lambda h: slot_of[:, h, bass.ds(e + 1, 1)]).then_inc(s_pe_ready, 1)
                dve.wait_ge(s_ring_used, e * PER + (NPRE + 8))
                clip_gate().then_inc(s_sig_in, 1)
                clip_up().then_inc(s_gu_free, 1)
                dve.wait_ge(s_gu_free, e + 2)
                up_gate().then_inc(s_gu_made, 1)
                dve.wait_ge(s_gu_made, e + 1)
                dve.wait_ge(s_sig_out, e + 1)
                activate().then_inc(s_act_ready, 1)
                dve.wait_ge(s_gathered, e + 2)
                copy_xT().then_inc(s_xT_ready, 1)
                dve.wait_ge(s_gpt_done, e + 1)
                set_gpick(lambda h: slot_of[:, h, bass.ds(e + 1, 1)], e + 1).then_inc(s_gp_ready, 1)
            dve.wait_ge(s_scattered, N_EXP)
            dve.wait_ge(s_flag_ready, 1)
            over = v.value_load(flag[0:1, 0:1], min_val=0, max_val=1)
            with v.If(over > 0):
                NB = N_BLK - 1
                with dve.Fori(0, N_EXP) as e:
                    for b in range(NB):
                        dve.wait_ge(s_ov_sc, e * NB + (b + 1))
                        for h in range(TH):
                            t = v.tensor_scalar(ov_slot[:, h:h + 1], slot_of[:, h, bass.ds(e, 1)], -float(CAP * (b + 1)), None,
                                                ALU.add)
                        t.then_inc(s_ov_base, 1)
                        dve.wait_ge(s_ov_base, e * NB + (b + 1))
                        set_pick(lambda h: ov_slot[:, h:h + 1])
                        set_gpick(lambda h: ov_slot[:, h:h + 1], e).then_inc(s_pe_ready, 1)
                        dve.wait_ge(s_gathered, e * NB + (N_EXP + 1 + b + 1))
                        copy_xT().then_inc(s_xT_ready, 1)
                        dve.wait_ge(s_ov_up, e * NB + (b + 1))
                        clip_gate().then_inc(s_sig_in, 1)
                        clip_up().then_inc(s_gu_free, 1)
                        dve.wait_ge(s_gu_free, e * NB + (N_EXP + 1 + b + 1))
                        up_gate().then_inc(s_gu_made, 1)
                        dve.wait_ge(s_gu_made, e * NB + (N_EXP + b + 1))
                        dve.wait_ge(s_sig_out, e * NB + (N_EXP + b + 1))
                        activate().then_inc(s_act_ready, 1)
                dve.wait_ge(s_ov_sc, N_EXP * NB + 1)
            add_residual(4)

            dve.wait_ge(s_norm_std, 5)
            v.reciprocal(stat[:, 42:44], stat[:, 26:28]).then_inc(s_norm_rstd, 1)
            dve.wait_ge(s_norm_rstd, 5)
            dve.wait_ge(s_g_loaded, 32)
            for h in range(TH):
                v.scalar_tensor_tensor(X[:, h, :], X[:, h, :], stat[:, 42 + h:43 + h], g_final, ALU.mult, ALU.mult)\
                    .then_inc(s_norm_rows, 1)
            dve.wait_ge(s_norm_std, 6)
            v.reciprocal(stat[:, 44:46], stat[:, 28:30]).then_inc(s_norm_rstd, 1)
            dve.wait_ge(s_norm_rstd, 6)
            v.tensor_scalar(HN[:, 0, :], X[:, 0, :], stat[:, 44:45], None, ALU.mult).then_inc(s_norm_rows, 1)
            evac_T(6, 0, HT, "g_pre_2")
            dve.wait_ge(s_ring_used, MOE_END + 1)
            v.tensor_copy(lora, PS[:, 4, 0:256]).then_inc(s_lora_evac, 1)
            dve.wait_ge(s_lora_evac, 1)
            v.tensor_tensor(lora_d[:, 1:], lora[:, 0:S - 1], lora[:, 1:], ALU.subtract)
            step(v.tensor_scalar(lora_d[:, 0:1], lora[:, 0:1], -1.0, None, ALU.mult))
            v.scalar_tensor_tensor(lora, lora_d, P("mu_shift_2", 16), lora, ALU.mult, ALU.add).then_inc(s_lora_mix, 1)
            dve.wait_ge(s_ring_used, MOE_END + 9)
            v.tensor_copy(rwT[:, 8:16, :], banks(4, 4, S)).then_inc(s_rw_evac, 1)
            dve.wait_ge(s_rw_evac, 2)
            v.tensor_tensor(diff[:, :, 1:], rwT[:, :, 0:S - 1], rwT[:, :, 1:], ALU.subtract)
            step(v.tensor_scalar(diff[:, :, 0:1], rwT[:, :, 0:1], -1.0, None, ALU.mult))
            for j in range(16):
                t = v.scalar_tensor_tensor(rwT[:, j, :], diff[:, j, :], P("mu_shift_2", j), rwT[:, j, :], ALU.mult, ALU.add)
            t.then_inc(s_rw_mix, 1)
            dve.wait_ge(s_rw_mix, 1)
            rr, kr, vr, zr = (tk(x, S) for x in (rT, rw_k, rw_v, rw_z))
            step(v.tensor_tensor(tk(kk, S), kr, Pn("k_k_2", 4, S), ALU.mult))
            v.tensor_tensor(kk_sq, kk, kk, ALU.mult).then_inc(s_kk_sq, 1)
            dve.wait_ge(s_ring_used, MOE_END + 17)
            v.tensor_copy(v2, PS[:, 4:6, :]).then_inc(s_a_evac, 1)
            v.tensor_copy(za, banks(6, 2, S)).then_inc(s_a_evac, 1)
            dve.wait_ge(s_wl_sig, 8)
            step(v.tensor_tensor_scan(cum, C("chunk_reset"), sg, 0.0, ALU.mult, ALU.add))
            v.tensor_tensor(sg, cum, sg, ALU.subtract).then_inc(s_wkv_cum, 1)
            step(v.scalar_tensor_tensor(tk(k2, S), tk(rate, S), 1.0, Pn("k_a_2", 4, S), ALU.subtract, ALU.mult))
            step(v.scalar_tensor_tensor(k2, k2, 1.0, rw_k, ALU.add, ALU.mult))
            step(v.tensor_tensor(tk(bon_in, S), rr, Pn("r_k_2", 4, S), ALU.mult))
            v.tensor_tensor(bon_in, bon_in, k2, ALU.mult).then_inc(s_bon_in, 1)
            dve.wait_ge(s_kk_sqrt, 1)
            step(v.tensor_scalar(kk_inv, kk_inv, 1e-12, None, ALU.max))
            step(v.reciprocal(kk_inv, kk_inv))
            step(v.tensor_tensor(kk, kk, kk_inv, ALU.mult))
            step(v.tensor_tensor(rate, rate, kk, ALU.mult))
            dve.wait_ge(s_wkv_exp, 3)
            dve.wait_ge(s_bon_sum, 1)
            v.tensor_tensor(bonus, PS[:, 6:8, :].rearrange("p b n -> p (b n)"), rw_v, ALU.mult).then_inc(s_bon_ready, 1)
            v.tensor_copy(dec_end[:, :], tk(dec, L)[:, :, L - 1])
            v.tensor_tensor(rT, rT, dec, ALU.mult)
            v.scalar_tensor_tensor(aT, kk, -1.0, dec_prev, ALU.mult, ALU.mult)
            step(v.tensor_tensor(bT, rate, dec_inv, ALU.mult))
            v.tensor_tensor(kTl, k2, dec_inv, ALU.mult).then_inc(s_wkv_T, 1)
            dve.wait_ge(s_za_sig, 1)
            step(v.tensor_tensor(buf(6, 1024), buf(6, 1024), z_sig, ALU.mult))
            dve.wait_ge(s_moba_s, 1)
            dve.wait_ge(s_bias_read, 32)
            for c, b in ((0, 0), (1, 1), (2, 0)):
                t = v.tensor_tensor(prob2[:, :, 128 * c:128 * c + 128], PS[:, :, 128 * c:128 * c + 128], bias[:, :, b, :], ALU.add)
            step(t)
            v.reduce_max(mstat[:, 0:8], prob2[:, :, 0:128], AX)
            step(v.reduce_max(mstat[:, 8:16], prob2[:, :, 128:384], AX))
            v.tensor_scalar(mstat[:, 16:32], mstat[:, 0:16], -1.0, None, ALU.mult).then_inc(s_moba_max, 1)
            dve.wait_ge(s_moba_exp, 16)
            step(v.reciprocal(mstat[:, 48:64], mstat[:, 32:48]))
            v.tensor_tensor(prob2[:, :, 0:128], prob2[:, :, 0:128], mstat[:, 48:56].unsqueeze(2).to_broadcast([128, 8, 128]),
                            ALU.mult)
            v.tensor_tensor(prob2[:, :, 128:384], prob2[:, :, 128:384],
                            mstat[:, 56:64].unsqueeze(2).to_broadcast([128, 8, 256]), ALU.mult).then_inc(s_moba_p, 1)
            dve.wait_ge(s_moba_tr, 1)
            v.tensor_copy(prob2T[:, 4:8, :], PS[:, 4:8, 0:384]).then_inc(s_moba_pT, 1)
            dve.wait_ge(s_moba_o, 1)
            v.tensor_tensor(ya, banks(0, 2, S), za, ALU.mult).then_inc(s_ya_ready, 1)

            def flat(bank):
                return PS[:, bank:bank + 2, :].rearrange("p b n -> p (b n)")

            def masked(name):
                return C(name).unsqueeze(1).to_broadcast([128, NSET, L])

            for i, (dst, bank) in enumerate(((v_tok, 2), (b_tok, 4), (k_tok, 6))):
                dve.wait_ge(s_rows_done, i + 1)
                v.tensor_copy(dst, flat(bank)).then_inc(s_rows_evac, 1)
            for i, (dst, name, bank) in ((0, (b0, "up_diag", 0)), (0, (offT, "up_off", 0)), (1, (a0, "low_diag", 2)),
                                         (2, (akT, "up_strict", 4)), (3, (rbT, "up_incl", 6)), (4, (rkT, "up_incl", 0))):
                dve.wait_ge(s_mat_done, i + 1)
                t = v.tensor_tensor(tk(dst, L), banks(bank, 2, L), masked(name), ALU.mult)
                t.then_inc(s_mat_evac, 1)
            dve.wait_ge(s_mat_evac, 6)
            v.tensor_tensor(tk(E1, L), tk(b0, L), masked("eye64"), ALU.add)
            v.tensor_tensor(tk(F1, L), tk(a0, L), masked("eye64"), ALU.add).then_inc(s_sol_ready, 1)
            dve.wait_ge(s_sol_ready, 1)
            for i, (dst, plus) in enumerate(SOLVED):
                dve.wait_ge(s_sol_done, i + 1)
                if plus is None:
                    t = v.tensor_copy(dst, flat(2 * (i % 4)))
                else:
                    t = v.tensor_tensor(dst, flat(2 * (i % 4)), plus, ALU.add)
                t.then_inc(s_sol_evac, 1)
            for c in range(NCH):
                dve.wait_ge(s_rec_x, c + 1)
                v.tensor_copy(rec_rhs, tk(PS[:, 0, 0:256], L)).then_inc(s_rec_xe, 1)
                dve.wait_ge(s_rec_sa, c + 1)
                v.tensor_copy(rec_sa, tk(PS[:, 1, 0:256], L)).then_inc(s_rec_sae, 1)
                if c < NCH - 1:
                    end = dec_end[:, :].rearrange("p (j c) -> p j c", c=NCH)[:, :, c].unsqueeze(2).to_broadcast([128, 4, HD])
                    new = state[(c + 1) % 2]
                    dve.wait_ge(s_rec_s, c + 1)
                    if c >= 2:
                        dve.wait_ge(s_y_psum, c - 1)
                    if c:
                        step(v.tensor_tensor(new, tk(PS[:, 2, 0:256], L), state[c % 2], ALU.add))
                        v.tensor_tensor(new, new, end, ALU.mult).then_inc(s_rec_state, 1)
                    else:
                        v.tensor_tensor(new, tk(PS[:, 2, 0:256], L), end, ALU.mult).then_inc(s_rec_state, 1)
            dve.wait_ge(s_y_psum, NCH)
            v.tensor_copy(yT, flat(4)).then_inc(s_yT_evac, 1)
            dve.wait_ge(s_zb_sig, 1)
            step(v.tensor_tensor(rw_z, rw_z, z_sig, ALU.mult))
            dve.wait_ge(s_gn_mean, 1)
            step(v.scalar_tensor_tensor(yT, flat(6), -1.0 / HD, yT, ALU.mult, ALU.add))
            v.tensor_tensor(ysq, yT, yT, ALU.mult).then_inc(s_gn_sq, 1)
            dve.wait_ge(s_gn_std, 1)
            step(v.reciprocal(ystd, ystd))
            step(v.tensor_tensor(yT, yT, ystd, ALU.mult))
            for j in range(4):
                t = v.tensor_scalar(tk(yT, S)[:, j, :], tk(yT, S)[:, j, :], P("ln_x_w_2", j), P("ln_x_b_2", j), ALU.mult, ALU.add)
            step(t)
            step(v.tensor_tensor(yT, yT, bonus, ALU.add))
            v.tensor_tensor(yT, yT, rw_z, ALU.mult).then_inc(s_yb_ready, 1)
            dve.wait_ge(s_gate_evac, 2)
            dve.wait_ge(s_ring_used, MOE_END + 27)
            v.tensor_tensor(gate_a, gate_a, banks(0, 4, S), ALU.mult)
            dve.wait_ge(s_ring_used, MOE_END + 29)
            step(v.tensor_tensor(gate_b, gate_b, banks(4, 4, S), ALU.mult))
            v.tensor_tensor(merged, gate_a, gate_b, ALU.add).then_inc(s_merged_ready, 1)
            dve.wait_ge(s_ple_pT, 1)
            v.tensor_copy(pT, banks(4, 1, S)).then_inc(s_ple_pTe, 1)
            dve.wait_ge(s_norm_std, 7)
            step(v.reciprocal(stat[:, 46:48], stat[:, 30:32]))
            for h in range(TH):
                step(v.scalar_tensor_tensor(HN[:, h, :], half(0, h), stat[:, 46 + h:47 + h], g_post, ALU.mult, ALU.mult))
                v.tensor_tensor(X[:, h, :], X[:, h, :], HN[:, h, :], ALU.add).then_inc(s_h2_ready, 1)
            evac_T(7, 0, HT, None)
            for h in range(TH):
                dve.wait_ge(s_pg_sig, h + 1)
                dve.wait_ge(s_h2_ready, 2)
                step(v.tensor_tensor(HN[:, h, :], pg_sig[:, h, :], half(4, h), ALU.mult))
                v.tensor_tensor(HN[:, h, :], HN[:, h, :], X[:, h, :], ALU.add).then_inc(s_out_ready, 1)



_INS = ["x", "mem", "w_in", "w_pool", "pool_scale", "w_out", "w_mem_q", "w_mem_kv", "w_mem_o", "w_router", "b_router",
        "w_expert_in", "b_expert_in", "w_expert_out", "b_expert_out", "g_final", "p_2", "w_in_2", "rel_bias_2",
        "w_up_2", "a_up_2", "p_a_2", "p_b_2", "w_out_2", "g_post_2", "w_ple_up_2", "w_ple_gate_2"]


def kernel(**inputs):
    import numpy as _np
    import concourse.bacc as _bacc
    from concourse import mybir as _mybir
    from concourse.bass_utils import run_bass_kernel_spmd as _run

    nc = _bacc.Bacc("TRN2", target_bir_lowering=False, num_devices=1)
    given = {n: _np.ascontiguousarray(inputs[n]) for n in _INS}
    given["params"] = _np.concatenate([_np.asarray(inputs[n]).reshape(-1, 128) for n, _ in PARAMS]
                                      + [_np.zeros((128 - P_ROWS, 128), _np.float32)], axis=0)
    given["consts"] = constants()
    arrays, args = {}, {}
    for name, v in given.items():
        arrays[f"in_{name}_dram"] = v
        args[name] = nc.dram_tensor(f"in_{name}_dram", v.shape, _mybir.dt.from_np(v.dtype), kind="ExternalInput").ap()
    out = nc.dram_tensor("out_0_dram", (1, S, D), _mybir.dt.float32, kind="ExternalOutput").ap()
    two_blocks(nc, args, out)
    r = _run(nc, [arrays], core_ids=[0])
    return r.results[0]["out_0_dram"]
```

```python
import math
from contextlib import ExitStack

import numpy as np
import concourse.bass as bass
from concourse import mybir

D = 1024
S = 256
KT = D // 128
TH = S // 128
SLOTS = 12
SLOT = 2048
N_EXP = 32
CAP = 64
N_BLK = S // CAP
NEG = -1.0e30
HEADS = 8
HD = 64
L = 64
NCH = S // L
NSET = 4 * NCH
DECAY = math.exp(-0.5)

PARAMS = [("g_mix", 8), ("g_sb_out", 4), ("g_pool_out", 4), ("g_mem_q", 8), ("g_mem_kv", 8), ("g_ffn", 8),
          ("g_pre_2", 8), ("mu_shift_2", 17), ("w0_2", 4), ("a0_2", 4), ("k_k_2", 4), ("k_a_2", 4),
          ("r_k_2", 4), ("ln_x_w_2", 4), ("ln_x_b_2", 4)]
P_AT, _at = {}, 0
for _n, _r in PARAMS:
    P_AT[_n] = _at
    _at += _r
P_ROWS = _at

CONSTS = [("ident", 128), ("tri_ge", 128), ("tri_lt", 128), ("ones", 128), ("head_ones", 128), ("iota", 128),
          ("causal", 128), ("neg_diag", 128), ("iota32", 32), ("up_strict", 64), ("up_incl", 64),
          ("up_diag", 64), ("up_off", 64), ("low_diag", 64), ("eye64", 64), ("bias_sel", 512), ("inv_count", 1024), ("chunk_reset", 1024)]
C_AT, _at = {}, 0
for _n, _r in CONSTS:
    C_AT[_n] = (_at, _at + _r)
    _at += _r
C_COLS = _at
LATE = C_AT["iota32"][0]


def constants():
    c = np.zeros((128, C_COLS), np.float32)

    def put(name, value):
        c[:value.shape[0], C_AT[name][0]:C_AT[name][1]] = value

    p = np.arange(128)
    put("ident", np.eye(128))
    put("tri_ge", p[:, None] >= p[None, :])
    put("tri_lt", p[:, None] < p[None, :])
    put("ones", np.ones((128, 128)))
    put("head_ones", p[:, None] // HD == p[None, :] // HD)
    put("iota", np.tile(p % CAP, (128, 1)))
    put("causal", p[:, None] < p[None, :])
    put("neg_diag", np.where(p[:, None] < p[None, :], 0.0, NEG))
    put("iota32", np.tile(np.arange(32), (128, 1)))
    r, q = p[:, None] % L, np.arange(L)[None, :]
    put("up_strict", r < q)
    put("up_incl", r <= q)
    near = r // 16 == q // 16
    put("up_diag", (r < q) & near)
    put("up_off", (r < q) & ~near)
    put("low_diag", (r > q) & near)
    put("eye64", r == q)
    dist = 255 - np.arange(512)
    n = np.maximum(dist, 0)
    large = 16 + (np.log(np.maximum(n, 1).astype(np.float32) / np.float32(16)) / np.float32(math.log(8.0))
                  * np.float32(16)).astype(np.int32)
    bucket = np.where(n < 16, n, np.minimum(large, 31))
    sel = np.zeros((33, 512))
    sel[:32] = (np.arange(32)[:, None] == bucket[None, :]) & (dist >= 0)[None, :]
    sel[32] = np.where(dist >= 0, 0.0, NEG)
    put("bias_sel", sel)
    cnt = np.stack([1.0 / np.minimum(np.arange(S) + 1, w) for w in (2, 4, 8, 16)])
    put("inv_count", np.tile(cnt.reshape(1, -1), (128, 1)))
    put("chunk_reset", np.tile((np.arange(1024) % L != 0)[None, :], (128, 1)))
    return c


def two_blocks(nc, a, out):
    f32, i32, u32 = mybir.dt.float32, mybir.dt.int32, mybir.dt.uint32
    ALU, ACT = mybir.AluOpType, mybir.ActivationFunctionType
    AX = mybir.AxisListType.X
    ctx = ExitStack()
    with ctx:
        def sb(name, shape, dt=f32):
            return ctx.enter_context(nc.sbuf_tensor(name, shape, dt))

        ring = sb("ring", [128, SLOTS * SLOT])
        big = sb("big", [128, 10 * 2048])
        cst = sb("cst", [128, C_COLS])
        par_rows = sb("par_rows", [128, 128])
        par = sb("par", [128, 128])
        w_pool = sb("w_pool_sb", [128, 512])
        scale_bc = sb("scale_bc", [128, 512])
        w_router = sb("w_router_sb", [128, KT, N_EXP])
        b_router = sb("b_router_sb", [1, N_EXP])
        stat = sb("stat", [128, 96])
        eps = sb("eps", [128, 4])
        mstat = sb("mstat", [128, 64])
        dec_end = sb("dec_end", [128, NSET])
        lora_w = sb("lora_w", [128, 512])
        rbias = sb("rbias", [33, HEADS])
        lg = sb("lg", [128, TH, N_EXP])
        top8 = sb("top8", [128, TH, 8])
        idx8 = sb("idx8", [128, TH, 8], u32)
        idxf = sb("idxf", [128, TH, 8])
        hot = sb("hot", [128, TH, 4, N_EXP])
        mask = sb("mask", [128, TH, N_EXP])
        gate = sb("gate", [128, TH, N_EXP + 1])
        slot_of = sb("slot_of", [128, TH, N_EXP + 1])
        ov_slot = sb("ov_slot", [128, TH])
        flag = sb("flag", [1, 1], i32)

        def buf(n, lo=0, hi=2048):
            return big[:, 2048 * n + lo:2048 * n + hi]

        def slot(n, lo=0, hi=SLOT):
            return ring[:, SLOT * n + lo:SLOT * n + hi]

        def C(name):
            return cst[:, C_AT[name][0]:C_AT[name][1]]

        def P(name, k=0):
            return par[:, P_AT[name] + k:P_AT[name] + k + 1]

        def Pn(name, n, inner):
            return par[:, P_AT[name]:P_AT[name] + n].unsqueeze(2).to_broadcast([128, n, inner])

        def tk(ap, t):
            return ap.rearrange("p (k t) -> p k t", t=t)

        ident, ones = C("ident"), C("ones")
        X, HN = tk(buf(0), D), tk(buf(1), D)
        HT = tk(buf(2), S)
        qkT = tk(buf(3), S)
        v_rows = tk(buf(4, 0, 1024), 512)
        u_T = tk(buf(4, 1024), S)
        pooled = tk(buf(2, 0, 1024), S)
        win = [buf(2, 1024 + 256 * n, 1280 + 256 * n) for n in range(3)]
        Z = tk(big[:, 5 * 2048:5 * 2048 + 3072], 384)
        SP = tk(big[:, 5 * 2048 + 3072:8 * 2048], 384)
        mem_rows, memT = tk(buf(5), D), tk(buf(6), S)
        mkT, mv_rows = tk(buf(8), S), tk(buf(9), D)
        mqT = tk(buf(3), S)
        prob = tk(buf(5), S)
        probT = tk(buf(6), S)
        oT = tk(buf(7), S)
        xT_e = tk(buf(3, 0, 512), CAP)
        actT = buf(3, 512, 1024).rearrange("p (b h c) -> p b h c", b=4, h=2)
        y_e, gpT = buf(3, 1024, 1536), buf(3, 1536, 1792)
        g7, u7 = buf(4, 0, 512), buf(4, 512, 1024)
        sig, gu = buf(4, 1024, 1536), buf(4, 1536, 2048)
        act_e = buf(5, 0, 512)
        pick = tk(buf(5, 512, 640), CAP)
        gpick = tk(buf(5, 640, 896), 128)
        b2_all, gT = buf(6, 0, 1024), buf(6, 1024, 1280)
        b1_rows = C("inv_count")
        frow = buf(6, 1280, 1792)
        g_final, g_post = buf(8, 0, 1024), buf(8, 1024, 2048)
        bias = buf(9).rearrange("p (h b s) -> p h b s", h=HEADS, b=2)
        arr = [slot(s, lo, lo + 1024) for s in (8, 9, 10, 11, 0, 1, 2, 3) for lo in (0, 1024)]
        rwT = tk(big[:, 3 * 2048:5 * 2048], S)
        diff = tk(big[:, 5 * 2048:7 * 2048], S)
        qk2 = tk(buf(5), S)
        v2, za = tk(buf(6, 0, 1024), 512), tk(buf(6, 1024), S)
        lora, lora_d, lora_t = buf(7, 0, 256), buf(7, 256, 512), buf(7, 512, 768)
        z_sig = buf(7, 1024)
        p_rows, pT = tk(buf(8, 0, 512), 256), tk(buf(8, 512, 1024), S)
        gate_a, gate_b = tk(buf(1), S), tk(buf(2), S)
        prob2, prob2T = tk(ring[:, 0:3072], 384), tk(ring[:, 3072:6144], 384)
        ya = za
        rT, rw_k, rw_v, rw_z = buf(3, 0, 1024), buf(3, 1024), buf(4, 0, 1024), buf(4, 1024)
        sg, cum, dec, dec_inv, dec_prev, rate, kk, kk_sq = arr[:8]
        k2, kk_inv = arr[14:16]
        bon_in = buf(1, 0, 1024)
        bonus = cum
        aT, bT, kTl = dec_prev, rate, dec_inv
        r_dec = kk_sq
        v_tok, b_tok, k_tok, b0, a0, akT, rbT, rkT = arr[8:16]
        offT, F, eye = sg, dec, rate
        a2, b2, a4, b4, b8 = kk, rT, buf(5, 0, 1024), buf(5, 1024), rw_k
        m1, m1T, ET, m2, t7, invT = rT, buf(5, 1024), buf(5, 0, 1024), dec, kk, dec_inv

        def pair_of(x0, x1):
            return bass.AP(x0.tensor, x0.offset, [list(x0.ap[0]), [x1.offset - x0.offset, 2], [1, 1024]])

        a_r, F_a2, off_eye = pair_of(aT, r_dec), pair_of(F, a2), pair_of(offT, eye)
        SOLVE = [(b0, a0, [(a2, None)]), (a0, b0, [(b2, None)]), (b2, F_a2, [(F, F), (a4, None)]),
                 (a2, b2, [(b4, None)]), (b4, F, [(F, F)]), (a4, b4, [(b8, None)]), (b8, F, [(F, F)]),
                 (F, off_eye, [(m1, None), (ET, None)]), (offT, F, [(m1T, None)]),
                 (m1, m1T, [(m2, None)]), (m1T, ET, [(t7, ET)]), (m2, t7, [(invT, t7)])]
        rec_rhs, rec_sa = tk(buf(7, 0, 256), HD), tk(buf(7, 256, 512), HD)
        state = tk(buf(7, 512, 768), HD), tk(buf(7, 768, 1024), HD)
        yT, ysq, ystd = sg, dec, kk
        e_rows = tk(slot(0), D)
        yb = tk(yT, S)
        merged = tk(buf(5), S)
        pg_sig = tk(buf(5), D)

        PS = ctx.enter_context(nc.psum_tensor("PS", [128, 8, 512], f32))

        def banks(lo, n, t):
            return PS[:, lo:lo + n, :].rearrange("p b (k t) -> p (b k) t", t=t)

        def sem(name):
            return ctx.enter_context(nc.semaphore(name))

        s_x_loaded = sem("s_x_loaded")
        s_mem_loaded = sem("s_mem_loaded")
        s_ring_used = sem("s_ring_used")
        s_b1_loaded = sem("s_b1_loaded")
        s_flag_ready = sem("s_flag_ready")
        s_ov_sc = sem("s_ov_sc")
        s_ov_loaded = sem("s_ov_loaded")
        s_out_ready = sem("s_out_ready")
        s_out_written = sem("s_out_written")
        s_norm_tr = sem("s_norm_tr")
        s_const_loaded = sem("s_const_loaded")
        s_param_loaded = sem("s_param_loaded")
        s_params_T = sem("s_params_T")
        s_norm_rows = sem("s_norm_rows")
        s_params_cols = sem("s_params_cols")
        s_norm_T = sem("s_norm_T")
        s_kv_evac = sem("s_kv_evac")
        s_win_evac = sem("s_win_evac")
        s_z_done = sem("s_z_done")
        s_sp_ready = sem("s_sp_ready")
        s_rev_done = sem("s_rev_done")
        s_w_ready = sem("s_w_ready")
        s_sb_done = sem("s_sb_done")
        s_pooled_ready = sem("s_pooled_ready")
        s_small_loaded = sem("s_small_loaded")
        s_pool_done = sem("s_pool_done")
        s_memq_evac = sem("s_memq_evac")
        s_score_done = sem("s_score_done")
        s_p_ready = sem("s_p_ready")
        s_tr_p = sem("s_tr_p")
        s_pT_evac = sem("s_pT_evac")
        s_o_done = sem("s_o_done")
        s_oT_evac = sem("s_oT_evac")
        s_logits_done = sem("s_logits_done")
        s_late_loaded = sem("s_late_loaded")
        s_rbias_ready = sem("s_rbias_ready")
        s_frow_done = sem("s_frow_done")
        s_mask_ready = sem("s_mask_ready")
        s_rank_done = sem("s_rank_done")
        s_gates_ready = sem("s_gates_ready")
        s_gT_done = sem("s_gT_done")
        s_gT_evac = sem("s_gT_evac")
        s_b2_loaded = sem("s_b2_loaded")
        s_pe_ready = sem("s_pe_ready")
        s_gathered = sem("s_gathered")
        s_frow_evac = sem("s_frow_evac")
        s_xT_ready = sem("s_xT_ready")
        s_gu_free = sem("s_gu_free")
        s_gp_ready = sem("s_gp_ready")
        s_gpt_done = sem("s_gpt_done")
        s_act_ready = sem("s_act_ready")
        s_gpt_evac = sem("s_gpt_evac")
        s_actT_done = sem("s_actT_done")
        s_actT_evac = sem("s_actT_evac")
        s_y_evac = sem("s_y_evac")
        s_scattered = sem("s_scattered")
        s_ov_up = sem("s_ov_up")
        s_ov_down = sem("s_ov_down")
        s_lora_evac = sem("s_lora_evac")
        s_rw_evac = sem("s_rw_evac")
        s_a_evac = sem("s_a_evac")
        s_tanh_ready = sem("s_tanh_ready")
        s_wl_done = sem("s_wl_done")
        s_kk_sq = sem("s_kk_sq")
        s_kk_sum = sem("s_kk_sum")
        s_bon_in = sem("s_bon_in")
        s_bon_sum = sem("s_bon_sum")
        s_wl_sig = sem("s_wl_sig")
        s_bon_ready = sem("s_bon_ready")
        s_gate_evac = sem("s_gate_evac")
        s_moba_s = sem("s_moba_s")
        s_moba_p = sem("s_moba_p")
        s_moba_read = sem("s_moba_read")
        s_eye_set = sem("s_eye_set")
        s_pa_used = sem("s_pa_used")
        s_e_evac = sem("s_e_evac")
        s_moba_tr = sem("s_moba_tr")
        s_moba_pT = sem("s_moba_pT")
        s_moba_o = sem("s_moba_o")
        s_wkv_T = sem("s_wkv_T")
        s_ya_ready = sem("s_ya_ready")
        s_rows_done = sem("s_rows_done")
        s_rows_evac = sem("s_rows_evac")
        s_mat_evac = sem("s_mat_evac")
        s_mat_done = sem("s_mat_done")
        s_sol_ready = sem("s_sol_ready")
        s_sol_evac = sem("s_sol_evac")
        s_sol_done = sem("s_sol_done")
        s_rec_state = sem("s_rec_state")
        s_rec_x = sem("s_rec_x")
        s_rec_xe = sem("s_rec_xe")
        s_rec_sa = sem("s_rec_sa")
        s_rec_sae = sem("s_rec_sae")
        s_rec_s = sem("s_rec_s")
        s_y_psum = sem("s_y_psum")
        s_yT_evac = sem("s_yT_evac")
        s_gn_mean = sem("s_gn_mean")
        s_gn_sq = sem("s_gn_sq")
        s_gn_var = sem("s_gn_var")
        s_yb_ready = sem("s_yb_ready")
        s_merged_ready = sem("s_merged_ready")
        s_p_loaded = sem("s_p_loaded")
        s_ple_pT = sem("s_ple_pT")
        s_ple_pTe = sem("s_ple_pTe")
        s_h2_ready = sem("s_h2_ready")
        s_norm_sq = sem("s_norm_sq")
        s_norm_std = sem("s_norm_std")
        s_norm_rstd = sem("s_norm_rstd")
        s_eps_set = sem("s_eps_set")
        s_z_copied = sem("s_z_copied")
        s_z_abs = sem("s_z_abs")
        s_z_ln = sem("s_z_ln")
        s_arg_ready = sem("s_arg_ready")
        s_mix_sq = sem("s_mix_sq")
        s_pool_scaled = sem("s_pool_scaled")
        s_mix_std = sem("s_mix_std")
        s_mix_rstd = sem("s_mix_rstd")
        s_x_new = sem("s_x_new")
        s_score_max = sem("s_score_max")
        s_p_exp = sem("s_p_exp")
        s_g_loaded = sem("s_g_loaded")
        s_top_ready = sem("s_top_ready")
        s_top_exp = sem("s_top_exp")
        s_bias_written = sem("s_bias_written")
        s_bias_read = sem("s_bias_read")
        s_sig_in = sem("s_sig_in")
        s_sig_out = sem("s_sig_out")
        s_lora_mix = sem("s_lora_mix")
        s_rw_mix = sem("s_rw_mix")
        s_za_sig = sem("s_za_sig")
        s_kk_sqrt = sem("s_kk_sqrt")
        s_wkv_cum = sem("s_wkv_cum")
        s_wkv_exp = sem("s_wkv_exp")
        s_moba_max = sem("s_moba_max")
        s_moba_exp = sem("s_moba_exp")
        s_zb_sig = sem("s_zb_sig")
        s_gn_std = sem("s_gn_std")
        s_pg_sig = sem("s_pg_sig")
        s_pool_chain = sem("s_pool_chain")
        s_dve_chain = sem("s_dve_chain")
        s_gu_made = sem("s_gu_made")
        s_ov_base = sem("s_ov_base")
        s_slot_loaded = [sem(f"s_slot_loaded{i}") for i in range(SLOTS)]

        def rows_of(w, k, n=1):
            return w[k * 128:(k + n) * 128, :].rearrange("(a p) n -> p a n", p=128)

        w_in, w_kv = a["w_in"][0], a["w_mem_kv"][0]
        PRE = ([rows_of(w_kv, k) for k in range(8)] + [rows_of(w_in, k) for k in range(8)]
               + [rows_of(a[n][0], k, 2) for n in ("w_out", "w_mem_q", "w_mem_o") for k in (0, 2, 4, 6)])
        w1, w2, b1 = a["w_expert_in"][0], a["w_expert_out"][0], a["b_expert_in"][0]
        wi2 = a["w_in_2"][0]
        A0, R0, G0 = 0, 4 * 512, 4 * 512 + 2176
        POST = ([wi2[:, R0 + 2048:G0].rearrange("(a p) n -> p a n", p=128)]
                + [rows_of(wi2[:, R0:R0 + 2048], k) for k in range(8)]
                + [rows_of(wi2[:, c:c + 1024], k, 2) for c in (A0, A0 + 1024, G0, G0 + 1024) for k in (0, 2, 4, 6)]
                + [rows_of(a["p_a_2"][0], k, 2) for k in (0, 2)] + [rows_of(a["w_ple_up_2"][0], 0, 2)]
                + [rows_of(a["p_b_2"][0], k, 2) for k in (0, 2)]
                + [rows_of(a[n][0], k, 2) for n in ("w_out_2", "w_ple_gate_2") for k in (0, 2, 4, 6)])
        assert len(POST) == 38
        USED_RW, USED_QK, USED_VZ, USED_GA, USED_GB = 9, 13, 17, 21, 25
        USED_PA, USED_UP, USED_PB, USED_OUT, USED_PG = 27, 28, 30, 34, 38
        NPRE, PER = len(PRE), 12
        MOE_END = NPRE + PER * N_EXP
        FIRST = NPRE % SLOTS
        assert PER == SLOTS and FIRST == 4
        POST_SLOTS = (4, 5, 6, 7)

        def moe_slot(j):
            return (FIRST + j) % SLOTS

        def loads_before(sl):
            return len(range(sl, MOE_END, SLOTS))

        def view(sl, ap):
            return tk(slot(sl, 0, ap.shape[1] * ap.shape[2]), ap.shape[2])

        def bias_view(start):
            return bass.AP(bias_dram.tensor, start, [[512, 128], [128 * 513, HEADS], [1, 128]])

        bias_dram = nc.dram_tensor("bias_rows", [HEADS, 128, 513], f32, kind="Internal").ap()

        block = ctx.enter_context(nc.Block())

        @block.sync
        def _(sp):
            for h in range(TH):
                sp.dma_start(X[:, h, :], a["x"][0, 128 * h:128 * h + 128, :]).then_inc(s_x_loaded, 16)
            for h in range(TH):
                sp.dma_start(mem_rows[:, h, :], a["mem"][0, 128 * h:128 * h + 128, :]).then_inc(s_mem_loaded, 16)
            for n, w in enumerate(PRE):
                if n >= SLOTS:
                    sp.wait_ge(s_ring_used, n - SLOTS + 1)
                sp.dma_start(view(n % SLOTS, w), w).then_inc(s_slot_loaded[n % SLOTS], 16)
            with sp.Fori(0, N_EXP) as e:
                for j in range(PER):
                    sp.wait_ge(s_ring_used, e * PER + NPRE + j - SLOTS + 1)
                    if j < 8:
                        sp.dma_start(slot(moe_slot(j)), w1[bass.ds(e, 1), 128 * j:128 * j + 128, :]
                                     .rearrange("a p n -> p (a n)")).then_inc(s_slot_loaded[moe_slot(j)], 16)
                    else:
                        sp.dma_start(tk(slot(moe_slot(j)), D),
                                     w2[bass.ds(e, 1), 256 * (j - 8):256 * (j - 8) + 256, :]
                                     .rearrange("a (k p) n -> p (a k) n", p=128)).then_inc(s_slot_loaded[moe_slot(j)], 16)
                    if j == 8:
                        sp.dma_start(b1_rows[0:33:32, :], b1[bass.ds(e, 1), :].rearrange("a (b n) -> (a b) n", b=2))\
                          .then_inc(s_b1_loaded, 16)
            sp.wait_ge(s_flag_ready, 1)
            over = sp.value_load(flag[0:1, 0:1], min_val=0, max_val=1)
            with sp.If(over > 0):
                sp.wait_ge(s_ring_used, MOE_END)
                with sp.Fori(0, N_EXP) as e:
                    sp.wait_ge(s_ov_sc, e * (N_BLK - 1) + 1)
                    for j in range(8):
                        sp.dma_start(slot(moe_slot(j)), w1[bass.ds(e, 1), 128 * j:128 * j + 128, :]
                                     .rearrange("a p n -> p (a n)")).then_inc(s_ov_loaded, 16)
                    for j in range(8, PER):
                        sp.dma_start(tk(slot(moe_slot(j)), D),
                                     w2[bass.ds(e, 1), 256 * (j - 8):256 * (j - 8) + 256, :]
                                     .rearrange("a (k p) n -> p (a k) n", p=128)).then_inc(s_ov_loaded, 16)
                    sp.dma_start(b1_rows[0:33:32, :], b1[bass.ds(e, 1), :].rearrange("a (b n) -> (a b) n", b=2))\
                      .then_inc(s_ov_loaded, 16)
                sp.wait_ge(s_ov_sc, N_EXP * (N_BLK - 1) + 1)
            for n, w in enumerate(POST):
                sl = POST_SLOTS[n % 4]
                if n < 4:
                    sp.wait_ge(s_ring_used, MOE_END - PER + n + 1)
                else:
                    sp.wait_ge(s_ring_used, MOE_END + n - 4 + 1)
                sp.dma_start(view(sl, w), w).then_inc(s_slot_loaded[sl], 16)
            for h in range(TH):
                sp.wait_ge(s_out_ready, h + 1)
                sp.dma_start(out[0, 128 * h:128 * h + 128, :], HN[:, h, :]).then_inc(s_out_written, 16)
            sp.wait_ge(s_out_written, 16 * TH)

        @block.tensor
        def _(pe):
            mm, transpose = nc.tensor.matmul, nc.tensor.transpose

            def pre_chunk(n):
                pe.wait_ge(s_slot_loaded[n % SLOTS], 16 * (n // SLOTS + 1))
                return view(n % SLOTS, PRE[n])

            def post_chunk(n):
                sl = POST_SLOTS[n % 4]
                pe.wait_ge(s_slot_loaded[sl], 16 * (loads_before(sl) + n // 4 + 1))
                return view(sl, POST[n])

            def transpose_rows(rows, bank):
                ps = banks(bank, 4, S)
                for k in range(KT):
                    for h in range(TH):
                        t = transpose(ps[:, k, 128 * h:128 * h + 128], rows[:, h, 128 * k:128 * k + 128], ident)
                    if k % 4 == 3:
                        t.then_inc(s_norm_tr, 1)

            def project_T(ps, w, x, first, last):
                for j in range(ps.shape[1]):
                    t = mm(ps[:, j, :], w[:, 128 * j:128 * j + 128], x, start=first and j % 2 == 0,
                           stop=last and j % 2 == 1)
                return t

            def project_rows(bank, xT, k, w, first, last, n=2):
                for h in range(TH):
                    for c in range(n):
                        t = mm(PS[:, bank + n * h + c, :], xT[:, k, 128 * h:128 * h + 128],
                               w[:, 512 * c:512 * c + 512], start=first, stop=last)
                return t

            def rows_from_pairs(n0, chunk, bank, xT):
                for n in range(4):
                    w = chunk(n0 + n)
                    for i in range(2):
                        t = project_rows(bank, xT, 2 * n + i, w[:, i, :], n + i == 0, n + i == 4)
                    t.then_inc(s_ring_used, 1)

            pe.wait_ge(s_const_loaded, 16)
            pe.wait_ge(s_param_loaded, 16)
            transpose(PS[:, 7, 0:128], par_rows[:, :], ident).then_inc(s_params_T, 1)
            pe.wait_ge(s_norm_rows, 2)
            transpose_rows(mem_rows, 0)
            pe.wait_ge(s_norm_rows, 4)
            pe.wait_ge(s_params_cols, 1)
            transpose_rows(HN, 4)

            pe.wait_ge(s_norm_T, 4)
            for k in range(KT):
                w = pre_chunk(k)[:, 0, :]
                project_T(banks(0, 4, S), w, memT[:, k, :], k == 0, k == KT - 1)
                project_rows(4, memT, k, w[:, D:], k == 0, k == KT - 1).then_inc(s_ring_used, 1)

            pe.wait_ge(s_kv_evac, 2)
            for k in range(KT):
                w = pre_chunk(8 + k)[:, 0, :]
                project_T(banks(0, 4, S), w, HT[:, k, :], k == 0, k == KT - 1)
                project_rows(4, HT, k, w[:, 1024:1536], k == 0, k == KT - 1, n=1)
                project_T(banks(6, 2, S), w[:, 1536:2048], HT[:, k, :], k == 0, k == KT - 1)\
                    .then_inc(s_ring_used, 1)

            pe.wait_ge(s_win_evac, 4)
            for h in range(HEADS):
                j, r = h // 2, HD * (h % 2)
                q, k = qkT[r:r + HD, j, :], qkT[r:r + HD, 4 + j, :]
                mm(PS[:, h, 0:256], k[:, 0:128], q, start=True, stop=False)
                t = mm(PS[:, h, 256:384], k[:, 128:256], q[:, 128:256], start=False, stop=True)
            t.then_inc(s_z_done, 1)
            pe.wait_ge(s_sp_ready, 1)
            for h in range(HEADS):
                mm(PS[:, h, 0:256], C("tri_ge"), SP[:, h, 0:256], start=True, stop=False)
                mm(PS[:, h, 128:256], ones, SP[:, h, 256:384], start=False, stop=False)
                t = mm(PS[:, h, 256:384], C("tri_ge"), SP[:, h, 256:384], start=False, stop=True)
            t.then_inc(s_rev_done, 1)
            pe.wait_ge(s_w_ready, 1)
            for h in range(HEADS):
                c = slice(HD * h, HD * h + HD)
                mm(PS[:, 0, c], SP[:, h, 0:128], v_rows[:, 0, c], start=h == 0, stop=h == HEADS - 1)
                mm(PS[:, 1, c], SP[:, h, 128:256], v_rows[:, 0, c], start=h == 0, stop=False)
                t = mm(PS[:, 1, c], SP[:, h, 256:384], v_rows[:, 1, c], start=False, stop=h == HEADS - 1)
            t.then_inc(s_sb_done, 1)
            pe.wait_ge(s_pooled_ready, 4)
            pe.wait_ge(s_small_loaded, 16 * 6)
            for h in range(TH):
                for g in range(4):
                    c = slice(128 * g, 128 * g + 128)
                    t = mm(PS[:, 2 + h, c], pooled[:, g, 128 * h:128 * h + 128], w_pool[:, c], start=g == 0, stop=g == 3)
            t.then_inc(s_pool_done, 1)
            pe.wait_ge(s_norm_rows, 6)
            transpose_rows(HN, 4)
            pe.wait_ge(s_norm_T, 6)
            rows_from_pairs(16, pre_chunk, 0, HT)

            pe.wait_ge(s_norm_rows, 8)
            transpose_rows(HN, 4)
            pe.wait_ge(s_norm_T, 8)
            for n in range(4):
                w = pre_chunk(20 + n)
                for i in range(2):
                    t = project_T(banks(0, 4, S), w[:, i, :], HT[:, 2 * n + i, :], n + i == 0, n + i == 4)
                t.then_inc(s_ring_used, 1)
            pe.wait_ge(s_memq_evac, 2)
            for h in range(4):
                for th in range(TH):
                    for d in range(2):
                        t = mm(PS[:, 4 + h, 256 * th:256 * th + 256], mqT[:, 2 * h + d, 128 * th:128 * th + 128],
                               mkT[:, 2 * h + d, :], start=th + d == 0, stop=th + d == 2)
            t.then_inc(s_score_done, 1)
            pe.wait_ge(s_p_ready, 1)
            for h in range(4):
                for m in range(2):
                    for th in range(TH):
                        t = transpose(banks(0, 4, S)[:, 2 * h + m, 128 * th:128 * th + 128],
                                      prob[:, 2 * h + th, 128 * m:128 * m + 128], ident)
            t.then_inc(s_tr_p, 1)
            pe.wait_ge(s_pT_evac, 2)
            for j in range(KT):
                for m in range(2):
                    t = mm(banks(4, 4, S)[:, j, :], mv_rows[:, m, 128 * j:128 * j + 128], probT[:, 2 * (j // 2) + m, :],
                           start=j % 2 == 0 and m == 0, stop=j % 2 == 1 and m == 1)
            t.then_inc(s_o_done, 1)
            pe.wait_ge(s_oT_evac, 2)
            rows_from_pairs(24, pre_chunk, 0, oT)

            pe.wait_ge(s_norm_rows, 10)
            transpose_rows(HN, 4)
            pe.wait_ge(s_norm_T, 10)
            for h in range(TH):
                c = slice(N_EXP * h, N_EXP * h + N_EXP)
                mm(PS[:, 0, c], ones[0:1, :], b_router[0:1, :], start=h == 0, stop=False)
                for k in range(KT):
                    t = mm(PS[:, 0, c], HT[:, k, 128 * h:128 * h + 128], w_router[:, k, :], start=False,
                           stop=h == 1 and k == KT - 1)
            t.then_inc(s_logits_done, 1)
            pe.wait_ge(s_late_loaded, 16)
            pe.wait_ge(s_rbias_ready, 16)
            mm(PS[0:HEADS, 3, :], rbias[0:33, :], C("bias_sel")[0:33, :], start=True, stop=True).then_inc(s_frow_done, 1)
            pe.wait_ge(s_mask_ready, 1)
            mm(PS[:, 1, 0:32], C("tri_lt"), mask[:, 0, :], start=True, stop=False)
            mm(PS[:, 1, 32:64], ones, mask[:, 0, :], start=False, stop=False)
            mm(PS[:, 1, 32:64], C("tri_lt"), mask[:, 1, :], start=False, stop=False)
            mm(PS[:, 1, 64:96], ones, mask[:, 0, :], start=False, stop=False)
            mm(PS[:, 1, 64:96], ones, mask[:, 1, :], start=False, stop=True).then_inc(s_rank_done, 1)
            pe.wait_ge(s_gates_ready, 1)
            for h in range(TH):
                t = transpose(PS[0:N_EXP, 2, 128 * h:128 * h + 128], gate[:, h, 0:N_EXP], ident)
            t.then_inc(s_gT_done, 1)
            pe.wait_ge(s_gT_evac, 1)
            pe.wait_ge(s_b2_loaded, 16)
            for h in range(TH):
                for c in range(2):
                    mm(PS[:, 4 + 2 * h + c, :], gT[0:N_EXP, 128 * h:128 * h + 128],
                       b2_all[0:N_EXP, 512 * c:512 * c + 512], start=True, stop=True)

            def gather():
                for k in range(KT):
                    for h in range(TH):
                        t = mm(banks(0, 1, CAP)[:, k, :], HN[:, h, 128 * k:128 * k + 128], pick[:, h, :],
                               start=k + h == 0, stop=k + h == KT)
                return t

            def up_bias():
                for c in range(2):
                    for b in range(2):
                        mm(PS[CAP * c:CAP * c + CAP, 2 + b, :], ones[32 * b:32 * b + 1, 0:CAP],
                           b1_rows[32 * b:32 * b + 1, 512 * c:512 * c + 512], start=True, stop=False)

            def up(k):
                w = slot(moe_slot(k))
                for b in range(2):
                    for c in range(2):
                        t = mm(PS[CAP * c:CAP * c + CAP, 2 + b, :], xT_e[:, k, :],
                               w[:, D * b + 512 * c:D * b + 512 * c + 512], start=False, stop=k == KT - 1)
                return t

            def turn_gpick():
                for h in range(TH):
                    t = transpose(PS[:, 1, 128 * h:128 * h + 128], gpick[:, h, :], ident)
                return t

            def turn_act():
                for b in range(4):
                    t = transpose(PS[:, 1, 128 * b:128 * b + 128], act_e[:, 128 * b:128 * b + 128], ident)
                return t

            def down(n):
                w = tk(slot(moe_slot(8 + n)), D)
                for i in range(2):
                    k = 2 * n + i
                    for c in range(2):
                        t = mm(PS[CAP * c:CAP * c + CAP, 0, :], actT[:, k % 4, k // 4, :],
                               w[:, i, 512 * c:512 * c + 512], start=k == 0, stop=k == KT - 1)
                return t

            def scatter():
                for h in range(TH):
                    for c in range(2):
                        t = mm(PS[:, 4 + 2 * h + c, :], gpT[CAP * c:CAP * c + CAP, 128 * h:128 * h + 128],
                               y_e[CAP * c:CAP * c + CAP, :], start=False, stop=True, skip_group_check=True)
                return t

            pe.wait_ge(s_pe_ready, 1)
            gather().then_inc(s_gathered, 1)
            pe.wait_ge(s_frow_evac, 1)
            with pe.Fori(0, N_EXP) as e:
                pe.wait_ge(s_xT_ready, e + 1)
                pe.wait_ge(s_gu_free, e + 1)
                pe.wait_ge(s_b1_loaded, (e + 1) * 16)
                up_bias()
                for k in range(KT):
                    pe.wait_ge(s_slot_loaded[moe_slot(k)], (e + ((NPRE + k) // SLOTS + 1)) * 16)
                    up(k).then_inc(s_ring_used, 1)
                pe.wait_ge(s_gp_ready, e + 1)
                turn_gpick().then_inc(s_gpt_done, 1)
                pe.wait_ge(s_pe_ready, e + 2)
                gather().then_inc(s_gathered, 1)
                pe.wait_ge(s_act_ready, e + 1)
                pe.wait_ge(s_gpt_evac, e + 1)
                turn_act().then_inc(s_actT_done, 1)
                pe.wait_ge(s_actT_evac, e + 1)
                pe.wait_ge(s_xT_ready, e + 2)
                for n in range(4):
                    pe.wait_ge(s_slot_loaded[moe_slot(8 + n)], (e + ((NPRE + 8 + n) // SLOTS + 1)) * 16)
                    down(n).then_inc(s_ring_used, 1)
                pe.wait_ge(s_y_evac, e + 1)
                scatter().then_inc(s_scattered, 1)

            pe.wait_ge(s_flag_ready, 1)
            over = pe.value_load(flag[0:1, 0:1], min_val=0, max_val=1)
            with pe.If(over > 0):
                NB = N_BLK - 1
                pe.wait_ge(s_gu_free, N_EXP + 1)
                with pe.Fori(0, N_EXP) as e:
                    pe.wait_ge(s_ov_loaded, (e + 1) * (16 * (PER + 1)))
                    for b in range(NB):
                        pe.wait_ge(s_pe_ready, e * NB + (N_EXP + 1 + b + 1))
                        gather().then_inc(s_gathered, 1)
                        turn_gpick().then_inc(s_gpt_done, 1)
                        pe.wait_ge(s_xT_ready, e * NB + (N_EXP + 1 + b + 1))
                        up_bias()
                        for k in range(KT):
                            t = up(k)
                        t.then_inc(s_ov_up, 1)
                        pe.wait_ge(s_gpt_evac, e * NB + (N_EXP + b + 1))
                        pe.wait_ge(s_act_ready, e * NB + (N_EXP + b + 1))
                        turn_act().then_inc(s_actT_done, 1)
                        pe.wait_ge(s_actT_evac, e * NB + (N_EXP + b + 1))
                        for n in range(4):
                            t = down(n)
                        t.then_inc(s_ov_down, 1)
                        pe.wait_ge(s_y_evac, e * NB + (N_EXP + b + 1))
                        scatter().then_inc(s_ov_sc, 1)
            pe.wait_ge(s_norm_rows, 14)
            transpose_rows(HN, 0)
            pe.wait_ge(s_norm_T, 12)
            n = 0
            w = post_chunk(n)
            for k in range(KT):
                t = mm(PS[:, 4, 0:256], w[:, k, :], HT[:, k, :], start=k == 0, stop=k == KT - 1)
            t.then_inc(s_ring_used, 1)
            n += 1
            pe.wait_ge(s_lora_evac, 1)
            for k in range(KT):
                w = post_chunk(n + k)[:, 0, :]
                project_T(banks(0, 8, S), w, HT[:, k, :], k == 0, k == KT - 1).then_inc(s_ring_used, 1)
            pe.wait_ge(s_rw_evac, 2)
            pe.wait_ge(s_tanh_ready, 1)
            for j in range(4):
                mm(banks(0, 2, S)[:, j, :], lora_w[0:64, 128 * j:128 * j + 128], lora_t[0:64, :],
                   start=j % 2 == 0, stop=j % 2 == 1)
            for j in range(4):
                t = mm(banks(2, 2, S)[:, j, :], lora_w[64:128, 128 * j:128 * j + 128], lora[64:128, :],
                       start=j % 2 == 0, stop=j % 2 == 1)
            t.then_inc(s_wl_done, 1)

            def cols_from_pairs(n0, lo, hi, bank):
                for n in range(lo, hi):
                    w = post_chunk(n0 + n)
                    for i in range(2):
                        t = project_T(banks(bank, 4, S), w[:, i, :], HT[:, 2 * n + i, :], n + i == 0, n + i == 4)
                    t.then_inc(s_ring_used, 1)

            cols_from_pairs(USED_RW, 0, 4, 4)
            pe.wait_ge(s_wl_sig, 8)
            pe.wait_ge(s_kk_sq, 1)
            for b in range(2):
                t = mm(PS[:, b, :], C("head_ones"), kk_sq[:, 512 * b:512 * b + 512], start=True, stop=True)
            t.then_inc(s_kk_sum, 1)
            pe.wait_ge(s_bon_in, 1)
            for b in range(2):
                t = mm(PS[:, 2 + b, :], C("head_ones"), bon_in[:, 512 * b:512 * b + 512], start=True, stop=True)
            t.then_inc(s_bon_sum, 1)
            def moba_scores(g):
                for i in range(4):
                    h = 4 * g + i
                    j, r = h // 2, HD * (h % 2)
                    q, k = qk2[r:r + HD, j, :], qk2[r:r + HD, 4 + j, :]
                    mm(PS[:, i, 0:128], q[:, 0:128], k[:, 0:128], start=True, stop=False)
                    t = mm(PS[:, i, 128:384], q[:, 128:256], k, start=False, stop=True)
                t.then_inc(s_moba_s, 1)

            pe.wait_ge(s_a_evac, 2)
            for n in range(4):
                w = post_chunk(USED_QK + n)
                for i in range(2):
                    k, first, last = 2 * n + i, n + i == 0, n + i == 4
                    project_rows(4, HT, k, w[:, i, 0:512], first, last, n=1)
                    t = project_T(banks(6, 2, S), w[:, i, 512:], HT[:, k, :], first, last)
                t.then_inc(s_ring_used, 1)
                if n == 1:
                    pe.wait_ge(s_kk_sqrt, 1)
                    pe.wait_ge(s_bon_ready, 1)
                    moba_scores(0)
            pe.wait_ge(s_moba_read, 1)
            moba_scores(1)

            def moba_turn(g):
                for i in range(4):
                    for b in range(3):
                        t = transpose(PS[:, 4 + i, 128 * b:128 * b + 128],
                                      prob2[:, 4 * g + i, 128 * b:128 * b + 128], ident)
                    if g:
                        t = transpose(PS[:, 4 + i, 384:512], p_rows[:, i % 2, 128 * (i // 2):128 * (i // 2) + 128], ident)
                t.then_inc(s_moba_tr, 1)

            def cols_part(n0, lo, hi, xT, tiles):
                for i in range(lo, hi):
                    k, j = i // 8, i % 8
                    w = post_chunk(n0 + k // 2)
                    t = mm(banks(0, 4, S)[:, j, :], w[:, k % 2, 128 * j:128 * j + 128], xT[:, k, :],
                           start=k == 0 and j % 2 == 0, stop=k == tiles - 1 and j % 2 == 1)
                    if i % 16 == 15:
                        t.then_inc(s_ring_used, 1)

            def gate_a_part(lo, hi):
                cols_part(USED_VZ, lo, hi, HT, KT)

            def gate_b_part(lo, hi):
                cols_part(USED_GA, lo, hi, HT, KT)

            def pa_part(lo, hi):
                cols_part(USED_GB, lo, hi, ya, 4)

            pe.wait_ge(s_moba_read, 2)
            gate_a_part(0, 16)
            pe.wait_ge(s_a_evac, 4)
            pe.wait_ge(s_moba_p, 1)
            moba_turn(0)
            gate_a_part(16, 32)
            pe.wait_ge(s_moba_pT, 2)
            pe.wait_ge(s_moba_p, 2)
            pe.wait_ge(s_p_loaded, 16)
            moba_turn(1)
            gate_a_part(32, 40)

            def pair_product(out, sets, lhs, rhs):
                for i, n in enumerate(sets):
                    for r in (0, HD):
                        t = mm(out[r:r + HD, i], lhs(n, r), rhs(n, r), start=True, stop=True)
                return t

            def of(x):
                if len(x.shape) == 3:
                    return lambda n, r: x[r:r + HD, :, L * n:L * n + L]
                v = tk(x, L)
                return lambda n, r: v[r:r + HD, n, :]

            def eye_block(n, r):
                return ident[r:r + HD, r:r + HD]

            def half_sets(hf):
                return range(NSET // 2 * hf, NSET // 2 * hf + NSET // 2)

            def wide(bank):
                return PS[:, bank:bank + 2, :].rearrange("p b (n a t) -> p (b n) a t", a=2, t=L)

            pe.wait_ge(s_moba_pT, 4)
            for h in range(HEADS):
                j, r, c = h // 2, HD * (h % 2), slice(HD * h, HD * h + HD)
                mm(banks(4, 2, S)[r:r + HD, j, :], v2[:, 0, c], prob2T[:, h, 0:256], start=j % 2 == 0, stop=False)
                t = mm(banks(4, 2, S)[r:r + HD, j, 128:256], v2[:, 1, c], prob2T[:, h, 256:384], start=False,
                       stop=j % 2 == 1)
            t.then_inc(s_moba_o, 1)
            pe.wait_ge(s_wkv_T, 1)
            pair_product(banks(6, 2, L), range(NSET), of(rw_v), eye_block).then_inc(s_rows_done, 1)
            gate_a_part(40, 44)
            pe.wait_ge(s_ya_ready, 1)
            pair_product(banks(4, 2, L), range(NSET), of(bT), eye_block).then_inc(s_rows_done, 1)
            gate_a_part(44, 48)
            pe.wait_ge(s_rows_evac, 1)
            pair_product(banks(6, 2, L), range(NSET), of(kTl), eye_block).then_inc(s_rows_done, 1)
            gate_a_part(48, 52)
            pe.wait_ge(s_rows_evac, 2)
            for hf in range(2):
                pair_product(banks(4 + hf, 1, L), half_sets(hf), of(aT), of(bT)).then_inc(s_mat_done, 1)
            gate_a_part(52, 56)
            pe.wait_ge(s_rows_evac, 3)
            pair_product(wide(6), half_sets(0), of(bT), of(a_r)).then_inc(s_mat_done, 1)
            gate_a_part(56, 60)
            pe.wait_ge(s_mat_evac, 2)
            pair_product(wide(4), half_sets(1), of(bT), of(a_r)).then_inc(s_mat_done, 1)
            gate_a_part(60, 64)
            pe.wait_ge(s_mat_evac, 5)
            pair_product(wide(6), half_sets(0), of(kTl), of(a_r)).then_inc(s_mat_done, 1)
            pe.wait_ge(s_gate_evac, 1)
            gate_b_part(0, 4)
            pe.wait_ge(s_mat_evac, 8)
            pair_product(wide(4), half_sets(1), of(kTl), of(a_r)).then_inc(s_mat_done, 1)
            gate_b_part(4, 8)
            pe.wait_ge(s_eye_set, 1)
            for i, (x, y, res) in enumerate(SOLVE):
                for hf in range(2):
                    if i == 0:
                        pe.wait_ge(s_sol_ready, 1 + hf)
                    else:
                        pe.wait_ge(s_sol_evac, 2 * (i - 1) + hf + 1)
                    ps = wide(6 - 2 * hf) if len(res) == 2 else banks(6 - 2 * hf, 1, L)
                    pair_product(ps, half_sets(hf), of(x), of(y)).then_inc(s_sol_done, 1)
                    n = 2 * i + hf
                    gate_b_part(8 + 56 * n // 24, 8 + 56 * (n + 1) // 24)
            pe.wait_ge(s_sol_evac, 2 * len(SOLVE))

            oY = banks(6, 2, S)
            for c in range(NCH):
                def pairs(g):
                    return [(j, j * NCH + c, r) for j in (2 * g, 2 * g + 1) for r in (0, HD)]

                def part(g, which, j, r):
                    return PS[r:r + HD, 4 + g, 128 * which + L * (j % 2):128 * which + L * (j % 2) + L]

                for g in range(2):
                    if c:
                        pe.wait_ge(s_rec_state, 2 * (c - 1) + g + 1)
                    for j, n, r in pairs(g):
                        t = mm(part(g, 0, j, r), of(akT)(n, r), of(v_tok)(n, r), start=j == 2 * g, stop=c == 0 and j == 2 * g + 1)
                    if c:
                        for j, n, r in pairs(g):
                            t = mm(part(g, 0, j, r), of(aT)(n, r), state[c % 2][r:r + HD, j, :], start=False, stop=j == 2 * g + 1)
                    t.then_inc(s_rec_x, 1)
                if c == 0:
                    pe.wait_ge(s_gate_evac, 2)
                pa_part(8 * c, 8 * c + 4)
                for g in range(2):
                    pe.wait_ge(s_rec_xe, 2 * c + g + 1)
                    for j, n, r in pairs(g):
                        t = mm(part(g, 1, j, r), of(invT)(n, r), rec_rhs[r:r + HD, j, :], start=j == 2 * g, stop=j == 2 * g + 1)
                    t.then_inc(s_rec_sa, 1)
                pa_part(8 * c + 4, 8 * c + 8)
                for g in range(2):
                    pe.wait_ge(s_rec_sae, 2 * c + g + 1)
                    if c < NCH - 1:
                        for j, n, r in pairs(g):
                            mm(part(g, 2, j, r), of(b_tok)(n, r), rec_sa[r:r + HD, j, :], start=j == 2 * g, stop=False)
                        for j, n, r in pairs(g):
                            t = mm(part(g, 2, j, r), of(k_tok)(n, r), of(v_tok)(n, r), start=False, stop=j == 2 * g + 1)
                        t.then_inc(s_rec_s, 1)
                for g in range(2):
                    for j, n, r in pairs(g):
                        o = oY[r:r + HD, j, L * c:L * c + L]
                        mm(o, rec_sa[r:r + HD, j, :], of(rbT)(n, r), start=c == 0 and j % 2 == 0, stop=False)
                    if c:
                        for j, n, r in pairs(g):
                            mm(oY[r:r + HD, j, L * c:L * c + L], state[c % 2][r:r + HD, j, :], of(r_dec)(n, r), start=False, stop=False)
                    for j, n, r in pairs(g):
                        t = mm(oY[r:r + HD, j, L * c:L * c + L], of(v_tok)(n, r), of(rkT)(n, r), start=False,
                               stop=c == NCH - 1 and j % 2 == 1)
                t.then_inc(s_y_psum, 1)
            pe.wait_ge(s_yT_evac, 1)
            for b in range(2):
                t = mm(PS[:, 4 + b, :], C("head_ones"), yT[:, 512 * b:512 * b + 512], start=True, stop=True)
            t.then_inc(s_gn_mean, 1)
            pe.wait_ge(s_pa_used, 1)
            w = post_chunk(USED_PA)
            project_rows(0, pT, 0, w[:, 0, :], True, False)
            pe.wait_ge(s_gn_sq, 1)
            for b in range(2):
                t = mm(PS[:, 6 + b, :], C("head_ones"), ysq[:, 512 * b:512 * b + 512], start=True, stop=True)
            t.then_inc(s_gn_var, 1)
            project_rows(0, pT, 1, w[:, 1, :], False, True).then_inc(s_ring_used, 1)
            pe.wait_ge(s_yb_ready, 1)
            pe.wait_ge(s_e_evac, 1)
            cols_part(USED_UP, 0, 32, yb, 4)
            pe.wait_ge(s_merged_ready, 1)
            rows_from_pairs(USED_PB, post_chunk, 4, merged)
            pe.wait_ge(s_h2_ready, 2)
            transpose_rows(X, 0)
            pe.wait_ge(s_norm_T, 14)
            rows_from_pairs(USED_OUT, post_chunk, 4, HT)

        @block.scalar
        def _(act):
            fn = nc.scalar.activation

            def stats(n, halves, width, eps_col):
                for h, (rows, scratch) in enumerate(halves):
                    fn(scratch, rows, ACT.Square, accum_out=stat[:, 2 * n + h:2 * n + h + 1]).then_inc(s_norm_sq, 1)
                act.wait_ge(s_norm_sq, 2 * n + 2)
                fn(stat[:, 16 + 2 * n:18 + 2 * n], stat[:, 2 * n:2 * n + 2], ACT.Sqrt, scale=1.0 / width,
                   bias=eps[:, eps_col:eps_col + 1]).then_inc(s_norm_std, 1)

            def scale_half(n, dst, src):
                act.wait_ge(s_norm_rstd, n + 1)
                fn(dst, src, ACT.Copy, scale=stat[:, 32 + 2 * n + 1:32 + 2 * n + 2]).then_inc(s_norm_rows, 1)

            def evac_T(m, bank, dst, gain):
                act.wait_ge(s_norm_tr, 2 * m)
                for k in range(4, KT):
                    t = fn(dst[:, k, :], banks(bank, 4, S)[:, k, :], ACT.Copy, scale=P(gain, k) if gain else 1.0)
                t.then_inc(s_norm_T, 1)

            act.dma_start(cst[:, 0:LATE], a["consts"][:, 0:LATE]).then_inc(s_const_loaded, 16)
            act.dma_start(par_rows[:, :], a["params"]).then_inc(s_param_loaded, 16)
            act.dma_start(cst[:, LATE:], a["consts"][:, LATE:]).then_inc(s_late_loaded, 16)
            act.dma_start(w_pool[:, :].rearrange("p (g e) -> p g e", g=4), a["w_pool"][0].rearrange("g c e -> c g e"))\
               .then_inc(s_small_loaded, 16)
            act.dma_start(scale_bc[:, :], a["pool_scale"][0].partition_broadcast(128)).then_inc(s_small_loaded, 16)
            act.dma_start(w_router[:, :, :], a["w_router"][0].rearrange("(k p) e -> p k e", p=128)).then_inc(s_small_loaded, 16)
            act.dma_start(b_router[:, :], a["b_router"]).then_inc(s_small_loaded, 16)
            act.dma_start(lora_w[0:64, :], a["w_up_2"][0]).then_inc(s_small_loaded, 16)
            act.dma_start(lora_w[64:128, :], a["a_up_2"][0]).then_inc(s_small_loaded, 16)

            act.wait_ge(s_eps_set, 1)
            act.wait_ge(s_mem_loaded, 32)
            stats(0, [(mem_rows[:, h, :], HN[:, h, :]) for h in range(TH)], D, 0)
            scale_half(0, mem_rows[:, 1, :], mem_rows[:, 1, :])
            act.wait_ge(s_x_loaded, 32)
            stats(1, [(X[:, h, :], HN[:, h, :]) for h in range(TH)], D, 0)
            scale_half(1, HN[:, 1, :], X[:, 1, :])
            act.wait_ge(s_params_cols, 1)
            evac_T(1, 0, memT, "g_mem_kv")
            evac_T(2, 4, HT, "g_mix")
            act.wait_ge(s_ring_used, 8)
            fn(mkT, banks(0, 4, S), ACT.Copy).then_inc(s_kv_evac, 1)
            act.wait_ge(s_ring_used, 16)
            fn(qkT[:, 0:4, :], banks(0, 2, S), ACT.Copy, scale=HD ** -0.5).then_inc(s_win_evac, 1)
            fn(qkT[:, 4:8, :], banks(2, 2, S), ACT.Copy).then_inc(s_win_evac, 1)
            act.wait_ge(s_z_copied, 1)
            fn(SP, Z, ACT.Abs).then_inc(s_z_abs, 1)
            act.wait_ge(s_z_abs, 1)
            fn(SP, SP, ACT.Exp, scale=-1.0).then_inc(s_z_abs, 1)
            act.wait_ge(s_z_abs, 2)
            fn(SP, SP, ACT.Ln, bias=1.0).then_inc(s_z_ln, 1)
            act.wait_ge(s_arg_ready, 1)
            fn(SP, Z, ACT.Exp).then_inc(s_w_ready, 1)
            act.wait_ge(s_sb_done, 1)
            for h in range(TH):
                fn(buf(7, 512 * h, 512 * h + 512), PS[:, h, :], ACT.Square, accum_out=stat[:, 48 + h:49 + h]).then_inc(s_mix_sq, 1)
            act.wait_ge(s_pool_scaled, 2)
            for h in range(TH):
                fn(buf(7, 1024 + 512 * h, 1536 + 512 * h), HN[:, h, 512:], ACT.Square,
                   accum_out=stat[:, 50 + h:51 + h]).then_inc(s_mix_sq, 1)
            act.wait_ge(s_mix_sq, 4)
            fn(stat[:, 52:56], stat[:, 48:52], ACT.Sqrt, scale=1.0 / 512, bias=eps[:, 0:1]).then_inc(s_mix_std, 1)
            act.wait_ge(s_mix_rstd, 1)
            for h in range(TH):
                t = fn(HN[:, h, 0:512], PS[:, h, :], ACT.Copy, scale=stat[:, 56 + h:57 + h])
            t.then_inc(s_norm_rows, 1)
            evac_T(3, 4, HT, "g_sb_out")
            for h in range(TH):
                act.wait_ge(s_x_new, h + 1)
                if h == 0:
                    act.wait_ge(s_norm_tr, 6)
                fn(HN[:, h, :], X[:, h, :], ACT.Square, accum_out=stat[:, 6 + h:7 + h]).then_inc(s_norm_sq, 1)
            act.wait_ge(s_norm_sq, 6)
            fn(stat[:, 22:24], stat[:, 6:8], ACT.Sqrt, scale=1.0 / D, bias=eps[:, 0:1]).then_inc(s_norm_std, 1)
            act.wait_ge(s_norm_rstd, 3)
            fn(HN[:, 1, :], X[:, 1, :], ACT.Copy, scale=stat[:, 39:40]).then_inc(s_norm_rows, 1)
            evac_T(4, 4, HT, "g_mem_q")
            act.wait_ge(s_ring_used, 24)
            fn(mqT[:, 0:4, :], banks(0, 2, S), ACT.Copy, scale=256 ** -0.5).then_inc(s_memq_evac, 1)
            act.wait_ge(s_score_max, 1)
            for i in range(8):
                fn(prob[:, i, :], banks(4, 4, S)[:, i, :], ACT.Exp, bias=mstat[:, 8 + i:9 + i],
                   accum_out=mstat[:, 16 + i:17 + i]).then_inc(s_p_exp, 1)
            act.wait_ge(s_tr_p, 1)
            fn(probT[:, 0:4, :], banks(0, 2, S), ACT.Copy).then_inc(s_pT_evac, 1)
            act.wait_ge(s_o_done, 1)
            fn(oT[:, 0:4, :], banks(4, 2, S), ACT.Copy).then_inc(s_oT_evac, 1)
            for h in range(TH):
                act.wait_ge(s_x_new, 2 + h + 1)
                if h == 0:
                    act.wait_ge(s_norm_tr, 8)
                fn(HN[:, h, :], X[:, h, :], ACT.Square, accum_out=stat[:, 8 + h:9 + h]).then_inc(s_norm_sq, 1)
            act.dma_start(b2_all[0:N_EXP, :], a["b_expert_out"][0]).then_inc(s_b2_loaded, 16)
            act.dma_start(g_final, a["g_final"].partition_broadcast(128)).then_inc(s_g_loaded, 16)
            act.dma_start(g_post, a["g_post_2"][0].partition_broadcast(128)).then_inc(s_g_loaded, 16)
            act.wait_ge(s_norm_sq, 8)
            fn(stat[:, 24:26], stat[:, 8:10], ACT.Sqrt, scale=1.0 / D, bias=eps[:, 0:1]).then_inc(s_norm_std, 1)
            act.wait_ge(s_norm_rstd, 4)
            fn(HN[:, 1, :], X[:, 1, :], ACT.Copy, scale=stat[:, 41:42]).then_inc(s_norm_rows, 1)
            evac_T(5, 4, HT, "g_ffn")
            act.wait_ge(s_top_ready, 1)
            for h in range(TH):
                t = fn(lg[:, h, :], lg[:, h, :], ACT.Exp, bias=stat[:, 60 + h:61 + h])
            t.then_inc(s_top_exp, 1)
            act.wait_ge(s_frow_done, 1)
            fn(frow[0:HEADS, :], PS[0:HEADS, 3, :], ACT.Copy).then_inc(s_frow_evac, 1)
            act.wait_ge(s_frow_evac, 1)
            act.dma_start(bias_dram[:, :, 0:512], frow[0:HEADS, :].unsqueeze(1).to_broadcast([HEADS, 128, 512])).then_inc(s_bias_written, 16)
            act.wait_ge(s_bias_written, 16)
            for b in range(2):
                src = bias_view(255 - 128 * b)
                act.dma_start(bias[:, :, b, :], src).then_inc(s_bias_read, 16)

            def silu_gate():
                return fn(sig, g7, ACT.Sigmoid, scale=1.702)

            def copy_gpT():
                return fn(gpT, PS[:, 1, 0:256], ACT.Copy)

            def copy_actT():
                return fn(actT, PS[:, 1, :].rearrange("p (b h c) -> p b h c", b=4, h=2), ACT.Copy)

            def copy_y():
                return fn(y_e, PS[:, 0, :], ACT.Copy)

            with act.Fori(0, N_EXP) as e:
                act.wait_ge(s_sig_in, e + 1)
                silu_gate().then_inc(s_sig_out, 1)
                act.wait_ge(s_gpt_done, e + 1)
                copy_gpT().then_inc(s_gpt_evac, 1)
                act.wait_ge(s_actT_done, e + 1)
                copy_actT().then_inc(s_actT_evac, 1)
                act.wait_ge(s_ring_used, e * PER + (NPRE + PER))
                copy_y().then_inc(s_y_evac, 1)
            act.wait_ge(s_flag_ready, 1)
            over = act.value_load(flag[0:1, 0:1], min_val=0, max_val=1)
            with act.If(over > 0):
                NB = N_BLK - 1
                with act.Fori(0, N_EXP * NB) as n:
                    act.wait_ge(s_gpt_done, n + (N_EXP + 1))
                    copy_gpT().then_inc(s_gpt_evac, 1)
                    act.wait_ge(s_sig_in, n + (N_EXP + 1))
                    silu_gate().then_inc(s_sig_out, 1)
                    act.wait_ge(s_actT_done, n + (N_EXP + 1))
                    copy_actT().then_inc(s_actT_evac, 1)
                    act.wait_ge(s_ov_down, n + 1)
                    copy_y().then_inc(s_y_evac, 1)

            for n in (5, 6):
                for h in range(TH):
                    if n == 5:
                        act.wait_ge(s_x_new, 4 + h + 1)
                    else:
                        act.wait_ge(s_norm_rows, 11 + h)
                    fn(HN[:, h, :], X[:, h, :], ACT.Square, accum_out=stat[:, 2 * n + h - 0:2 * n + h + 1])\
                        .then_inc(s_norm_sq, 1)
                act.wait_ge(s_norm_sq, 2 * n)
                fn(stat[:, 16 + 2 * n:18 + 2 * n], stat[:, 2 * n:2 * n + 2], ACT.Sqrt, scale=1.0 / D,
                   bias=eps[:, n - 5:n - 4]).then_inc(s_norm_std, 1)
            act.wait_ge(s_norm_rstd, 6)
            fn(HN[:, 1, :], X[:, 1, :], ACT.Copy, scale=stat[:, 45:46]).then_inc(s_norm_rows, 1)
            act.dma_start(p_rows, a["p_2"][0, 0].rearrange("(h p) n -> p h n", p=128)).then_inc(s_p_loaded, 16)
            evac_T(6, 0, HT, "g_pre_2")
            act.wait_ge(s_lora_mix, 1)
            fn(lora_t[0:64, :], lora[0:64, :], ACT.Tanh).then_inc(s_tanh_ready, 1)
            act.wait_ge(s_ring_used, MOE_END + 9)
            fn(rwT[:, 0:8, :], banks(0, 4, S), ACT.Copy).then_inc(s_rw_evac, 1)
            act.wait_ge(s_wl_done, 1)
            for j in range(4):
                fn(tk(sg, S)[:, j, :], banks(0, 2, S)[:, j, :], ACT.Sigmoid, bias=P("w0_2", j)).then_inc(s_wl_sig, 1)
            for j in range(4):
                fn(tk(rate, S)[:, j, :], banks(2, 2, S)[:, j, :], ACT.Sigmoid, bias=P("a0_2", j)).then_inc(s_wl_sig, 1)
            act.wait_ge(s_wkv_cum, 1)
            fn(dec, cum, ACT.Exp, scale=-DECAY).then_inc(s_wkv_exp, 1)
            fn(dec_inv, cum, ACT.Exp, scale=DECAY).then_inc(s_wkv_exp, 1)
            fn(dec_prev, sg, ACT.Exp, scale=-DECAY).then_inc(s_wkv_exp, 1)
            act.wait_ge(s_ring_used, MOE_END + USED_QK)
            act.wait_ge(s_rw_mix, 1)
            fn(qk2[:, 0:4, :], banks(4, 2, S), ACT.Copy, scale=HD ** -0.5).then_inc(s_a_evac, 1)
            act.wait_ge(s_kk_sum, 1)
            fn(kk_inv, PS[:, 0:2, :].rearrange("p b n -> p (b n)"), ACT.Sqrt).then_inc(s_kk_sqrt, 1)
            act.wait_ge(s_ring_used, MOE_END + USED_VZ)
            fn(z_sig, PS[:, 6:8, :].rearrange("p b n -> p (b n)"), ACT.Sigmoid).then_inc(s_za_sig, 1)

            def moba_exp(g):
                act.wait_ge(s_moba_max, g + 1)
                for h in range(4 * g, 4 * g + 4):
                    for i, c in enumerate((slice(0, 128), slice(128, 384))):
                        fn(prob2[:, h, c], prob2[:, h, c], ACT.Exp, bias=mstat[:, 16 + 8 * i + h:17 + 8 * i + h],
                           accum_out=mstat[:, 32 + 8 * i + h:33 + 8 * i + h]).then_inc(s_moba_exp, 1)

            def moba_evac(g):
                act.wait_ge(s_moba_tr, g + 1)
                t = fn(prob2T[:, 4 * g:4 * g + 2, :], PS[:, 4:6, 0:384], ACT.Copy)
                if g:
                    t = fn(pT[:, 0, :].rearrange("p (h t) -> p h t", h=2), PS[:, 4:6, 384:512], ACT.Copy)
                t.then_inc(s_moba_pT, 1)

            moba_exp(0)
            moba_exp(1)
            moba_evac(0)
            moba_evac(1)
            act.wait_ge(s_a_evac, 4)
            fn(z_sig, buf(4, 1024), ACT.Sigmoid).then_inc(s_zb_sig, 1)
            act.wait_ge(s_ring_used, MOE_END + USED_GA)
            fn(gate_a, banks(0, 4, S), ACT.Sigmoid).then_inc(s_gate_evac, 1)
            act.wait_ge(s_ring_used, MOE_END + USED_GB)
            fn(gate_b, banks(0, 4, S), ACT.Sigmoid).then_inc(s_gate_evac, 1)
            act.wait_ge(s_gn_var, 1)
            fn(ystd, PS[:, 6:8, :].rearrange("p b n -> p (b n)"), ACT.Sqrt, scale=1.0 / HD, bias=eps[:, 2:3])\
                .then_inc(s_gn_std, 1)
            act.wait_ge(s_ring_used, MOE_END + USED_UP)
            fn(e_rows, PS[:, 0:4, :].rearrange("p (h b) n -> p h (b n)", h=TH), ACT.Copy).then_inc(s_e_evac, 1)
            act.wait_ge(s_ring_used, MOE_END + USED_OUT)
            for h in range(TH):
                fn(HN[:, h, :], PS[:, 4 + 2 * h:6 + 2 * h, :].rearrange("p b n -> p (b n)"), ACT.Square,
                   accum_out=stat[:, 14 + h:15 + h]).then_inc(s_norm_sq, 1)
            act.wait_ge(s_norm_sq, 14)
            fn(stat[:, 30:32], stat[:, 14:16], ACT.Sqrt, scale=1.0 / D, bias=eps[:, 1:2]).then_inc(s_norm_std, 1)
            evac_T(7, 0, HT, None)
            act.wait_ge(s_ring_used, MOE_END + USED_PG)
            for h in range(TH):
                fn(pg_sig[:, h, :], PS[:, 4 + 2 * h:6 + 2 * h, :].rearrange("p b n -> p (b n)"), ACT.Sigmoid)\
                    .then_inc(s_pg_sig, 1)

        @block.gpsimd
        def _(pool):
            done = [0]

            def step(ins):
                done[0] += 1
                ins.then_inc(s_pool_chain, 1)
                pool.wait_ge(s_pool_chain, done[0])

            nc.gpsimd.memset(eps[:, 0:1], 1e-5)
            nc.gpsimd.memset(eps[:, 1:2], 1e-6)
            nc.gpsimd.memset(eps[:, 2:3], 64e-5).then_inc(s_eps_set, 1)
            nc.gpsimd.memset(eps[:, 3:4], 0.0).then_inc(s_gu_free, 1)
            nc.gpsimd.memset(gate[:, :, N_EXP:], 0.0).then_inc(s_ov_sc, 1)
            nc.gpsimd.memset(slot_of[:, :, N_EXP:], -1.0)
            step(nc.gpsimd.memset(rbias[:, :], 1.0))
            pool.dma_start(rbias[0:32, :], a["rel_bias_2"]).then_inc(s_rbias_ready, 16)
            pool.wait_ge(s_win_evac, 4)
            pool.wait_ge(s_late_loaded, 16)
            for g in range(4):
                src = u_T[:, g, :]
                for n in range(g + 1):
                    w, dst = 1 << n, win[n % 2]
                    nc.gpsimd.tensor_copy(dst[:, 0:w], src[:, 0:w])
                    step(nc.gpsimd.tensor_tensor(dst[:, w:], src[:, w:], src[:, 0:S - w], ALU.add))
                    src = dst
                step(nc.gpsimd.tensor_tensor(win[2], src, C("inv_count")[:, S * g:S * g + S], ALU.mult))
                nc.gpsimd.tensor_tensor(pooled[:, g, :], win[2], u_T[:, g, :], ALU.subtract).then_inc(s_pooled_ready, 1)
                pool.wait_ge(s_pooled_ready, g + 1)
            pool.wait_ge(s_mat_done, 6)
            nc.gpsimd.tensor_copy(tk(eye, L), C("eye64").unsqueeze(1).to_broadcast([128, NSET, L])).then_inc(s_eye_set, 1)

        @block.vector
        def _(dve):
            v = nc.vector
            done = [0]

            def step(ins):
                done[0] += 1
                ins.then_inc(s_dve_chain, 1)
                dve.wait_ge(s_dve_chain, done[0])

            def rstd(n):
                dve.wait_ge(s_norm_std, n + 1)
                v.reciprocal(stat[:, 32 + 2 * n:34 + 2 * n], stat[:, 16 + 2 * n:18 + 2 * n]).then_inc(s_norm_rstd, 1)
                dve.wait_ge(s_norm_rstd, n + 1)

            def scale_half(n, dst, src):
                v.tensor_scalar(dst, src, stat[:, 32 + 2 * n:33 + 2 * n], None, ALU.mult).then_inc(s_norm_rows, 1)

            def evac_T(m, bank, dst, gain):
                dve.wait_ge(s_norm_tr, 2 * m - 1)
                if gain:
                    t = v.tensor_tensor(dst[:, 0:4, :], banks(bank, 2, S), Pn(gain, 4, S), ALU.mult)
                else:
                    t = v.tensor_copy(dst[:, 0:4, :], banks(bank, 2, S))
                t.then_inc(s_norm_T, 1)

            def rows_half(bank, h):
                return PS[:, bank + 2 * h:bank + 2 * h + 2, :].rearrange("p b n -> p (b n)")

            def add_residual(bank):
                for h in range(TH):
                    v.tensor_tensor(X[:, h, :], rows_half(bank, h), X[:, h, :], ALU.add).then_inc(s_x_new, 1)

            rstd(0)
            scale_half(0, mem_rows[:, 0, :], mem_rows[:, 0, :])
            dve.wait_ge(s_params_T, 1)
            v.tensor_copy(par[:, :], PS[:, 7, 0:128]).then_inc(s_params_cols, 1)
            rstd(1)
            scale_half(1, HN[:, 0, :], X[:, 0, :])
            dve.wait_ge(s_params_cols, 1)
            evac_T(1, 0, memT, "g_mem_kv")
            evac_T(2, 4, HT, "g_mix")
            dve.wait_ge(s_ring_used, 8)
            v.tensor_copy(tk(buf(9), 512), PS[:, 4:8, :]).then_inc(s_kv_evac, 1)
            dve.wait_ge(s_ring_used, 16)
            v.tensor_copy(v_rows, PS[:, 4:6, :]).then_inc(s_win_evac, 1)
            v.tensor_copy(u_T, banks(6, 2, S)).then_inc(s_win_evac, 1)
            causal = C("causal").unsqueeze(1).to_broadcast([128, HEADS, 128])
            neg = C("neg_diag").unsqueeze(1).to_broadcast([128, HEADS, 128])
            diag = (slice(0, 128), slice(256, 384))
            dve.wait_ge(s_z_done, 1)
            v.tensor_copy(Z, PS[:, :, 0:384]).then_inc(s_z_copied, 1)
            dve.wait_ge(s_z_copied, 1)
            dve.wait_ge(s_z_ln, 1)
            step(v.scalar_tensor_tensor(SP, Z, 0.0, SP, ALU.max, ALU.add))
            for c in diag:
                t = v.tensor_tensor(SP[:, :, c], SP[:, :, c], causal, ALU.mult)
            t.then_inc(s_sp_ready, 1)
            for c in diag:
                t = v.tensor_tensor(Z[:, :, c], Z[:, :, c], neg, ALU.add)
            step(t)
            dve.wait_ge(s_rev_done, 1)
            v.tensor_tensor(Z, Z, PS[:, :, 0:384], ALU.subtract).then_inc(s_arg_ready, 1)
            dve.wait_ge(s_pool_done, 1)
            dve.wait_ge(s_small_loaded, 16 * 6)
            for h in range(TH):
                v.tensor_tensor(HN[:, h, 512:], PS[:, 2 + h, :], scale_bc[:, :], ALU.mult).then_inc(s_pool_scaled, 1)
            dve.wait_ge(s_mix_std, 1)
            v.reciprocal(stat[:, 56:60], stat[:, 52:56]).then_inc(s_mix_rstd, 1)
            dve.wait_ge(s_mix_rstd, 1)
            for h in range(TH):
                t = v.tensor_scalar(HN[:, h, 512:], HN[:, h, 512:], stat[:, 58 + h:59 + h], None, ALU.mult)
            t.then_inc(s_norm_rows, 1)
            evac_T(3, 4, HT, "g_sb_out")
            dve.wait_ge(s_ring_used, 20)
            add_residual(0)
            dve.wait_ge(s_norm_std, 3)
            v.reciprocal(stat[:, 38:40], stat[:, 22:24]).then_inc(s_norm_rstd, 1)
            dve.wait_ge(s_norm_rstd, 3)
            v.tensor_scalar(HN[:, 0, :], X[:, 0, :], stat[:, 38:39], None, ALU.mult).then_inc(s_norm_rows, 1)
            evac_T(4, 4, HT, "g_mem_q")
            dve.wait_ge(s_ring_used, 24)
            v.tensor_scalar(mqT[:, 4:8, :], banks(2, 2, S), 256 ** -0.5, None, ALU.mult).then_inc(s_memq_evac, 1)
            dve.wait_ge(s_score_done, 1)
            step(v.reduce_max(mstat[:, 0:8], banks(4, 4, S), AX))
            v.tensor_scalar(mstat[:, 8:16], mstat[:, 0:8], -1.0, None, ALU.mult).then_inc(s_score_max, 1)
            dve.wait_ge(s_p_exp, 8)
            step(v.reciprocal(mstat[:, 24:32], mstat[:, 16:24]))
            v.tensor_tensor(prob, prob, mstat[:, 24:32].unsqueeze(2).to_broadcast([128, 8, S]), ALU.mult)\
                .then_inc(s_p_ready, 1)
            dve.wait_ge(s_tr_p, 1)
            v.tensor_copy(probT[:, 4:8, :], banks(2, 2, S)).then_inc(s_pT_evac, 1)
            dve.wait_ge(s_o_done, 1)
            v.tensor_copy(oT[:, 4:8, :], banks(6, 2, S)).then_inc(s_oT_evac, 1)
            dve.wait_ge(s_ring_used, 28)
            add_residual(0)
            dve.wait_ge(s_norm_std, 4)
            v.reciprocal(stat[:, 40:42], stat[:, 24:26]).then_inc(s_norm_rstd, 1)
            dve.wait_ge(s_norm_rstd, 4)
            v.tensor_scalar(HN[:, 0, :], X[:, 0, :], stat[:, 40:41], None, ALU.mult).then_inc(s_norm_rows, 1)
            evac_T(5, 4, HT, "g_ffn")
            dve.wait_ge(s_logits_done, 1)
            step(v.tensor_copy(lg[:, :, :], PS[:, 0, 0:64].rearrange("p (h e) -> p h e", h=TH)))
            for h in range(TH):
                t = v.max(top8[:, h, :], lg[:, h, :])
            step(t)
            for h in range(TH):
                v.tensor_scalar(stat[:, 60 + h:61 + h], top8[:, h, 0:1], -1.0, None, ALU.mult)
                t = v.max_index(idx8[:, h, :], top8[:, h, :], lg[:, h, :])
            t.then_inc(s_top_ready, 1)
            dve.wait_ge(s_top_ready, 1)
            step(v.tensor_copy(idxf[:, :, :], idx8[:, :, :]))
            for h in range(TH):
                t = v.tensor_tensor(hot[:, h, :, :], C("iota32").unsqueeze(1).to_broadcast([128, 4, N_EXP]),
                                    idxf[:, h, 0:4].unsqueeze(2).to_broadcast([128, 4, N_EXP]), ALU.is_equal)
            step(t)
            v.tensor_reduce(mask[:, :, :], hot[:, :, :, :].rearrange("p h k e -> p h e k"), AX, ALU.add)\
                .then_inc(s_mask_ready, 1)
            dve.wait_ge(s_top_exp, 1)
            dve.wait_ge(s_mask_ready, 1)
            step(v.tensor_tensor(lg[:, :, :], lg[:, :, :], mask[:, :, :], ALU.mult))
            step(v.tensor_reduce(stat[:, 62:64], lg[:, :, :], AX, ALU.add))
            step(v.reciprocal(stat[:, 64:66], stat[:, 62:64]))
            v.tensor_tensor(gate[:, :, 0:N_EXP], lg[:, :, :], stat[:, 64:66].unsqueeze(2).to_broadcast([128, TH, N_EXP]),
                            ALU.mult).then_inc(s_gates_ready, 1)
            dve.wait_ge(s_rank_done, 1)
            step(v.scalar_tensor_tensor(slot_of[:, :, 0:N_EXP], PS[:, 1, 0:64].rearrange("p (h e) -> p h e", h=TH), 1.0,
                                        mask[:, :, :], ALU.add, ALU.mult))
            step(v.tensor_scalar(slot_of[:, :, 0:N_EXP], slot_of[:, :, 0:N_EXP], -1.0, None, ALU.add))
            dve.wait_ge(s_ov_sc, 1)

            def set_pick(col):
                for h in range(TH):
                    t = v.tensor_scalar(pick[:, h, :], C("iota")[:, 0:CAP], col(h), None, ALU.is_equal)
                return t

            def set_gpick(col, e):
                for h in range(TH):
                    t = v.tensor_scalar(gpick[:, h, :], C("iota"), col(h), gate[:, h, bass.ds(e, 1)], ALU.is_equal,
                                        ALU.mult)
                return t

            def copy_xT():
                return v.tensor_tensor(xT_e, banks(0, 1, CAP), Pn("g_ffn", KT, CAP), ALU.mult)

            def clip_gate():
                return v.tensor_scalar(g7, PS[:, 2, :], 7.0, None, ALU.min)

            def clip_up():
                return v.tensor_scalar(u7, PS[:, 3, :], 7.0, -7.0, ALU.min, ALU.max)

            def up_gate():
                return v.scalar_tensor_tensor(gu, u7, 1.0, g7, ALU.add, ALU.mult)

            def activate():
                return v.tensor_tensor(act_e, gu, sig, ALU.mult)

            set_pick(lambda h: slot_of[:, h, 0:1]).then_inc(s_pe_ready, 1)
            step(v.reduce_max(stat[0:1, 66:67], PS[0:1, 1, 64:96], AX))
            v.tensor_scalar(flag[0:1, 0:1], stat[0:1, 66:67], float(CAP), None, ALU.is_gt).then_inc(s_flag_ready, 1)
            dve.wait_ge(s_gates_ready, 1)
            for h in range(TH):
                t = v.tensor_scalar(gpick[:, h, :], C("iota"), slot_of[:, h, 0:1], gate[:, h, 0:1], ALU.is_equal, ALU.mult)
            t.then_inc(s_gp_ready, 1)
            dve.wait_ge(s_gT_done, 1)
            v.tensor_copy(gT[0:N_EXP, :], PS[0:N_EXP, 2, 0:256]).then_inc(s_gT_evac, 1)
            dve.wait_ge(s_gathered, 1)
            copy_xT().then_inc(s_xT_ready, 1)

            with dve.Fori(0, N_EXP) as e:
                dve.wait_ge(s_gathered, e + 1)
                set_pick(lambda h: slot_of[:, h, bass.ds(e + 1, 1)]).then_inc(s_pe_ready, 1)
                dve.wait_ge(s_ring_used, e * PER + (NPRE + 8))
                clip_gate().then_inc(s_sig_in, 1)
                clip_up().then_inc(s_gu_free, 1)
                dve.wait_ge(s_gu_free, e + 2)
                up_gate().then_inc(s_gu_made, 1)
                dve.wait_ge(s_gu_made, e + 1)
                dve.wait_ge(s_sig_out, e + 1)
                activate().then_inc(s_act_ready, 1)
                dve.wait_ge(s_gathered, e + 2)
                copy_xT().then_inc(s_xT_ready, 1)
                dve.wait_ge(s_gpt_done, e + 1)
                set_gpick(lambda h: slot_of[:, h, bass.ds(e + 1, 1)], e + 1).then_inc(s_gp_ready, 1)
            dve.wait_ge(s_scattered, N_EXP)
            dve.wait_ge(s_flag_ready, 1)
            over = v.value_load(flag[0:1, 0:1], min_val=0, max_val=1)
            with v.If(over > 0):
                NB = N_BLK - 1
                with dve.Fori(0, N_EXP) as e:
                    for b in range(NB):
                        dve.wait_ge(s_ov_sc, e * NB + (b + 1))
                        for h in range(TH):
                            t = v.tensor_scalar(ov_slot[:, h:h + 1], slot_of[:, h, bass.ds(e, 1)], -float(CAP * (b + 1)), None,
                                                ALU.add)
                        t.then_inc(s_ov_base, 1)
                        dve.wait_ge(s_ov_base, e * NB + (b + 1))
                        set_pick(lambda h: ov_slot[:, h:h + 1])
                        set_gpick(lambda h: ov_slot[:, h:h + 1], e).then_inc(s_pe_ready, 1)
                        dve.wait_ge(s_gathered, e * NB + (N_EXP + 1 + b + 1))
                        copy_xT().then_inc(s_xT_ready, 1)
                        dve.wait_ge(s_ov_up, e * NB + (b + 1))
                        clip_gate().then_inc(s_sig_in, 1)
                        clip_up().then_inc(s_gu_free, 1)
                        dve.wait_ge(s_gu_free, e * NB + (N_EXP + 1 + b + 1))
                        up_gate().then_inc(s_gu_made, 1)
                        dve.wait_ge(s_gu_made, e * NB + (N_EXP + b + 1))
                        dve.wait_ge(s_sig_out, e * NB + (N_EXP + b + 1))
                        activate().then_inc(s_act_ready, 1)
                dve.wait_ge(s_ov_sc, N_EXP * NB + 1)
            add_residual(4)

            dve.wait_ge(s_norm_std, 5)
            v.reciprocal(stat[:, 42:44], stat[:, 26:28]).then_inc(s_norm_rstd, 1)
            dve.wait_ge(s_norm_rstd, 5)
            dve.wait_ge(s_g_loaded, 32)
            for h in range(TH):
                v.scalar_tensor_tensor(X[:, h, :], X[:, h, :], stat[:, 42 + h:43 + h], g_final, ALU.mult, ALU.mult)\
                    .then_inc(s_norm_rows, 1)
            dve.wait_ge(s_norm_std, 6)
            v.reciprocal(stat[:, 44:46], stat[:, 28:30]).then_inc(s_norm_rstd, 1)
            dve.wait_ge(s_norm_rstd, 6)
            v.tensor_scalar(HN[:, 0, :], X[:, 0, :], stat[:, 44:45], None, ALU.mult).then_inc(s_norm_rows, 1)
            evac_T(6, 0, HT, "g_pre_2")
            dve.wait_ge(s_ring_used, MOE_END + 1)
            v.tensor_copy(lora, PS[:, 4, 0:256]).then_inc(s_lora_evac, 1)
            dve.wait_ge(s_lora_evac, 1)
            v.tensor_tensor(lora_d[:, 1:], lora[:, 0:S - 1], lora[:, 1:], ALU.subtract)
            step(v.tensor_scalar(lora_d[:, 0:1], lora[:, 0:1], -1.0, None, ALU.mult))
            v.scalar_tensor_tensor(lora, lora_d, P("mu_shift_2", 16), lora, ALU.mult, ALU.add).then_inc(s_lora_mix, 1)
            dve.wait_ge(s_ring_used, MOE_END + 9)
            v.tensor_copy(rwT[:, 8:16, :], banks(4, 4, S)).then_inc(s_rw_evac, 1)
            dve.wait_ge(s_rw_evac, 2)
            v.tensor_tensor(diff[:, :, 1:], rwT[:, :, 0:S - 1], rwT[:, :, 1:], ALU.subtract)
            step(v.tensor_scalar(diff[:, :, 0:1], rwT[:, :, 0:1], -1.0, None, ALU.mult))
            for j in range(16):
                t = v.scalar_tensor_tensor(rwT[:, j, :], diff[:, j, :], P("mu_shift_2", j), rwT[:, j, :], ALU.mult, ALU.add)
            t.then_inc(s_rw_mix, 1)
            dve.wait_ge(s_rw_mix, 1)
            rr, kr, vr, zr = (tk(x, S) for x in (rT, rw_k, rw_v, rw_z))
            step(v.tensor_tensor(tk(kk, S), kr, Pn("k_k_2", 4, S), ALU.mult))
            v.tensor_tensor(kk_sq, kk, kk, ALU.mult).then_inc(s_kk_sq, 1)
            dve.wait_ge(s_wl_sig, 8)
            step(v.tensor_tensor_scan(cum, C("chunk_reset"), sg, 0.0, ALU.mult, ALU.add))
            v.tensor_tensor(sg, cum, sg, ALU.subtract).then_inc(s_wkv_cum, 1)
            step(v.scalar_tensor_tensor(tk(k2, S), tk(rate, S), 1.0, Pn("k_a_2", 4, S), ALU.subtract, ALU.mult))
            step(v.scalar_tensor_tensor(k2, k2, 1.0, rw_k, ALU.add, ALU.mult))
            step(v.tensor_tensor(tk(bon_in, S), rr, Pn("r_k_2", 4, S), ALU.mult))
            v.tensor_tensor(bon_in, bon_in, k2, ALU.mult).then_inc(s_bon_in, 1)
            dve.wait_ge(s_ring_used, MOE_END + USED_QK)
            v.tensor_copy(qk2[:, 4:8, :], banks(6, 2, S)).then_inc(s_a_evac, 1)
            dve.wait_ge(s_kk_sqrt, 1)
            step(v.tensor_scalar(kk_inv, kk_inv, 1e-12, None, ALU.max))
            step(v.reciprocal(kk_inv, kk_inv))
            step(v.tensor_tensor(kk, kk, kk_inv, ALU.mult))
            step(v.tensor_tensor(rate, rate, kk, ALU.mult))
            dve.wait_ge(s_wkv_exp, 3)
            dve.wait_ge(s_bon_sum, 1)
            v.tensor_tensor(bonus, PS[:, 2:4, :].rearrange("p b n -> p (b n)"), rw_v, ALU.mult).then_inc(s_bon_ready, 1)
            v.tensor_copy(dec_end[:, :], tk(dec, L)[:, :, L - 1])
            v.tensor_tensor(r_dec, rT, dec, ALU.mult)
            v.scalar_tensor_tensor(aT, kk, -1.0, dec_prev, ALU.mult, ALU.mult)
            step(v.tensor_tensor(bT, rate, dec_inv, ALU.mult))
            v.tensor_tensor(kTl, k2, dec_inv, ALU.mult).then_inc(s_wkv_T, 1)
            dve.wait_ge(s_bias_read, 32)

            def moba_bias(g):
                hs = slice(4 * g, 4 * g + 4)
                dve.wait_ge(s_moba_s, g + 1)
                for c, b in ((0, 0), (1, 1), (2, 0)):
                    t = v.tensor_tensor(prob2[:, hs, 128 * c:128 * c + 128], PS[:, 0:4, 128 * c:128 * c + 128],
                                        bias[:, hs, b, :], ALU.add)
                t.then_inc(s_moba_read, 1)
                dve.wait_ge(s_moba_read, g + 1)
                v.reduce_max(mstat[:, 4 * g:4 * g + 4], prob2[:, hs, 0:128], AX)
                step(v.reduce_max(mstat[:, 8 + 4 * g:12 + 4 * g], prob2[:, hs, 128:384], AX))
                v.tensor_scalar(halves_of(16, g), halves_of(0, g), -1.0, None, ALU.mult).then_inc(s_moba_max, 1)

            def halves_of(lo, g):
                return mstat[:, lo:lo + 16].rearrange("p (i h) -> p i h", i=2)[:, :, 4 * g:4 * g + 4]

            def moba_probs(g):
                hs = slice(4 * g, 4 * g + 4)
                dve.wait_ge(s_moba_exp, 8 * (g + 1))
                step(v.reciprocal(halves_of(48, g), halves_of(32, g)))
                v.tensor_tensor(prob2[:, hs, 0:128], prob2[:, hs, 0:128],
                                mstat[:, 48 + 4 * g:52 + 4 * g].unsqueeze(2).to_broadcast([128, 4, 128]), ALU.mult)
                v.tensor_tensor(prob2[:, hs, 128:384], prob2[:, hs, 128:384],
                                mstat[:, 56 + 4 * g:60 + 4 * g].unsqueeze(2).to_broadcast([128, 4, 256]), ALU.mult)\
                    .then_inc(s_moba_p, 1)

            def moba_evac(g):
                dve.wait_ge(s_moba_tr, g + 1)
                t = v.tensor_copy(prob2T[:, 4 * g + 2:4 * g + 4, :], PS[:, 6:8, 0:384])
                if g:
                    t = v.tensor_copy(pT[:, 1, :].rearrange("p (h t) -> p h t", h=2), PS[:, 6:8, 384:512])
                t.then_inc(s_moba_pT, 1)

            moba_bias(0)
            moba_bias(1)
            dve.wait_ge(s_ring_used, MOE_END + USED_VZ)
            v.tensor_copy(v2, PS[:, 4:6, :]).then_inc(s_a_evac, 1)
            dve.wait_ge(s_za_sig, 1)
            v.tensor_tensor(za, banks(6, 2, S), tk(z_sig, S), ALU.mult).then_inc(s_a_evac, 1)
            moba_probs(0)
            moba_probs(1)
            moba_evac(0)
            moba_evac(1)

            def flat(bank):
                return PS[:, bank:bank + 2, :].rearrange("p b n -> p (b n)")

            def half(x, hf):
                return tk(x, L)[:, NSET // 2 * hf:NSET // 2 * hf + NSET // 2, :]

            def masked(name):
                return C(name).unsqueeze(1).to_broadcast([128, NSET // 2, L])

            def wide(bank):
                return PS[:, bank:bank + 2, :].rearrange("p b (n a t) -> p a (b n) t", a=2, t=L)

            dve.wait_ge(s_moba_o, 1)
            v.tensor_tensor(ya, banks(4, 2, S), za, ALU.mult).then_inc(s_ya_ready, 1)
            for i, (dst, bank) in enumerate(((v_tok, 6), (b_tok, 4), (k_tok, 6))):
                dve.wait_ge(s_rows_done, i + 1)
                v.tensor_copy(dst, flat(bank)).then_inc(s_rows_evac, 1)
            for hf in range(2):
                dve.wait_ge(s_mat_done, hf + 1)
                v.tensor_tensor(half(a0, hf), banks(4 + hf, 1, L), masked("low_diag"), ALU.mult).then_inc(s_mat_evac, 1)
            dve.wait_ge(s_mat_evac, 2)
            for hf in range(2):
                v.tensor_tensor(half(F, hf), half(a0, hf), masked("eye64"), ALU.add)
                dve.wait_ge(s_mat_done, 2 + hf + 1)
                ps = wide(6 - 2 * hf)
                v.tensor_tensor(half(b0, hf), ps[:, 0], masked("up_diag"), ALU.mult).then_inc(s_mat_evac, 1)
                v.tensor_tensor(half(offT, hf), ps[:, 0], masked("up_off"), ALU.mult).then_inc(s_mat_evac, 1)
                v.tensor_tensor(half(rbT, hf), ps[:, 1], masked("up_incl"), ALU.mult).then_inc(s_mat_evac, 1)
            for hf in range(2):
                dve.wait_ge(s_mat_done, 4 + hf + 1)
                ps = wide(6 - 2 * hf)
                v.tensor_tensor(half(akT, hf), ps[:, 0], masked("up_strict"), ALU.mult)
                v.tensor_tensor(half(rkT, hf), ps[:, 1], masked("up_incl"), ALU.mult).then_inc(s_sol_ready, 1)
            for i, (x, y, res) in enumerate(SOLVE):
                for hf in range(2):
                    dve.wait_ge(s_sol_done, 2 * i + hf + 1)
                    bank = 6 - 2 * hf
                    for q, (dst, plus) in enumerate(res):
                        ps = wide(bank)[:, q] if len(res) == 2 else banks(bank, 1, L)
                        if plus is None:
                            t = v.tensor_copy(half(dst, hf), ps)
                        else:
                            t = v.tensor_tensor(half(dst, hf), ps, half(plus, hf), ALU.add)
                    t.then_inc(s_sol_evac, 1)
            for c in range(NCH):
                for g in range(2):
                    dve.wait_ge(s_rec_x, 2 * c + g + 1)
                    v.tensor_copy(rec_rhs[:, 2 * g:2 * g + 2, :], tk(PS[:, 4 + g, 0:128], L)).then_inc(s_rec_xe, 1)
                for g in range(2):
                    dve.wait_ge(s_rec_sa, 2 * c + g + 1)
                    v.tensor_copy(rec_sa[:, 2 * g:2 * g + 2, :], tk(PS[:, 4 + g, 128:256], L)).then_inc(s_rec_sae, 1)
                for g in range(2):
                    if c < NCH - 1:
                        js = slice(2 * g, 2 * g + 2)
                        end = dec_end[:, :].rearrange("p (j c) -> p j c", c=NCH)[:, js, c].unsqueeze(2).to_broadcast([128, 2, HD])
                        new, old, ps = state[(c + 1) % 2][:, js, :], state[c % 2][:, js, :], tk(PS[:, 4 + g, 256:384], L)
                        dve.wait_ge(s_rec_s, 2 * c + g + 1)
                        if c:
                            step(v.tensor_tensor(new, ps, old, ALU.add))
                            v.tensor_tensor(new, new, end, ALU.mult).then_inc(s_rec_state, 1)
                        else:
                            v.tensor_tensor(new, ps, end, ALU.mult).then_inc(s_rec_state, 1)
            dve.wait_ge(s_y_psum, NCH)
            v.tensor_copy(yT, flat(6)).then_inc(s_yT_evac, 1)
            dve.wait_ge(s_gate_evac, 2)
            dve.wait_ge(s_ring_used, MOE_END + USED_PA)
            v.tensor_tensor(gate_a, gate_a, banks(0, 4, S), ALU.mult).then_inc(s_pa_used, 1)
            dve.wait_ge(s_yT_evac, 1)
            dve.wait_ge(s_gn_mean, 1)
            step(v.scalar_tensor_tensor(yT, flat(4), -1.0 / HD, yT, ALU.mult, ALU.add))
            v.tensor_tensor(ysq, yT, yT, ALU.mult).then_inc(s_gn_sq, 1)
            dve.wait_ge(s_zb_sig, 1)
            step(v.tensor_tensor(rw_z, rw_z, z_sig, ALU.mult))
            dve.wait_ge(s_gn_std, 1)
            step(v.reciprocal(ystd, ystd))
            step(v.tensor_tensor(yT, yT, ystd, ALU.mult))
            for j in range(4):
                t = v.tensor_scalar(tk(yT, S)[:, j, :], tk(yT, S)[:, j, :], P("ln_x_w_2", j), P("ln_x_b_2", j), ALU.mult, ALU.add)
            step(t)
            step(v.tensor_tensor(yT, yT, bonus, ALU.add))
            v.tensor_tensor(yT, yT, rw_z, ALU.mult).then_inc(s_yb_ready, 1)
            dve.wait_ge(s_ring_used, MOE_END + USED_PB)
            dve.wait_ge(s_pa_used, 1)
            step(v.tensor_tensor(gate_b, gate_b, banks(0, 4, S), ALU.mult))
            v.tensor_tensor(merged, gate_a, gate_b, ALU.add).then_inc(s_merged_ready, 1)
            dve.wait_ge(s_norm_std, 7)
            step(v.reciprocal(stat[:, 46:48], stat[:, 30:32]))
            for h in range(TH):
                step(v.scalar_tensor_tensor(HN[:, h, :], rows_half(4, h), stat[:, 46 + h:47 + h], g_post, ALU.mult, ALU.mult))
                v.tensor_tensor(X[:, h, :], X[:, h, :], HN[:, h, :], ALU.add).then_inc(s_h2_ready, 1)
            evac_T(7, 0, HT, None)
            for h in range(TH):
                dve.wait_ge(s_pg_sig, h + 1)
                dve.wait_ge(s_h2_ready, 2)
                dve.wait_ge(s_e_evac, 1)
                step(v.tensor_tensor(HN[:, h, :], pg_sig[:, h, :], e_rows[:, h, :], ALU.mult))
                v.tensor_tensor(HN[:, h, :], HN[:, h, :], X[:, h, :], ALU.add).then_inc(s_out_ready, 1)



_INS = ["x", "mem", "w_in", "w_pool", "pool_scale", "w_out", "w_mem_q", "w_mem_kv", "w_mem_o", "w_router", "b_router",
        "w_expert_in", "b_expert_in", "w_expert_out", "b_expert_out", "g_final", "p_2", "w_in_2", "rel_bias_2",
        "w_up_2", "a_up_2", "p_a_2", "p_b_2", "w_out_2", "g_post_2", "w_ple_up_2", "w_ple_gate_2"]


def kernel(**inputs):
    import numpy as _np
    import concourse.bacc as _bacc
    from concourse import mybir as _mybir
    from concourse.bass_utils import run_bass_kernel_spmd as _run

    nc = _bacc.Bacc("TRN2", target_bir_lowering=False, num_devices=1)
    given = {n: _np.ascontiguousarray(inputs[n]) for n in _INS}
    given["params"] = _np.concatenate([_np.asarray(inputs[n]).reshape(-1, 128) for n, _ in PARAMS]
                                      + [_np.zeros((128 - P_ROWS, 128), _np.float32)], axis=0)
    given["consts"] = constants()
    arrays, args = {}, {}
    for name, v in given.items():
        arrays[f"in_{name}_dram"] = v
        args[name] = nc.dram_tensor(f"in_{name}_dram", v.shape, _mybir.dt.from_np(v.dtype), kind="ExternalInput").ap()
    out = nc.dram_tensor("out_0_dram", (1, S, D), _mybir.dt.float32, kind="ExternalOutput").ap()
    two_blocks(nc, args, out)
    r = _run(nc, [arrays], core_ids=[0])
    return r.results[0]["out_0_dram"]
```

```python
import math
from contextlib import ExitStack

import numpy as np
import concourse.bass as bass
from concourse import mybir

D = 1024
S = 256
KT = D // 128
TH = S // 128
SLOTS = 12
SLOT = 2048
PRE_SLOTS = 4
N_EXP = 32
CAP = 64
N_BLK = S // CAP
NEG = -1.0e30
HEADS = 8
HD = 64
L = 64
NCH = S // L
NSET = 4 * NCH
DECAY = math.exp(-0.5)

PARAMS = [("g_mix", 8), ("g_sb_out", 4), ("g_pool_out", 4), ("g_mem_q", 8), ("g_mem_kv", 8), ("g_ffn", 8),
          ("g_pre_2", 8), ("mu_shift_2", 17), ("w0_2", 4), ("a0_2", 4), ("k_k_2", 4), ("k_a_2", 4),
          ("r_k_2", 4), ("ln_x_w_2", 4), ("ln_x_b_2", 4)]
P_AT, _at = {}, 0
for _n, _r in PARAMS:
    P_AT[_n] = _at
    _at += _r
P_ROWS = _at

CONSTS = [("ident", 128), ("tri_ge", 128), ("tri_lt", 128), ("ones", 128), ("head_ones", 128), ("iota", 128),
          ("causal", 128), ("neg_diag", 128), ("iota32", 32), ("up_strict", 64), ("up_incl", 64),
          ("up_diag", 64), ("up_off", 64), ("low_diag", 64), ("eye64", 64), ("bias_sel", 512), ("chunk_reset", 1024),
          ("inv_count", 1024)]
C_AT, _at = {}, 0
for _n, _r in CONSTS:
    C_AT[_n] = (_at, _at + _r)
    _at += _r
C_COLS = _at
LATE = C_AT["iota32"][0]


def constants():
    c = np.zeros((128, C_COLS), np.float32)

    def put(name, value):
        c[:value.shape[0], C_AT[name][0]:C_AT[name][1]] = value

    p = np.arange(128)
    put("ident", np.eye(128))
    put("tri_ge", p[:, None] >= p[None, :])
    put("tri_lt", p[:, None] < p[None, :])
    put("ones", np.ones((128, 128)))
    put("head_ones", p[:, None] // HD == p[None, :] // HD)
    put("iota", np.tile(p % CAP, (128, 1)))
    put("causal", p[:, None] < p[None, :])
    put("neg_diag", np.where(p[:, None] < p[None, :], 0.0, NEG))
    put("iota32", np.tile(np.arange(32), (128, 1)))
    r, q = p[:, None] % L, np.arange(L)[None, :]
    put("up_strict", r < q)
    put("up_incl", r <= q)
    near = r // 16 == q // 16
    put("up_diag", (r < q) & near)
    put("up_off", (r < q) & ~near)
    put("low_diag", (r > q) & near)
    put("eye64", r == q)
    dist = 255 - np.arange(512)
    n = np.maximum(dist, 0)
    large = 16 + (np.log(np.maximum(n, 1).astype(np.float32) / np.float32(16)) / np.float32(math.log(8.0))
                  * np.float32(16)).astype(np.int32)
    bucket = np.where(n < 16, n, np.minimum(large, 31))
    sel = np.zeros((33, 512))
    sel[:32] = (np.arange(32)[:, None] == bucket[None, :]) & (dist >= 0)[None, :]
    sel[32] = np.where(dist >= 0, 0.0, NEG)
    put("bias_sel", sel)
    cnt = np.stack([1.0 / np.minimum(np.arange(S) + 1, w) for w in (2, 4, 8, 16)])
    put("inv_count", np.tile(cnt.reshape(1, -1), (128, 1)))
    put("chunk_reset", np.tile((np.arange(1024) % L != 0)[None, :], (128, 1)))
    return c


def two_blocks(nc, a, out):
    f32, f32r, i32, u32 = mybir.dt.float32, mybir.dt.float32r, mybir.dt.int32, mybir.dt.uint32
    ALU, ACT = mybir.AluOpType, mybir.ActivationFunctionType
    AX = mybir.AxisListType.X
    ctx = ExitStack()
    with ctx:
        def sb(name, shape, dt=f32):
            return ctx.enter_context(nc.sbuf_tensor(name, shape, dt))

        ring = sb("ring", [128, SLOTS * SLOT])
        ring_at = nc.sbuf_base - 4 * SLOTS * SLOT
        big = sb("big", [128, 10 * 2048])
        cst = sb("cst", [128, C_COLS])
        cst_at = nc.sbuf_base - 4 * C_COLS
        w_pool = sb("w_pool_sb", [128, 512])
        scale_bc = sb("scale_bc", [128, 512])
        mu_keep = sb("mu_keep", [128, 16])
        par_rows = sb("par_rows", [128, 128])
        par = sb("par", [128, 128])
        w_router = sb("w_router_sb", [128, KT, N_EXP])
        b_router = sb("b_router_sb", [1, N_EXP])
        stat = sb("stat", [128, 96])
        eps = sb("eps", [128, 4])
        mstat = sb("mstat", [128, 64])
        dec_end = sb("dec_end", [128, NSET])
        lora_w = sb("lora_w", [128, 512])
        rbias = sb("rbias", [33, HEADS])
        lg = sb("lg", [128, TH, N_EXP])
        top8 = sb("top8", [128, TH, 8])
        idx8 = sb("idx8", [128, TH, 8], u32)
        idxf = sb("idxf", [128, TH, 8])
        hot = sb("hot", [128, TH, 4, N_EXP])
        mask = sb("mask", [128, TH, N_EXP])
        gate = sb("gate", [128, TH, N_EXP + 1])
        slot_of = sb("slot_of", [128, TH, N_EXP + 1])
        ov_slot = sb("ov_slot", [128, TH])
        flag = sb("flag", [1, 1], i32)

        def buf(n, lo=0, hi=2048):
            return big[:, 2048 * n + lo:2048 * n + hi]

        def slot(n, lo=0, hi=SLOT):
            return ring[:, SLOT * n + lo:SLOT * n + hi]

        def split_buf(name, n):
            return nc.alloc_sbuf_tensor_at(name, [128, SLOT], f32r, offset=ring_at + 4 * SLOT * n)

        memH, memL = split_buf("mem_high", 4), split_buf("mem_rest", 5)
        W_high = [split_buf(f"w_high{i}", 6 + 2 * i) for i in range(2)]
        W_rest = [split_buf(f"w_rest{i}", 7 + 2 * i) for i in range(2)]
        HTH, HTL = split_buf("hT_high", 10), split_buf("hT_rest", 11)
        W2_high, W2_rest = [[nc.alloc_sbuf_tensor_at(f"{n}{i}", [128, D], f32r, offset=ring_at + 4 * SLOT * sl + 4 * D * i)
                             for i in range(2)] for n, sl in (("w2_high", 6), ("w2_rest", 7))]
        uTH = split_buf("uT_high", 2)
        assert C_AT["inv_count"] == (C_COLS - 1024, C_COLS)
        uTL = nc.alloc_sbuf_tensor_at("uT_rest", [128, KT * S], f32r, offset=cst_at + 4 * C_AT["inv_count"][0])

        def C(name):
            return cst[:, C_AT[name][0]:C_AT[name][1]]

        def P(name, k=0):
            return par[:, P_AT[name] + k:P_AT[name] + k + 1]

        def Pn(name, n, inner):
            return par[:, P_AT[name]:P_AT[name] + n].unsqueeze(2).to_broadcast([128, n, inner])

        def tk(ap, t):
            return ap.rearrange("p (k t) -> p k t", t=t)

        ident, ones = C("ident"), C("ones")
        X, HN = tk(buf(0), D), tk(buf(1), D)
        HT = tk(buf(2), S)
        qkT = tk(buf(3), S)
        v_rows = tk(buf(4, 0, 1024), 512)
        u_T = tk(buf(4, 1024), S)
        pooled = tk(buf(2, 0, 1024), S)
        win = [buf(2, 1024 + 256 * n, 1280 + 256 * n) for n in range(3)]
        Z = tk(big[:, 5 * 2048:5 * 2048 + 3072], 384)
        SP = tk(big[:, 5 * 2048 + 3072:8 * 2048], 384)
        mem_rows = tk(buf(5), D)
        mkT, mv_rows = tk(buf(8), S), tk(buf(9), D)
        mqT = tk(buf(3), S)
        prob = tk(buf(5), S)
        probT = tk(buf(6), S)
        xT_e = tk(buf(3, 0, 512), CAP)
        actT = buf(3, 512, 1024).rearrange("p (b h c) -> p b h c", b=4, h=2)
        y_e, gpT = buf(3, 1024, 1536), buf(3, 1536, 1792)
        g7, u7 = buf(4, 0, 512), buf(4, 512, 1024)
        sig, gu = buf(4, 1024, 1536), buf(4, 1536, 2048)
        act_e = buf(5, 0, 512)
        pick = tk(buf(5, 512, 640), CAP)
        gpick = tk(buf(5, 640, 896), 128)
        b2_all, gT = buf(6, 0, 1024), buf(6, 1024, 1280)
        b1_rows = C("inv_count")
        frow = buf(6, 1280, 1792)
        g_final, g_post = buf(8, 0, 1024), buf(8, 1024, 2048)
        bias = buf(9).rearrange("p (h b s) -> p h b s", h=HEADS, b=2)
        arr = [slot(s, lo, lo + 1024) for s in (8, 9, 10, 11, 0, 1, 2, 3) for lo in (0, 1024)]
        rwT = tk(big[:, 3 * 2048:5 * 2048], S)
        qk2 = tk(buf(5), S)
        v2, za = tk(buf(6, 0, 1024), 512), tk(buf(6, 1024), S)
        lora, lora_d, lora_t = buf(7, 0, 256), buf(7, 256, 512), buf(7, 512, 768)
        z_sig = buf(7, 1024)
        p_rows, pT = tk(buf(8, 0, 512), 256), tk(buf(8, 512, 1024), S)
        gate_a, gate_b = tk(buf(1), S), tk(buf(2), S)
        prob2, prob2T = tk(ring[:, 0:3072], 384), tk(ring[:, 3072:6144], 384)
        ya = za
        rT, rw_k, rw_v, rw_z = buf(3, 0, 1024), buf(3, 1024), buf(4, 0, 1024), buf(4, 1024)
        sg, cum, dec, dec_inv, dec_prev, rate, kk, kk_sq = arr[:8]
        k2, kk_inv = arr[14:16]
        bon_in = buf(1, 0, 1024)
        bonus = cum
        aT, bT, kTl = dec_prev, rate, dec_inv
        r_dec = kk_sq
        v_tok, b_tok, k_tok, b0, a0, akT, rbT, rkT = arr[8:16]
        offT, F, eye = sg, dec, rate
        a2, b2, a4, b4, b8 = kk, rT, buf(5, 0, 1024), buf(5, 1024), rw_k
        m1, m1T, ET, m2, t7, invT = rT, buf(5, 1024), buf(5, 0, 1024), dec, kk, dec_inv

        def pair_of(x0, x1):
            return bass.AP(x0.tensor, x0.offset, [list(x0.ap[0]), [x1.offset - x0.offset, 2], [1, 1024]])

        a_r, F_a2, off_eye = pair_of(aT, r_dec), pair_of(F, a2), pair_of(offT, eye)
        SOLVE = [(b0, a0, [(a2, None)]), (a0, b0, [(b2, None)]), (b2, F_a2, [(F, F), (a4, None)]),
                 (a2, b2, [(b4, None)]), (b4, F, [(F, F)]), (a4, b4, [(b8, None)]), (b8, F, [(F, F)]),
                 (F, off_eye, [(m1, None), (ET, None)]), (offT, F, [(m1T, None)]),
                 (m1, m1T, [(m2, None)]), (m1T, ET, [(t7, ET)]), (m2, t7, [(invT, t7)])]
        rec_rhs, rec_sa = tk(buf(7, 0, 256), HD), tk(buf(7, 256, 512), HD)
        state = tk(buf(7, 512, 768), HD), tk(buf(7, 768, 1024), HD)
        yT, ysq, ystd = sg, dec, kk
        e_rows = tk(slot(0), D)
        yb = tk(yT, S)
        merged = tk(buf(5), S)
        pg_sig = tk(buf(5), D)

        PS = ctx.enter_context(nc.psum_tensor("PS", [128, 8, 512], f32))

        def banks(lo, n, t):
            return PS[:, lo:lo + n, :].rearrange("p b (k t) -> p (b k) t", t=t)

        def sem(name):
            return ctx.enter_context(nc.semaphore(name))

        s_x_loaded = sem("s_x_loaded")
        s_mem_loaded = sem("s_mem_loaded")
        s_ring_used = sem("s_ring_used")
        s_b1_loaded = sem("s_b1_loaded")
        s_flag_ready = sem("s_flag_ready")
        s_ov_sc = sem("s_ov_sc")
        s_ov_loaded = sem("s_ov_loaded")
        s_out_ready = sem("s_out_ready")
        s_out_written = sem("s_out_written")
        s_norm_tr = sem("s_norm_tr")
        s_const_loaded = sem("s_const_loaded")
        s_param_loaded = sem("s_param_loaded")
        s_params_T = sem("s_params_T")
        s_norm_rows = sem("s_norm_rows")
        s_params_cols = sem("s_params_cols")
        s_norm_T = sem("s_norm_T")
        s_qkv_evac = sem("s_qkv_evac")
        s_w_high = sem("s_w_high")
        s_w_rest = sem("s_w_rest")
        s_t_high = sem("s_t_high")
        s_t_rest = sem("s_t_rest")
        s_vu_evac = sem("s_vu_evac")
        s_z_done = sem("s_z_done")
        s_sp_ready = sem("s_sp_ready")
        s_rev_done = sem("s_rev_done")
        s_w_ready = sem("s_w_ready")
        s_sb_done = sem("s_sb_done")
        s_pooled_ready = sem("s_pooled_ready")
        s_small_loaded = sem("s_small_loaded")
        s_pool_done = sem("s_pool_done")
        s_memq_evac = sem("s_memq_evac")
        s_score_done = sem("s_score_done")
        s_p_ready = sem("s_p_ready")
        s_tr_p = sem("s_tr_p")
        s_pT_evac = sem("s_pT_evac")
        s_o_done = sem("s_o_done")
        s_logits_done = sem("s_logits_done")
        s_late_loaded = sem("s_late_loaded")
        s_rbias_ready = sem("s_rbias_ready")
        s_frow_done = sem("s_frow_done")
        s_mask_ready = sem("s_mask_ready")
        s_rank_done = sem("s_rank_done")
        s_gates_ready = sem("s_gates_ready")
        s_gT_done = sem("s_gT_done")
        s_gT_evac = sem("s_gT_evac")
        s_b2_loaded = sem("s_b2_loaded")
        s_pe_ready = sem("s_pe_ready")
        s_gathered = sem("s_gathered")
        s_frow_evac = sem("s_frow_evac")
        s_xT_ready = sem("s_xT_ready")
        s_gu_free = sem("s_gu_free")
        s_gp_ready = sem("s_gp_ready")
        s_gpt_done = sem("s_gpt_done")
        s_act_ready = sem("s_act_ready")
        s_gpt_evac = sem("s_gpt_evac")
        s_actT_done = sem("s_actT_done")
        s_actT_evac = sem("s_actT_evac")
        s_y_evac = sem("s_y_evac")
        s_scattered = sem("s_scattered")
        s_ov_up = sem("s_ov_up")
        s_ov_down = sem("s_ov_down")
        s_lora_evac = sem("s_lora_evac")
        s_rw_kept = sem("s_rw_kept")
        s_k2_ready = sem("s_k2_ready")
        s_a_evac = sem("s_a_evac")
        s_tanh_ready = sem("s_tanh_ready")
        s_wl_done = sem("s_wl_done")
        s_kk_sq = sem("s_kk_sq")
        s_bon_in = sem("s_bon_in")
        s_head_sums = sem("s_head_sums")
        s_wl_sig = sem("s_wl_sig")
        s_bon_ready = sem("s_bon_ready")
        s_gate_evac = sem("s_gate_evac")
        s_moba_s = sem("s_moba_s")
        s_moba_p = sem("s_moba_p")
        s_moba_read = sem("s_moba_read")
        s_eye_set = sem("s_eye_set")
        s_pa_used = sem("s_pa_used")
        s_e_evac = sem("s_e_evac")
        s_moba_tr = sem("s_moba_tr")
        s_moba_pT = sem("s_moba_pT")
        s_moba_o = sem("s_moba_o")
        s_wkv_T = sem("s_wkv_T")
        s_ya_ready = sem("s_ya_ready")
        s_rows_evac = sem("s_rows_evac")
        s_mat_evac = sem("s_mat_evac")
        s_pairs_done = sem("s_pairs_done")
        s_sol_ready = sem("s_sol_ready")
        s_sol_evac = sem("s_sol_evac")
        s_sol_done = sem("s_sol_done")
        s_rec_state = sem("s_rec_state")
        s_rec_x = sem("s_rec_x")
        s_rec_xe = sem("s_rec_xe")
        s_rec_sa = sem("s_rec_sa")
        s_rec_sae = sem("s_rec_sae")
        s_rec_s = sem("s_rec_s")
        s_y_psum = sem("s_y_psum")
        s_yT_evac = sem("s_yT_evac")
        s_gn_sums = sem("s_gn_sums")
        s_gn_sq = sem("s_gn_sq")
        s_yb_ready = sem("s_yb_ready")
        s_merged_ready = sem("s_merged_ready")
        s_p_loaded = sem("s_p_loaded")
        s_ple_pT = sem("s_ple_pT")
        s_ple_pTe = sem("s_ple_pTe")
        s_h2_ready = sem("s_h2_ready")
        s_norm_sq = sem("s_norm_sq")
        s_norm_std = sem("s_norm_std")
        s_norm_rstd = sem("s_norm_rstd")
        s_eps_set = sem("s_eps_set")
        s_z_copied = sem("s_z_copied")
        s_z_abs = sem("s_z_abs")
        s_z_ln = sem("s_z_ln")
        s_arg_ready = sem("s_arg_ready")
        s_mix_sq = sem("s_mix_sq")
        s_pool_scaled = sem("s_pool_scaled")
        s_mix_std = sem("s_mix_std")
        s_mix_rstd = sem("s_mix_rstd")
        s_x_new = sem("s_x_new")
        s_score_max = sem("s_score_max")
        s_p_exp = sem("s_p_exp")
        s_g_loaded = sem("s_g_loaded")
        s_top_ready = sem("s_top_ready")
        s_top_exp = sem("s_top_exp")
        s_bias_written = sem("s_bias_written")
        s_bias_read = sem("s_bias_read")
        s_sig_in = sem("s_sig_in")
        s_sig_out = sem("s_sig_out")
        s_lora_mix = sem("s_lora_mix")
        s_rw_mix = sem("s_rw_mix")
        s_za_sig = sem("s_za_sig")
        s_kk_sqrt = sem("s_kk_sqrt")
        s_kk_max = sem("s_kk_max")
        s_wkv_cum = sem("s_wkv_cum")
        s_wkv_exp = sem("s_wkv_exp")
        s_moba_max = sem("s_moba_max")
        s_moba_exp = sem("s_moba_exp")
        s_zb_sig = sem("s_zb_sig")
        s_gn_std = sem("s_gn_std")
        s_pg_sig = sem("s_pg_sig")
        s_part_done = sem("s_part_done")
        P_B_DONE = 1
        s_pool_chain = sem("s_pool_chain")
        s_dve_chain = sem("s_dve_chain")
        s_gu_made = sem("s_gu_made")
        s_ov_base = sem("s_ov_base")
        s_slot_loaded = [sem(f"s_slot_loaded{i}") for i in range(SLOTS)]

        def rows_of(w, k, n=1):
            return w[k * 128:(k + n) * 128, :].rearrange("(a p) n -> p a n", p=128)

        w_in, w_kv = a["w_in"][0], a["w_mem_kv"][0]
        PRE = [rows_of(w, k, 2) for w in (w_in[:, 0:1024], w_in[:, 1024:], w_kv[:, 0:D], w_kv[:, D:], a["w_out"][0],
                                          a["w_mem_q"][0], a["w_mem_o"][0]) for k in (0, 2, 4, 6)]
        C_QK, C_VU, C_K, C_V, C_OUT, C_MQ, C_MO = range(0, 28, 4)
        w1, w2, b1 = a["w_expert_in"][0], a["w_expert_out"][0], a["b_expert_in"][0]
        wi2 = a["w_in_2"][0]
        A0, R0, G0 = 0, 4 * 512, 4 * 512 + 2176
        POST = ([wi2[:, R0 + 2048:G0].rearrange("(a p) n -> p a n", p=128)]
                + [rows_of(wi2[:, R0:R0 + 2048], k) for k in range(8)]
                + [rows_of(wi2[:, c:c + 1024], k, 2) for c in (A0, A0 + 1024, G0, G0 + 1024) for k in (0, 2, 4, 6)]
                + [rows_of(a["p_a_2"][0], k, 2) for k in (0, 2)] + [rows_of(a["w_ple_up_2"][0], 0, 2)]
                + [rows_of(a["p_b_2"][0], k, 2) for k in (0, 2)]
                + [rows_of(a[n][0], k, 2) for n in ("w_out_2", "w_ple_gate_2") for k in (0, 2, 4, 6)])
        P_GA, P_GB, P_PA, P_UP, P_PB, P_OUT = 17, 21, 25, 27, 28, 30
        assert len(POST) == 38
        U_RW, U_QK, U_VZ, U_OUT, U_PG, U_END = 1, 17, 25, 33, 41, 49
        USED_RW, USED_QK, USED_VZ, USED_GA, USED_GB = 17, 25, 33, 37, 41
        USED_PA, USED_UP, USED_PB, USED_OUT, USED_PG = 43, 44, 46, 54, 62
        NPRE, PER = len(PRE), 12
        MOE_END = NPRE + PER * N_EXP
        assert PER == SLOTS and NPRE % PRE_SLOTS == 0
        POST_SLOTS = (4, 5)

        def moe_slot(j):
            return j

        def pre_loads(sl):
            return NPRE // PRE_SLOTS if sl < PRE_SLOTS else 0

        def loads_before(sl):
            return pre_loads(sl) + N_EXP

        POST_ORDER = [n for n in range(len(POST)) if n not in (29, 30, 31)]
        POST_ORDER[29:29] = [30, 31, 29]

        def post_slot(n):
            if n in (30, 31):
                sl = (3, 10)[n - 30]
                return sl, loads_before(sl) + 1
            sl = POST_SLOTS[n % 2]
            return sl, loads_before(sl) + n // 2 + (1 if n < 30 else 0)

        def unit_chunk(u):
            if u == 0:
                return 0, 0
            return (1 + (u - 1) // 2, (u - 1) % 2) if u < U_OUT else (P_OUT + (u - U_OUT) // 2, (u - U_OUT) % 2)

        def used_after(u):
            return u + 1 if u < U_OUT else u + 1 + P_OUT - P_GA

        def view(sl, ap):
            return tk(slot(sl, 0, ap.shape[1] * ap.shape[2]), ap.shape[2])

        def bias_view(start):
            return bass.AP(bias_dram.tensor, start, [[512, 128], [128 * 513, HEADS], [1, 128]])

        bias_dram = nc.dram_tensor("bias_rows", [HEADS, 128, 513], f32, kind="Internal").ap()

        block = ctx.enter_context(nc.Block())

        @block.sync
        def _(sp):
            for h in range(TH):
                sp.dma_start(X[:, h, :], a["x"][0, 128 * h:128 * h + 128, :]).then_inc(s_x_loaded, 16)
            for n, w in enumerate(PRE):
                if n == 2:
                    for h in range(TH):
                        sp.dma_start(mem_rows[:, h, :], a["mem"][0, 128 * h:128 * h + 128, :]).then_inc(s_mem_loaded, 16)
                if n >= PRE_SLOTS:
                    sp.wait_ge(s_w_rest, n - PRE_SLOTS + 1)
                sp.dma_start(view(n % PRE_SLOTS, w), w).then_inc(s_slot_loaded[n % PRE_SLOTS], 16)

            def load_up(e, j):
                sp.dma_start(slot(moe_slot(j)), w1[bass.ds(e, 1), 128 * j:128 * j + 128, :]
                             .rearrange("a p n -> p (a n)")).then_inc(s_slot_loaded[moe_slot(j)], 16)

            def load_down(e, j):
                sp.dma_start(tk(slot(moe_slot(j)), D), w2[bass.ds(e, 1), 256 * (j - 8):256 * (j - 8) + 256, :]
                             .rearrange("a (k p) n -> p (a k) n", p=128)).then_inc(s_slot_loaded[moe_slot(j)], 16)

            def load_bias(e):
                sp.dma_start(b1_rows[0:33:32, :], b1[bass.ds(e, 1), :].rearrange("a (b n) -> (a b) n", b=2))\
                  .then_inc(s_b1_loaded, 16)

            sp.wait_ge(s_pooled_ready, 4)
            load_bias(0)
            sp.wait_ge(s_ring_used, C_OUT)
            load_up(0, 4)
            load_up(0, 5)
            for j in range(PRE_SLOTS):
                sp.wait_ge(s_w_rest, NPRE - PRE_SLOTS + j + 1)
                load_up(0, j)
            sp.wait_ge(s_ring_used, NPRE)
            load_up(0, 6)
            load_up(0, 7)
            for j in range(8, PER):
                load_down(0, j)
            with sp.Fori(1, N_EXP) as e:
                for j in range(PER):
                    sp.wait_ge(s_ring_used, e * PER + (NPRE + j - SLOTS + 1))
                    if j < 8:
                        load_up(e, j)
                    else:
                        load_down(e, j)
                    if j == 8:
                        load_bias(e)
            sp.wait_ge(s_flag_ready, 1)
            over = sp.value_load(flag[0:1, 0:1], min_val=0, max_val=1)
            with sp.If(over > 0):
                sp.wait_ge(s_ring_used, MOE_END)
                with sp.Fori(0, N_EXP) as e:
                    sp.wait_ge(s_ov_sc, e * (N_BLK - 1) + 1)
                    for j in range(8):
                        sp.dma_start(slot(moe_slot(j)), w1[bass.ds(e, 1), 128 * j:128 * j + 128, :]
                                     .rearrange("a p n -> p (a n)")).then_inc(s_ov_loaded, 16)
                    for j in range(8, PER):
                        sp.dma_start(tk(slot(moe_slot(j)), D),
                                     w2[bass.ds(e, 1), 256 * (j - 8):256 * (j - 8) + 256, :]
                                     .rearrange("a (k p) n -> p (a k) n", p=128)).then_inc(s_ov_loaded, 16)
                    sp.dma_start(b1_rows[0:33:32, :], b1[bass.ds(e, 1), :].rearrange("a (b n) -> (a b) n", b=2))\
                      .then_inc(s_ov_loaded, 16)
                sp.wait_ge(s_ov_sc, N_EXP * (N_BLK - 1) + 1)
            for n in POST_ORDER:
                sl, w = post_slot(n)[0], POST[n]
                gone = n - 4 if n in (32, 33) else n - 2
                if n < 2:
                    sp.wait_ge(s_ring_used, MOE_END - PER + sl + 1)
                elif n in (30, 31):
                    sp.wait_ge(s_y_psum, NCH)
                elif P_GA <= gone < P_OUT:
                    sp.wait_ge(s_ring_used, MOE_END + USED_VZ + gone - P_GA + 1)
                else:
                    last = 0 if gone == 0 else 2 * gone if gone < P_GA else U_OUT + 2 * (gone - P_OUT) + 1
                    sp.wait_ge(s_w_rest, NPRE + last + 1)
                sp.dma_start(view(sl, w), w).then_inc(s_slot_loaded[sl], 16)
            for h in range(TH):
                sp.wait_ge(s_out_ready, h + 1)
                sp.dma_start(out[0, 128 * h:128 * h + 128, :], HN[:, h, :]).then_inc(s_out_written, 16)
            sp.wait_ge(s_out_written, 16 * TH)

        @block.tensor
        def _(pe):
            mm, transpose = nc.tensor.matmul, nc.tensor.transpose

            def pre_chunk(n):
                pe.wait_ge(s_w_rest, n + 1)
                return tk(W_high[n % 2][:, :], D), tk(W_rest[n % 2][:, :], D)

            def xT_tile(m, k):
                pe.wait_ge(s_t_rest, 4 * m + k // 2 + 1)

            def post_chunk(n):
                sl, loads = post_slot(n)
                pe.wait_ge(s_slot_loaded[sl], 16 * loads)
                return view(sl, POST[n])

            def transpose_rows(rows, bank):
                ps = banks(bank, 4, S)
                for k in range(KT):
                    for h in range(TH):
                        t = transpose(ps[:, k, 128 * h:128 * h + 128], rows[:, h, 128 * k:128 * k + 128], ident)
                    if k % 4 == 3:
                        t.then_inc(s_norm_tr, 1)

            def project_rows(bank, xT, k, w, first, last, n=2):
                for h in range(TH):
                    for c in range(n):
                        t = mm(PS[:, bank + n * h + c, :], xT[:, k, 128 * h:128 * h + 128],
                               w[:, 512 * c:512 * c + 512], start=first, stop=last)
                return t

            def transpose_halves(rows, bank, ready, n):
                ps = banks(bank, 4, S)
                for h in range(TH):
                    pe.wait_ge(ready, n + h)
                    for k in range(KT):
                        t = transpose(ps[:, k, 128 * h:128 * h + 128], rows[:, h, 128 * k:128 * k + 128], ident)
                        if h == 1 and k % 4 == 3:
                            t.then_inc(s_norm_tr, 1)

            pe.wait_ge(s_const_loaded, 16)
            pe.wait_ge(s_param_loaded, 16)
            transpose(PS[:, 7, 0:128], par_rows[:, :], ident).then_inc(s_params_T, 1)
            hT, memT = (tk(HTH[:, :], S), tk(HTL[:, :], S)), (tk(memH[:, :], S), tk(memL[:, :], S))

            def split_T(wH, wL, c, xH, xL, o, first, last):
                cs = slice(128 * c, 128 * c + 128)
                mm(o, wH[:, cs], xH, start=first, stop=False)
                mm(o, wH[:, cs], xL, start=False, stop=False)
                return mm(o, wL[:, cs], xH, start=False, stop=last)

            def split_rows(wH, wL, cs, xH, xL, o, first, last):
                mm(o, xH, wH[:, cs], start=first, stop=False)
                mm(o, xH, wL[:, cs], start=False, stop=False)
                return mm(o, xL, wH[:, cs], start=False, stop=last)

            def dense_T(n0, lo, hi, m, xT, tiles=range(KT)):
                for n in range(lo, hi):
                    wH, wL = pre_chunk(n0 + n)
                    for i in range(2):
                        k = 2 * n + i
                        xT_tile(m, k)
                        for j in tiles:
                            t = split_T(wH[:, i], wL[:, i], j, xT[0][:, k, :], xT[1][:, k, :], banks(4, 4, S)[:, j, :],
                                        k == 0 and j % 2 == 0, k == KT - 1 and j % 2 == 1)
                    t.then_inc(s_ring_used, 1)

            def dense_rows(n0, lo, hi, m, xT, half_done=None):
                for n in range(lo, hi):
                    wH, wL = pre_chunk(n0 + n)
                    for i in range(2):
                        k = 2 * n + i
                        xT_tile(m, k)
                        for h in range(TH):
                            ts = slice(128 * h, 128 * h + 128)
                            for c in range(2):
                                t = split_rows(wH[:, i], wL[:, i], slice(512 * c, 512 * c + 512), xT[0][:, k, ts],
                                               xT[1][:, k, ts], PS[:, 4 + 2 * h + c, :], k == 0, k == KT - 1)
                            if half_done is not None and k == KT - 1 and h == 0:
                                t.then_inc(half_done, 1)
                    t.then_inc(s_ring_used, 1)

            pe.wait_ge(s_norm_rows, 2)
            transpose_rows(HN, 0)
            pe.wait_ge(s_params_cols, 1)
            dense_T(C_QK, 0, 2, 0, hT)
            pe.wait_ge(s_norm_rows, 4)
            transpose_rows(mem_rows, 0)
            dense_T(C_QK, 2, 4, 0, hT)
            pe.wait_ge(s_t_rest, 8)
            for n in range(4):
                wH, wL = pre_chunk(C_VU + n)
                for i in range(2):
                    k = 2 * n + i
                    first, last = k == 0, k == KT - 1
                    for h in range(TH):
                        ts = slice(128 * h, 128 * h + 128)
                        split_rows(wH[:, i], wL[:, i], slice(0, 512), hT[0][:, k, ts], hT[1][:, k, ts], PS[:, h, :],
                                   first, last)
                    for j in range(4):
                        t = split_T(wH[:, i], wL[:, i], 4 + j, hT[0][:, k, :], hT[1][:, k, :], banks(2, 2, S)[:, j, :],
                                    first and j % 2 == 0, last and j % 2 == 1)
                t.then_inc(s_ring_used, 1)

            def sb_scores(bank, g):
                for jj in range(2):
                    j = 2 * g + jj
                    for r in (0, HD):
                        mm(PS[:, bank + 2 * jj + r // HD, 0:256], qkT[r:r + HD, 4 + j, 0:128], qkT[r:r + HD, j, :],
                           start=True, stop=False)
                    for r in (0, HD):
                        t = mm(PS[:, bank + 2 * jj + r // HD, 256:384], qkT[r:r + HD, 4 + j, 128:256],
                               qkT[r:r + HD, j, 128:256], start=False, stop=True)
                t.then_inc(s_z_done, 1)

            def sb_sums(g):
                pe.wait_ge(s_sp_ready, g + 1)
                for i in range(4):
                    h = 4 * g + i
                    mm(PS[:, i, 0:256], C("tri_ge"), SP[:, h, 0:256], start=True, stop=False)
                    mm(PS[:, i, 128:256], ones, SP[:, h, 256:384], start=False, stop=False)
                    t = mm(PS[:, i, 256:384], C("tri_ge"), SP[:, h, 256:384], start=False, stop=True)
                t.then_inc(s_rev_done, 1)

            pe.wait_ge(s_qkv_evac, 2)
            sb_scores(4, 0)
            pe.wait_ge(s_vu_evac, 2)
            sb_scores(0, 1)
            pe.wait_ge(s_z_copied, 2)
            dense_T(C_K, 0, 3, 1, memT)
            sb_sums(0)
            dense_T(C_K, 3, 4, 1, memT)
            pe.wait_ge(s_arg_ready, 1)
            sb_sums(1)
            pe.wait_ge(s_qkv_evac, 4)
            dense_rows(C_V, 0, 1, 1, memT)
            pe.wait_ge(s_w_ready, 2)
            for h in range(HEADS):
                c = slice(HD * h, HD * h + HD)
                mm(PS[:, 0, c], SP[:, h, 0:128], v_rows[:, 0, c], start=h == 0, stop=h == HEADS - 1)
                mm(PS[:, 1, c], SP[:, h, 128:256], v_rows[:, 0, c], start=h == 0, stop=False)
                t = mm(PS[:, 1, c], SP[:, h, 256:384], v_rows[:, 1, c], start=False, stop=h == HEADS - 1)
            t.then_inc(s_sb_done, 1)
            pe.wait_ge(s_pooled_ready, 4)
            pe.wait_ge(s_small_loaded, 16 * 6)
            for h in range(TH):
                for g in range(4):
                    c = slice(128 * g, 128 * g + 128)
                    t = mm(PS[:, 2 + h, c], pooled[:, g, 128 * h:128 * h + 128], w_pool[:, c], start=g == 0, stop=g == 3)
            t.then_inc(s_pool_done, 1)
            dense_rows(C_V, 1, 4, 1, memT)
            pe.wait_ge(s_norm_rows, 6)
            transpose_rows(HN, 0)
            pe.wait_ge(s_qkv_evac, 6)
            dense_rows(C_OUT, 0, 4, 2, hT)

            transpose_halves(HN, 0, s_norm_rows, 7)
            dense_T(C_MQ, 0, 4, 3, hT)
            pe.wait_ge(s_memq_evac, 2)
            for h in range(4):
                for th in range(TH):
                    for d in range(2):
                        t = mm(PS[:, h, 256 * th:256 * th + 256], mqT[:, 2 * h + d, 128 * th:128 * th + 128],
                               mkT[:, 2 * h + d, :], start=th + d == 0, stop=th + d == 2)
                if h % 2 == 1:
                    t.then_inc(s_score_done, 1)
            for h in range(4):
                if h % 2 == 0:
                    pe.wait_ge(s_p_ready, h // 2 + 1)
                for m in range(2):
                    for th in range(TH):
                        t = transpose(banks(4, 4, S)[:, 2 * h + m, 128 * th:128 * th + 128],
                                      prob[:, 2 * h + th, 128 * m:128 * m + 128], ident)
                if h % 2 == 1:
                    t.then_inc(s_tr_p, 1)
            pe.wait_ge(s_pT_evac, 2)
            for j in range(KT):
                for m in range(2):
                    t = mm(banks(0, 4, S)[:, j, :], mv_rows[:, m, 128 * j:128 * j + 128], probT[:, 2 * (j // 2) + m, :],
                           start=j % 2 == 0 and m == 0, stop=j % 2 == 1 and m == 1)
                if j % 2 == 1:
                    t.then_inc(s_o_done, 1)
            dense_rows(C_MO, 0, 4, 4, hT, s_part_done)

            transpose_halves(HN, 4, s_norm_rows, 9)
            pe.wait_ge(s_norm_T, 2)
            for h in range(TH):
                c = slice(N_EXP * h, N_EXP * h + N_EXP)
                mm(PS[:, 0, c], ones[0:1, :], b_router[0:1, :], start=h == 0, stop=False)
                for k in range(KT):
                    t = mm(PS[:, 0, c], HT[:, k, 128 * h:128 * h + 128], w_router[:, k, :], start=False,
                           stop=h == 1 and k == KT - 1)
            t.then_inc(s_logits_done, 1)
            pe.wait_ge(s_late_loaded, 16)
            pe.wait_ge(s_rbias_ready, 16)
            mm(PS[0:HEADS, 3, :], rbias[0:33, :], C("bias_sel")[0:33, :], start=True, stop=True).then_inc(s_frow_done, 1)
            pe.wait_ge(s_mask_ready, 1)
            mm(PS[:, 1, 0:32], C("tri_lt"), mask[:, 0, :], start=True, stop=False)
            mm(PS[:, 1, 32:64], ones, mask[:, 0, :], start=False, stop=False)
            mm(PS[:, 1, 32:64], C("tri_lt"), mask[:, 1, :], start=False, stop=False)
            mm(PS[:, 1, 64:96], ones, mask[:, 0, :], start=False, stop=False)
            mm(PS[:, 1, 64:96], ones, mask[:, 1, :], start=False, stop=True).then_inc(s_rank_done, 1)
            pe.wait_ge(s_gates_ready, 1)
            for h in range(TH):
                t = transpose(PS[0:N_EXP, 2, 128 * h:128 * h + 128], gate[:, h, 0:N_EXP], ident)
            t.then_inc(s_gT_done, 1)

            def gather():
                for k in range(KT):
                    for h in range(TH):
                        t = mm(banks(0, 1, CAP)[:, k, :], HN[:, h, 128 * k:128 * k + 128], pick[:, h, :],
                               start=k + h == 0, stop=k + h == KT)
                return t

            def up_bias():
                for c in range(2):
                    for b in range(2):
                        mm(PS[CAP * c:CAP * c + CAP, 2 + b, :], ones[32 * b:32 * b + 1, 0:CAP],
                           b1_rows[32 * b:32 * b + 1, 512 * c:512 * c + 512], start=True, stop=False)

            def up(k):
                w = slot(moe_slot(k))
                for b in range(2):
                    for c in range(2):
                        t = mm(PS[CAP * c:CAP * c + CAP, 2 + b, :], xT_e[:, k, :],
                               w[:, D * b + 512 * c:D * b + 512 * c + 512], start=False, stop=k == KT - 1)
                return t

            def turn_gpick():
                for h in range(TH):
                    t = transpose(PS[:, 1, 128 * h:128 * h + 128], gpick[:, h, :], ident)
                return t

            def turn_act():
                for b in range(4):
                    t = transpose(PS[:, 1, 128 * b:128 * b + 128], act_e[:, 128 * b:128 * b + 128], ident)
                return t

            def down(n):
                w = tk(slot(moe_slot(8 + n)), D)
                for i in range(2):
                    k = 2 * n + i
                    for c in range(2):
                        t = mm(PS[CAP * c:CAP * c + CAP, 0, :], actT[:, k % 4, k // 4, :],
                               w[:, i, 512 * c:512 * c + 512], start=k == 0, stop=k == KT - 1)
                return t

            def scatter():
                for h in range(TH):
                    for c in range(2):
                        t = mm(PS[:, 4 + 2 * h + c, :], gpT[CAP * c:CAP * c + CAP, 128 * h:128 * h + 128],
                               y_e[CAP * c:CAP * c + CAP, :], start=False, stop=True, skip_group_check=True)
                return t

            pe.wait_ge(s_pe_ready, 1)
            gather().then_inc(s_gathered, 1)
            pe.wait_ge(s_frow_evac, 1)
            pe.wait_ge(s_gT_evac, 1)

            def expert_products(e, first=False):
                pe.wait_ge(s_gu_free, e + 1)
                pe.wait_ge(s_b1_loaded, (e + 1) * 16)
                up_bias()
                pe.wait_ge(s_xT_ready, e + 1)
                for k in range(KT):
                    pe.wait_ge(s_slot_loaded[moe_slot(k)], (e + (pre_loads(moe_slot(k)) + 1)) * 16)
                    up(k).then_inc(s_ring_used, 1)
                pe.wait_ge(s_gp_ready, e + 1)
                turn_gpick().then_inc(s_gpt_done, 1)
                pe.wait_ge(s_pe_ready, e + 2)
                gather().then_inc(s_gathered, 1)
                if first:
                    pe.wait_ge(s_b2_loaded, 16)
                    for h in range(TH):
                        for c in range(2):
                            mm(PS[:, 4 + 2 * h + c, :], gT[0:N_EXP, 128 * h:128 * h + 128],
                               b2_all[0:N_EXP, 512 * c:512 * c + 512], start=True, stop=True)
                pe.wait_ge(s_act_ready, e + 1)
                pe.wait_ge(s_gpt_evac, e + 1)
                turn_act().then_inc(s_actT_done, 1)
                pe.wait_ge(s_actT_evac, e + 1)
                pe.wait_ge(s_xT_ready, e + 2)
                for n in range(4):
                    pe.wait_ge(s_slot_loaded[moe_slot(8 + n)], (e + (pre_loads(moe_slot(8 + n)) + 1)) * 16)
                    down(n).then_inc(s_ring_used, 1)
                pe.wait_ge(s_y_evac, e + 1)
                scatter().then_inc(s_scattered, 1)

            expert_products(0, first=True)
            with pe.Fori(1, N_EXP) as e:
                expert_products(e)

            pe.wait_ge(s_flag_ready, 1)
            over = pe.value_load(flag[0:1, 0:1], min_val=0, max_val=1)
            with pe.If(over > 0):
                NB = N_BLK - 1
                pe.wait_ge(s_gu_free, N_EXP + 1)
                with pe.Fori(0, N_EXP) as e:
                    pe.wait_ge(s_ov_loaded, (e + 1) * (16 * (PER + 1)))
                    for b in range(NB):
                        pe.wait_ge(s_pe_ready, e * NB + (N_EXP + 1 + b + 1))
                        gather().then_inc(s_gathered, 1)
                        turn_gpick().then_inc(s_gpt_done, 1)
                        pe.wait_ge(s_xT_ready, e * NB + (N_EXP + 1 + b + 1))
                        up_bias()
                        for k in range(KT):
                            t = up(k)
                        t.then_inc(s_ov_up, 1)
                        pe.wait_ge(s_gpt_evac, e * NB + (N_EXP + b + 1))
                        pe.wait_ge(s_act_ready, e * NB + (N_EXP + b + 1))
                        turn_act().then_inc(s_actT_done, 1)
                        pe.wait_ge(s_actT_evac, e * NB + (N_EXP + b + 1))
                        for n in range(4):
                            t = down(n)
                        t.then_inc(s_ov_down, 1)
                        pe.wait_ge(s_y_evac, e * NB + (N_EXP + b + 1))
                        scatter().then_inc(s_ov_sc, 1)
            transpose_halves(HN, 0, s_norm_rows, 13)
            uT = tk(uTH[:, :], S), tk(uTL[:, :], S)

            def post_unit(u):
                pe.wait_ge(s_w_rest, NPRE + u + 1)
                return W2_high[u % 2][:, :], W2_rest[u % 2][:, :]

            def unit_T(u, k, bank, tiles=range(KT)):
                wH, wL = post_unit(u)
                for j in tiles:
                    t = split_T(wH, wL, j, uT[0][:, k, :], uT[1][:, k, :], banks(bank, 4, S)[:, j, :],
                                k == 0 and j % 2 == 0, k == KT - 1 and j % 2 == 1)
                return t

            def unit_rows(u, k, m):
                wH, wL = post_unit(u)
                xT_tile(m, k)
                for h in range(TH):
                    ts = slice(128 * h, 128 * h + 128)
                    for c in range(2):
                        t = split_rows(wH, wL, slice(512 * c, 512 * c + 512), uT[0][:, k, ts], uT[1][:, k, ts],
                                       PS[:, 4 + 2 * h + c, :], k == 0, k == KT - 1)
                    if k == KT - 1 and h == 0:
                        t.then_inc(s_part_done, 1)
                t.then_inc(s_ring_used, 1)

            wH, wL = (tk(w, 128) for w in post_unit(0))
            for k in range(KT):
                xT_tile(5, k)
                t = split_T(wH[:, k, :], wL[:, k, :], 0, uT[0][:, k, :], uT[1][:, k, :], PS[:, 4, 0:256], k == 0, k == KT - 1)
            t.then_inc(s_ring_used, 1)
            for k in range(KT):
                for half in range(2):
                    if k == 0 and half == 1:
                        pe.wait_ge(s_lora_evac, 1)
                    unit_T(U_RW + 2 * k + half, k, 4 * half).then_inc(s_ring_used, 1)
            pe.wait_ge(s_tanh_ready, 1)
            pe.wait_ge(s_rw_mix, 2)
            for j in range(4):
                mm(banks(0, 2, S)[:, j, :], lora_w[0:64, 128 * j:128 * j + 128], lora_t[0:64, :],
                   start=j % 2 == 0, stop=j % 2 == 1)
            pe.wait_ge(s_rw_mix, 4)
            for j in range(4):
                t = mm(banks(2, 2, S)[:, j, :], lora_w[64:128, 128 * j:128 * j + 128], lora[64:128, :],
                       start=j % 2 == 0, stop=j % 2 == 1)
            t.then_inc(s_wl_done, 1)

            pe.wait_ge(s_rw_mix, 8)
            for k in range(KT):
                unit_T(U_QK + k, k, 4).then_inc(s_ring_used, 1)
            pe.wait_ge(s_wl_sig, 8)
            pe.wait_ge(s_kk_sq, 1)
            for b in range(2):
                t = mm(PS[:, b, :], C("head_ones"), kk_sq[:, 512 * b:512 * b + 512], start=True, stop=True)
            t.then_inc(s_head_sums, 1)
            pe.wait_ge(s_bon_in, 1)
            for b in range(2):
                t = mm(PS[:, 2 + b, :], C("head_ones"), bon_in[:, 512 * b:512 * b + 512], start=True, stop=True)
            t.then_inc(s_head_sums, 1)
            def moba_scores(g):
                for jj in range(2):
                    j = 2 * g + jj
                    for r in (0, HD):
                        q, k = qk2[r:r + HD, j, :], qk2[r:r + HD, 4 + j, :]
                        mm(PS[:, 2 * jj + r // HD, 0:128], q[:, 0:128], k[:, 0:128], start=True, stop=False)
                    for r in (0, HD):
                        q, k = qk2[r:r + HD, j, :], qk2[r:r + HD, 4 + j, :]
                        t = mm(PS[:, 2 * jj + r // HD, 128:384], q[:, 128:256], k, start=False, stop=True)
                t.then_inc(s_moba_s, 1)

            pe.wait_ge(s_qkv_evac, 8)
            for k in range(KT):
                wH, wL = post_unit(U_VZ + k)
                for h in range(TH):
                    ts = slice(128 * h, 128 * h + 128)
                    split_rows(wH, wL, slice(0, 512), uT[0][:, k, ts], uT[1][:, k, ts], PS[:, 4 + h, :], k == 0, k == KT - 1)
                for j in range(4):
                    t = split_T(wH, wL, 4 + j, uT[0][:, k, :], uT[1][:, k, :], banks(6, 2, S)[:, j, :],
                                k == 0 and j % 2 == 0, k == KT - 1 and j % 2 == 1)
                t.then_inc(s_ring_used, 1)
                if k == 3:
                    pe.wait_ge(s_kk_sqrt, 1)
                    pe.wait_ge(s_bon_ready, 1)
                    moba_scores(0)
                if k == 5:
                    pe.wait_ge(s_moba_read, 1)
                    moba_scores(1)

            def moba_turn(g):
                for i in range(4):
                    for b in range(3):
                        t = transpose(PS[:, 4 + i, 128 * b:128 * b + 128],
                                      prob2[:, 4 * g + i, 128 * b:128 * b + 128], ident)
                    if g:
                        t = transpose(PS[:, 4 + i, 384:512], p_rows[:, i % 2, 128 * (i // 2):128 * (i // 2) + 128], ident)
                t.then_inc(s_moba_tr, 1)

            def part(n0, lo, hi, xT, tiles, bank_done=None):
                for i in range(lo, hi):
                    k, j = i // 8, i % 8
                    w = post_chunk(n0 + k // 2)
                    t = mm(banks(0, 4, S)[:, j, :], w[:, k % 2, 128 * j:128 * j + 128], xT[:, k, :],
                           start=k == 0 and j % 2 == 0, stop=k == tiles - 1 and j % 2 == 1)
                    if i % 16 == 15:
                        t.then_inc(s_ring_used, 1)
                    elif bank_done is not None and k == tiles - 1 and j % 2 == 1:
                        t.then_inc(bank_done, 1)

            def gate_a_part(lo, hi):
                part(P_GA, lo, hi, HT, KT)

            def gate_b_part(lo, hi):
                part(P_GB, lo, hi, HT, KT)

            pe.wait_ge(s_norm_T, 3)
            pe.wait_ge(s_moba_read, 2)
            gate_a_part(0, 16)
            pe.wait_ge(s_a_evac, 2)
            pe.wait_ge(s_moba_p, 1)
            moba_turn(0)
            gate_a_part(16, 32)
            pe.wait_ge(s_moba_pT, 2)
            pe.wait_ge(s_moba_p, 2)
            pe.wait_ge(s_p_loaded, 16)
            moba_turn(1)
            gate_a_part(32, 40)

            def pair_product(out, sets, lhs, rhs):
                for i, n in enumerate(sets):
                    for r in (0, HD):
                        t = mm(out[r:r + HD, i], lhs(n, r), rhs(n, r), start=True, stop=True)
                return t

            def of(x):
                if len(x.shape) == 3:
                    return lambda n, r: x[r:r + HD, :, L * n:L * n + L]
                v = tk(x, L)
                return lambda n, r: v[r:r + HD, n, :]

            def eye_block(n, r):
                return ident[r:r + HD, r:r + HD]

            def half_sets(hf):
                return range(NSET // 2 * hf, NSET // 2 * hf + NSET // 2)

            def wide(bank):
                return PS[:, bank:bank + 2, :].rearrange("p b (n a t) -> p (b n) a t", a=2, t=L)

            pe.wait_ge(s_moba_pT, 4)
            for h in range(HEADS):
                j, r, c = h // 2, HD * (h % 2), slice(HD * h, HD * h + HD)
                mm(banks(4, 2, S)[r:r + HD, j, :], v2[:, 0, c], prob2T[:, h, 0:256], start=j % 2 == 0, stop=False)
                t = mm(banks(4, 2, S)[r:r + HD, j, 128:256], v2[:, 1, c], prob2T[:, h, 256:384], start=False,
                       stop=j % 2 == 1)
            t.then_inc(s_moba_o, 1)
            pair_product(banks(6, 2, L), range(NSET), of(rw_v), eye_block).then_inc(s_pairs_done, 1)
            gate_a_part(40, 44)
            pe.wait_ge(s_ya_ready, 1)
            pe.wait_ge(s_wkv_T, 3)
            pair_product(banks(4, 2, L), range(NSET), of(bT), eye_block).then_inc(s_pairs_done, 1)
            gate_a_part(44, 48)
            pe.wait_ge(s_rows_evac, 1)
            pair_product(banks(6, 2, L), range(NSET), of(kTl), eye_block).then_inc(s_pairs_done, 1)
            gate_a_part(48, 52)
            pe.wait_ge(s_rows_evac, 2)
            for hf in range(2):
                pair_product(banks(4 + hf, 1, L), half_sets(hf), of(aT), of(bT)).then_inc(s_pairs_done, 1)
            gate_a_part(52, 56)
            pe.wait_ge(s_rows_evac, 3)
            pair_product(wide(6), half_sets(0), of(bT), of(a_r)).then_inc(s_pairs_done, 1)
            gate_a_part(56, 60)
            pe.wait_ge(s_mat_evac, 2)
            pair_product(wide(4), half_sets(1), of(bT), of(a_r)).then_inc(s_pairs_done, 1)
            gate_a_part(60, 64)
            pe.wait_ge(s_mat_evac, 5)
            pair_product(wide(6), half_sets(0), of(kTl), of(a_r)).then_inc(s_pairs_done, 1)
            pe.wait_ge(s_gate_evac, 1)
            gate_b_part(0, 4)
            pe.wait_ge(s_mat_evac, 8)
            pair_product(wide(4), half_sets(1), of(kTl), of(a_r)).then_inc(s_pairs_done, 1)
            gate_b_part(4, 8)
            for i, (x, y, res) in enumerate(SOLVE):
                for hf in range(2):
                    if i == 0:
                        pe.wait_ge(s_sol_ready, 1 + hf)
                    else:
                        pe.wait_ge(s_sol_evac, 2 * (i - 1) + hf + 1)
                    if y is off_eye and hf == 0:
                        pe.wait_ge(s_eye_set, 1)
                    ps = wide(6 - 2 * hf) if len(res) == 2 else banks(6 - 2 * hf, 1, L)
                    pair_product(ps, half_sets(hf), of(x), of(y)).then_inc(s_sol_done, 1)
                    n = 2 * i + hf
                    gate_b_part(8 + 56 * n // 24, 8 + 56 * (n + 1) // 24)
            pe.wait_ge(s_sol_evac, 2 * len(SOLVE))

            oY = banks(6, 2, S)
            for c in range(NCH):
                def pairs(g):
                    return [(j, j * NCH + c, r) for j in (2 * g, 2 * g + 1) for r in (0, HD)]

                def block_of(g, which, j, r):
                    return PS[r:r + HD, 4 + g, 128 * which + L * (j % 2):128 * which + L * (j % 2) + L]

                for g in range(2):
                    if c:
                        pe.wait_ge(s_rec_state, 2 * (c - 1) + g + 1)
                    for j, n, r in pairs(g):
                        t = mm(block_of(g, 0, j, r), of(akT)(n, r), of(v_tok)(n, r), start=j == 2 * g, stop=c == 0 and j == 2 * g + 1)
                    if c:
                        for j, n, r in pairs(g):
                            t = mm(block_of(g, 0, j, r), of(aT)(n, r), state[c % 2][r:r + HD, j, :], start=False, stop=j == 2 * g + 1)
                    t.then_inc(s_rec_x, 1)
                if c:
                    part(P_PA, 8 * c, 8 * c + 4, ya, 4)
                for g in range(2):
                    pe.wait_ge(s_rec_xe, 2 * c + g + 1)
                    for j, n, r in pairs(g):
                        t = mm(block_of(g, 1, j, r), of(invT)(n, r), rec_rhs[r:r + HD, j, :], start=j == 2 * g, stop=j == 2 * g + 1)
                    t.then_inc(s_rec_sa, 1)
                if c:
                    part(P_PA, 8 * c + 4, 8 * c + 8, ya, 4)
                else:
                    pe.wait_ge(s_gate_evac, 2)
                    part(P_PA, 0, 8, ya, 4)
                for g in range(2):
                    pe.wait_ge(s_rec_sae, 2 * c + g + 1)
                    if c < NCH - 1:
                        for j, n, r in pairs(g):
                            mm(block_of(g, 2, j, r), of(b_tok)(n, r), rec_sa[r:r + HD, j, :], start=j == 2 * g, stop=False)
                        for j, n, r in pairs(g):
                            t = mm(block_of(g, 2, j, r), of(k_tok)(n, r), of(v_tok)(n, r), start=False, stop=j == 2 * g + 1)
                        t.then_inc(s_rec_s, 1)
                for g in range(2):
                    for j, n, r in pairs(g):
                        o = oY[r:r + HD, j, L * c:L * c + L]
                        mm(o, rec_sa[r:r + HD, j, :], of(rbT)(n, r), start=c == 0 and j % 2 == 0, stop=False)
                    if c:
                        for j, n, r in pairs(g):
                            mm(oY[r:r + HD, j, L * c:L * c + L], state[c % 2][r:r + HD, j, :], of(r_dec)(n, r), start=False, stop=False)
                    for j, n, r in pairs(g):
                        t = mm(oY[r:r + HD, j, L * c:L * c + L], of(v_tok)(n, r), of(rkT)(n, r), start=False,
                               stop=c == NCH - 1 and j % 2 == 1)
                t.then_inc(s_y_psum, 1)
            pe.wait_ge(s_yT_evac, 1)
            for b in range(2):
                t = mm(PS[:, 4 + b, :], C("head_ones"), yT[:, 512 * b:512 * b + 512], start=True, stop=True)
            t.then_inc(s_gn_sums, 1)
            pe.wait_ge(s_pa_used, 1)
            w = post_chunk(P_UP)
            project_rows(0, pT, 0, w[:, 0, :], True, False)
            pe.wait_ge(s_gn_sq, 1)
            for b in range(2):
                t = mm(PS[:, 6 + b, :], C("head_ones"), ysq[:, 512 * b:512 * b + 512], start=True, stop=True)
            t.then_inc(s_gn_sums, 1)
            project_rows(0, pT, 1, w[:, 1, :], False, True).then_inc(s_ring_used, 1)
            pe.wait_ge(s_e_evac, 1)
            for k in range(4):
                pe.wait_ge(s_yb_ready, k + 1)
                part(P_PB, 8 * k, 8 * k + 8, yb, 4, s_part_done)
            for k in range(KT):
                unit_rows(U_OUT + k, k, 6)
            transpose_halves(X, 0, s_h2_ready, 1)
            for k in range(KT):
                unit_rows(U_PG + k, k, 7)

        @block.scalar
        def _(act):
            fn = nc.scalar.activation

            def stats(n, halves, width, eps_col):
                for h, (rows, scratch) in enumerate(halves):
                    fn(scratch, rows, ACT.Square, accum_out=stat[:, 2 * n + h:2 * n + h + 1]).then_inc(s_norm_sq, 1)
                act.wait_ge(s_norm_sq, 2 * n + 2)
                fn(stat[:, 16 + 2 * n:18 + 2 * n], stat[:, 2 * n:2 * n + 2], ACT.Sqrt, scale=1.0 / width,
                   bias=eps[:, eps_col:eps_col + 1]).then_inc(s_norm_std, 1)

            def scale_half(n, dst, src):
                act.wait_ge(s_norm_rstd, n + 1)
                fn(dst, src, ACT.Copy, scale=stat[:, 32 + 2 * n + 1:32 + 2 * n + 2]).then_inc(s_norm_rows, 1)

            warmed = [0]

            def warm(func):
                col = 80 + warmed[0]
                warmed[0] += 1
                fn(stat[:, col:col + 1], eps[:, 0:1], func)

            def half_root(n, h, eps_col, rows, scratch):
                fn(scratch, rows, ACT.Square, accum_out=stat[:, 2 * n + h:2 * n + h + 1]).then_inc(s_norm_sq, 1)
                act.wait_ge(s_norm_sq, 2 * n - 1 + h)
                fn(stat[:, 16 + 2 * n + h:17 + 2 * n + h], stat[:, 2 * n + h:2 * n + h + 1], ACT.Sqrt, scale=1.0 / D,
                   bias=eps[:, eps_col:eps_col + 1]).then_inc(s_norm_std, 1)

            def second_half(n):
                act.wait_ge(s_norm_rstd, 2 * n - 2)
                fn(HN[:, 1, :], X[:, 1, :], ACT.Copy, scale=stat[:, 33 + 2 * n:34 + 2 * n]).then_inc(s_norm_rows, 1)

            def evac_T(m, bank, dst, gain):
                act.wait_ge(s_norm_tr, 2 * m)
                for k in range(4, KT):
                    t = fn(dst[:, k, :], banks(bank, 4, S)[:, k, :], ACT.Copy, scale=P(gain, k) if gain else 1.0)
                t.then_inc(s_norm_T, 1)

            def split_w(n):
                act.wait_ge(s_slot_loaded[n % PRE_SLOTS], 16 * (n // PRE_SLOTS + 1))
                if n >= 2:
                    act.wait_ge(s_ring_used, n - 1)
                fn(W_high[n % 2][:, :], slot(n % PRE_SLOTS), ACT.Copy).then_inc(s_w_high, 1)

            def split_unit(u):
                n, half = unit_chunk(u)
                sl, loads = post_slot(n)
                act.wait_ge(s_slot_loaded[sl], 16 * loads)
                if u >= 2:
                    act.wait_ge(s_ring_used, MOE_END + used_after(u - 2))
                fn(W2_high[u % 2][:, :], slot(sl, D * half, D * half + D), ACT.Copy).then_inc(s_w_high, 1)

            def split_units(lo, hi):
                for u in range(lo, hi):
                    split_unit(u)

            def split_T(m, high, gain):
                ps, dst = banks(0, 4, S), tk(high[:, :], S)
                for k in range(0, KT, 2):
                    if k % 4 == 0:
                        act.wait_ge(s_norm_tr, 2 * m + k // 4 + 1)
                    if gain is None:
                        fn(dst[:, k:k + 2, :], ps[:, k:k + 2, :], ACT.Copy).then_inc(s_t_high, 1)
                        continue
                    fn(dst[:, k, :], ps[:, k, :], ACT.Copy, scale=P(gain, k))
                    fn(dst[:, k + 1, :], ps[:, k + 1, :], ACT.Copy, scale=P(gain, k + 1)).then_inc(s_t_high, 1)

            act.dma_start(cst[:, 0:LATE], a["consts"][:, 0:LATE]).then_inc(s_const_loaded, 16)
            act.dma_start(par_rows[:, :], a["params"]).then_inc(s_param_loaded, 16)
            act.dma_start(cst[:, LATE:], a["consts"][:, LATE:]).then_inc(s_late_loaded, 16)
            act.dma_start(w_pool[:, :].rearrange("p (g e) -> p g e", g=4), a["w_pool"][0].rearrange("g c e -> c g e"))\
               .then_inc(s_small_loaded, 16)
            act.dma_start(scale_bc[:, :], a["pool_scale"][0].partition_broadcast(128)).then_inc(s_small_loaded, 16)
            act.dma_start(w_router[:, :, :], a["w_router"][0].rearrange("(k p) e -> p k e", p=128)).then_inc(s_small_loaded, 16)
            act.dma_start(b_router[:, :], a["b_router"]).then_inc(s_small_loaded, 16)
            act.dma_start(lora_w[0:64, :], a["w_up_2"][0]).then_inc(s_small_loaded, 16)
            act.dma_start(lora_w[64:128, :], a["a_up_2"][0]).then_inc(s_small_loaded, 16)

            act.wait_ge(s_eps_set, 1)
            warm(ACT.Sqrt)
            act.wait_ge(s_x_loaded, 32)
            stats(0, [(X[:, h, :], HN[:, h, :]) for h in range(TH)], D, 0)
            scale_half(0, HN[:, 1, :], X[:, 1, :])
            split_w(0)
            act.wait_ge(s_params_cols, 1)
            split_T(0, HTH, "g_mix")
            split_w(1)
            act.wait_ge(s_norm_tr, 2)
            act.wait_ge(s_mem_loaded, 32)
            stats(1, [(mem_rows[:, h, :], HN[:, h, :]) for h in range(TH)], D, 0)
            scale_half(1, mem_rows[:, 1, :], mem_rows[:, 1, :])
            split_w(2)
            split_w(3)
            split_T(1, memH, "g_mem_kv")
            split_w(4)
            act.wait_ge(s_ring_used, C_VU)
            fn(qkT[:, 0:4, :], banks(4, 2, S), ACT.Copy, scale=HD ** -0.5).then_inc(s_qkv_evac, 1)
            for n in range(5, 9):
                split_w(n)
            act.wait_ge(s_ring_used, C_K)
            fn(v_rows, PS[:, 0:2, :], ACT.Copy).then_inc(s_vu_evac, 1)
            split_w(9)
            act.wait_ge(s_z_done, 2)
            fn(Z[:, 4:8, :], PS[:, 0:4, 0:384], ACT.Copy).then_inc(s_z_copied, 1)

            def heads(x, g):
                return x[:, 4 * g:4 * g + 4, :]

            def weights(g):
                act.wait_ge(s_arg_ready, g + 1)
                fn(SP[:, 4 * g:4 * g + 4, :], Z[:, 4 * g:4 * g + 4, :], ACT.Exp).then_inc(s_w_ready, 1)

            act.wait_ge(s_z_copied, 2)
            for g in range(2):
                fn(heads(SP, g), heads(Z, g), ACT.Abs).then_inc(s_z_abs, 1)
            for g in range(2):
                act.wait_ge(s_z_abs, g + 1)
                fn(heads(SP, g), heads(SP, g), ACT.Exp, scale=-1.0).then_inc(s_z_abs, 1)
            split_w(10)
            for g in range(2):
                act.wait_ge(s_z_abs, 2 + g + 1)
                fn(heads(SP, g), heads(SP, g), ACT.Ln, bias=1.0).then_inc(s_z_ln, 1)
            split_w(11)
            warm(ACT.Exp)
            split_w(12)
            weights(0)
            act.wait_ge(s_ring_used, C_V)
            fn(mkT[:, 0:4, :], banks(4, 2, S), ACT.Copy).then_inc(s_qkv_evac, 1)
            split_w(13)
            weights(1)
            warm(ACT.Sqrt)
            split_w(14)
            act.wait_ge(s_sb_done, 1)
            for h in range(TH):
                fn(buf(7, 512 * h, 512 * h + 512), PS[:, h, :], ACT.Square, accum_out=stat[:, 48 + h:49 + h]).then_inc(s_mix_sq, 1)
            act.wait_ge(s_pool_scaled, 2)
            for h in range(TH):
                fn(buf(7, 1024 + 512 * h, 1536 + 512 * h), HN[:, h, 512:], ACT.Square,
                   accum_out=stat[:, 50 + h:51 + h]).then_inc(s_mix_sq, 1)
            act.wait_ge(s_mix_sq, 4)
            fn(stat[:, 52:56], stat[:, 48:52], ACT.Sqrt, scale=1.0 / 512, bias=eps[:, 0:1]).then_inc(s_mix_std, 1)
            act.wait_ge(s_mix_rstd, 1)
            for h in range(TH):
                t = fn(HN[:, h, 0:512], PS[:, h, :], ACT.Copy, scale=stat[:, 56 + h:57 + h])
            t.then_inc(s_norm_rows, 1)
            split_w(15)
            split_w(16)
            act.wait_ge(s_ring_used, C_OUT)
            fn(mv_rows[:, 0, :].rearrange("p (b n) -> p b n", b=2), PS[:, 4:6, :], ACT.Copy).then_inc(s_qkv_evac, 1)
            split_T(2, HTH, "g_sb_out")
            for n in range(17, 21):
                split_w(n)
            for h in range(TH):
                act.wait_ge(s_x_new, h + 1)
                if h == 0:
                    act.wait_ge(s_norm_tr, 6)
                half_root(3, h, 0, X[:, h, :], HN[:, h, :])
            second_half(3)
            split_T(3, HTH, "g_mem_q")
            for n in range(21, 25):
                split_w(n)
            act.wait_ge(s_ring_used, C_MO)
            fn(mqT[:, 0:4, :], banks(4, 2, S), ACT.Copy, scale=256 ** -0.5).then_inc(s_memq_evac, 1)
            split_w(25)
            warm(ACT.Exp)
            for i in range(8):
                if i % 4 == 0:
                    act.wait_ge(s_score_max, i // 4 + 1)
                fn(prob[:, i, :], banks(0, 4, S)[:, i, :], ACT.Exp, bias=mstat[:, 8 + i:9 + i],
                   accum_out=mstat[:, 16 + i:17 + i]).then_inc(s_p_exp, 1)
            act.wait_ge(s_tr_p, 1)
            fn(probT[:, 0:4, :], banks(4, 2, S), ACT.Copy).then_inc(s_pT_evac, 1)
            for b in range(4):
                act.wait_ge(s_o_done, b + 1)
                fn(tk(HTH[:, :], S)[:, 2 * b:2 * b + 2, :], banks(b, 1, S), ACT.Copy).then_inc(s_t_high, 1)
            split_w(26)
            split_w(27)
            warm(ACT.Sqrt)
            for h in range(TH):
                act.wait_ge(s_x_new, 2 + h + 1)
                if h == 0:
                    act.wait_ge(s_norm_tr, 8)
                half_root(4, h, 0, X[:, h, :], HN[:, h, :])
            second_half(4)
            evac_T(5, 4, HT, "g_ffn")
            act.dma_start(b2_all[0:N_EXP, :], a["b_expert_out"][0]).then_inc(s_b2_loaded, 16)
            act.dma_start(g_final, a["g_final"].partition_broadcast(128)).then_inc(s_g_loaded, 16)
            act.dma_start(g_post, a["g_post_2"][0].partition_broadcast(128)).then_inc(s_g_loaded, 16)
            act.wait_ge(s_top_ready, 1)
            for h in range(TH):
                t = fn(lg[:, h, :], lg[:, h, :], ACT.Exp, bias=stat[:, 60 + h:61 + h])
            t.then_inc(s_top_exp, 1)
            act.wait_ge(s_frow_done, 1)
            fn(frow[0:HEADS, :], PS[0:HEADS, 3, :], ACT.Copy).then_inc(s_frow_evac, 1)
            act.wait_ge(s_frow_evac, 1)
            act.dma_start(bias_dram[:, :, 0:512], frow[0:HEADS, :].unsqueeze(1).to_broadcast([HEADS, 128, 512])).then_inc(s_bias_written, 16)
            act.wait_ge(s_bias_written, 16)
            for b in range(2):
                src = bias_view(255 - 128 * b)
                act.dma_start(bias[:, :, b, :], src).then_inc(s_bias_read, 16)

            def silu_gate():
                return fn(sig, g7, ACT.Sigmoid, scale=1.702)

            def copy_gpT():
                return fn(gpT, PS[:, 1, 0:256], ACT.Copy)

            def copy_actT():
                return fn(actT, PS[:, 1, :].rearrange("p (b h c) -> p b h c", b=4, h=2), ACT.Copy)

            def copy_y():
                return fn(y_e, PS[:, 0, :], ACT.Copy)

            with act.Fori(0, N_EXP) as e:
                act.wait_ge(s_sig_in, e + 1)
                silu_gate().then_inc(s_sig_out, 1)
                act.wait_ge(s_gpt_done, e + 1)
                copy_gpT().then_inc(s_gpt_evac, 1)
                act.wait_ge(s_actT_done, e + 1)
                copy_actT().then_inc(s_actT_evac, 1)
                act.wait_ge(s_ring_used, e * PER + (NPRE + PER))
                copy_y().then_inc(s_y_evac, 1)
            act.wait_ge(s_flag_ready, 1)
            over = act.value_load(flag[0:1, 0:1], min_val=0, max_val=1)
            with act.If(over > 0):
                NB = N_BLK - 1
                with act.Fori(0, N_EXP * NB) as n:
                    act.wait_ge(s_gpt_done, n + (N_EXP + 1))
                    copy_gpT().then_inc(s_gpt_evac, 1)
                    act.wait_ge(s_sig_in, n + (N_EXP + 1))
                    silu_gate().then_inc(s_sig_out, 1)
                    act.wait_ge(s_actT_done, n + (N_EXP + 1))
                    copy_actT().then_inc(s_actT_evac, 1)
                    act.wait_ge(s_ov_down, n + 1)
                    copy_y().then_inc(s_y_evac, 1)

            split_units(0, 2)
            warm(ACT.Sqrt)
            for n in (5, 6):
                for h in range(TH):
                    if n == 5:
                        act.wait_ge(s_x_new, 4 + h + 1)
                    else:
                        act.wait_ge(s_norm_rows, 11 + h)
                    half_root(n, h, n - 5, X[:, h, :], HN[:, h, :])
            second_half(6)
            act.dma_start(p_rows, a["p_2"][0, 0].rearrange("(h p) n -> p h n", p=128)).then_inc(s_p_loaded, 16)
            split_T(5, uTH, "g_pre_2")
            split_unit(2)
            act.wait_ge(s_lora_mix, 1)
            fn(lora_t[0:64, :], lora[0:64, :], ACT.Tanh).then_inc(s_tanh_ready, 1)
            split_units(3, 18)
            act.wait_ge(s_ring_used, MOE_END + USED_RW)
            act.wait_ge(s_params_cols, 2)
            for j in range(16):
                t = fn(rwT[:, j, :], banks(0, 8, S)[:, j, :], ACT.Copy, scale=mu_keep[:, j:j + 1])
                if j % 2 == 1:
                    t.then_inc(s_rw_kept, 1)
                if j == 7:
                    split_unit(18)
            act.wait_ge(s_wl_done, 1)
            for j in range(4):
                fn(tk(sg, S)[:, j, :], banks(0, 2, S)[:, j, :], ACT.Sigmoid, bias=P("w0_2", j)).then_inc(s_wl_sig, 1)
            for j in range(4):
                fn(tk(rate, S)[:, j, :], banks(2, 2, S)[:, j, :], ACT.Sigmoid, bias=P("a0_2", j)).then_inc(s_wl_sig, 1)
            split_units(19, 22)
            act.wait_ge(s_wkv_cum, 1)
            fn(dec, cum, ACT.Exp, scale=-DECAY).then_inc(s_wkv_exp, 1)
            fn(dec_inv, cum, ACT.Exp, scale=DECAY).then_inc(s_wkv_exp, 1)
            fn(dec_prev, sg, ACT.Exp, scale=-DECAY).then_inc(s_wkv_exp, 1)
            split_units(22, 26)
            act.wait_ge(s_ring_used, MOE_END + USED_QK)
            fn(qk2[:, 0:4, :], banks(4, 2, S), ACT.Copy, scale=HD ** -0.5).then_inc(s_qkv_evac, 1)
            split_unit(26)
            act.wait_ge(s_head_sums, 1)
            fn(kk_inv, PS[:, 0:2, :].rearrange("p b n -> p (b n)"), ACT.Sqrt).then_inc(s_kk_sqrt, 1)
            split_units(27, 32)

            def moba_exp(g):
                act.wait_ge(s_moba_max, g + 1)
                for h in range(4 * g, 4 * g + 4):
                    for i, c in enumerate((slice(0, 128), slice(128, 384))):
                        fn(prob2[:, h, c], prob2[:, h, c], ACT.Exp, bias=mstat[:, 16 + 8 * i + h:17 + 8 * i + h],
                           accum_out=mstat[:, 32 + 8 * i + h:33 + 8 * i + h]).then_inc(s_moba_exp, 1)

            moba_exp(0)
            split_unit(32)
            act.wait_ge(s_ring_used, MOE_END + USED_VZ)
            fn(z_sig, PS[:, 6:8, :].rearrange("p b n -> p (b n)"), ACT.Sigmoid).then_inc(s_za_sig, 1)

            def moba_evac(g):
                act.wait_ge(s_moba_tr, g + 1)
                t = fn(prob2T[:, 4 * g:4 * g + 2, :], PS[:, 4:6, 0:384], ACT.Copy)
                if g:
                    t = fn(pT[:, 0, :].rearrange("p (h t) -> p h t", h=2), PS[:, 4:6, 384:512], ACT.Copy)
                t.then_inc(s_moba_pT, 1)

            moba_exp(1)
            moba_evac(0)
            moba_evac(1)
            act.wait_ge(s_a_evac, 2)
            fn(z_sig, buf(4, 1024), ACT.Sigmoid).then_inc(s_zb_sig, 1)
            act.wait_ge(s_ring_used, MOE_END + USED_GA)
            fn(gate_a, banks(0, 4, S), ACT.Sigmoid).then_inc(s_gate_evac, 1)
            act.wait_ge(s_ring_used, MOE_END + USED_GB)
            fn(gate_b, banks(0, 4, S), ACT.Sigmoid).then_inc(s_gate_evac, 1)
            warm(ACT.Sqrt)
            act.wait_ge(s_gn_sums, 2)
            fn(ystd, PS[:, 6:8, :].rearrange("p b n -> p (b n)"), ACT.Sqrt, scale=1.0 / HD, bias=eps[:, 2:3])\
                .then_inc(s_gn_std, 1)
            act.wait_ge(s_ring_used, MOE_END + USED_UP)
            fn(e_rows, PS[:, 0:4, :].rearrange("p (h b) n -> p h (b n)", h=TH), ACT.Copy).then_inc(s_e_evac, 1)
            split_units(33, 35)
            for b in range(4):
                act.wait_ge(s_merged_ready, b + 1)
                fn(tk(uTH[:, :], S)[:, 2 * b:2 * b + 2, :], merged[:, 2 * b:2 * b + 2, :], ACT.Copy).then_inc(s_t_high, 1)
            split_units(35, 42)
            for h in range(TH):
                if h == 0:
                    act.wait_ge(s_part_done, P_B_DONE + 3 + 1)
                else:
                    act.wait_ge(s_ring_used, MOE_END + USED_OUT)
                half_root(7, h, 1, PS[:, 4 + 2 * h:6 + 2 * h, :].rearrange("p b n -> p (b n)"), pg_sig[:, h, :])
            split_units(42, 43)
            split_T(6, uTH, None)
            split_units(43, U_END)
            warm(ACT.Sigmoid)
            for h in range(TH):
                if h == 0:
                    act.wait_ge(s_part_done, P_B_DONE + 3 + 2)
                else:
                    act.wait_ge(s_ring_used, MOE_END + USED_PG)
                fn(pg_sig[:, h, :], PS[:, 4 + 2 * h:6 + 2 * h, :].rearrange("p b n -> p (b n)"), ACT.Sigmoid)\
                    .then_inc(s_pg_sig, 1)

        @block.gpsimd
        def _(pool):
            done = [0]

            def step(ins):
                done[0] += 1
                ins.then_inc(s_pool_chain, 1)
                pool.wait_ge(s_pool_chain, done[0])

            nc.gpsimd.memset(eps[:, 0:1], 1e-5)
            nc.gpsimd.memset(eps[:, 1:2], 1e-6)
            nc.gpsimd.memset(eps[:, 2:3], 64e-5).then_inc(s_eps_set, 1)
            nc.gpsimd.memset(eps[:, 3:4], 0.0).then_inc(s_gu_free, 1)
            nc.gpsimd.memset(gate[:, :, N_EXP:], 0.0).then_inc(s_ov_sc, 1)
            nc.gpsimd.memset(slot_of[:, :, N_EXP:], -1.0)
            step(nc.gpsimd.memset(rbias[:, :], 1.0))
            pool.dma_start(rbias[0:32, :], a["rel_bias_2"]).then_inc(s_rbias_ready, 16)
            pool.wait_ge(s_vu_evac, 2)
            pool.wait_ge(s_late_loaded, 16)
            for g in range(4):
                src = u_T[:, g, :]
                for n in range(g + 1):
                    w, dst = 1 << n, win[n % 2]
                    nc.gpsimd.tensor_copy(dst[:, 0:w], src[:, 0:w])
                    step(nc.gpsimd.tensor_tensor(dst[:, w:], src[:, w:], src[:, 0:S - w], ALU.add))
                    src = dst
                step(nc.gpsimd.tensor_tensor(win[2], src, C("inv_count")[:, S * g:S * g + S], ALU.mult))
                nc.gpsimd.tensor_tensor(pooled[:, g, :], win[2], u_T[:, g, :], ALU.subtract).then_inc(s_pooled_ready, 1)
                pool.wait_ge(s_pooled_ready, g + 1)
            tt = nc.gpsimd.tensor_tensor
            pool.wait_ge(s_t_rest, 24)
            tt(HT, tk(uTH[:, :].bitcast(f32), S), tk(uTL[:, :].bitcast(f32), S), ALU.add).then_inc(s_norm_T, 1)
            pool.wait_ge(s_rw_mix, 4)
            step(tt(tk(kk, S), tk(rw_k, S), Pn("k_k_2", 4, S), ALU.mult))
            tt(kk_sq, kk, kk, ALU.mult).then_inc(s_kk_sq, 1)
            step(tt(tk(bon_in, S), tk(rT, S), Pn("r_k_2", 4, S), ALU.mult))
            pool.wait_ge(s_k2_ready, 1)
            tt(bon_in, bon_in, k2, ALU.mult).then_inc(s_bon_in, 1)
            pool.wait_ge(s_wkv_exp, 2)
            tt(rate, rate, dec_inv, ALU.mult).then_inc(s_wkv_T, 1)
            tt(kTl, k2, dec_inv, ALU.mult)
            pool.wait_ge(s_head_sums, 1)
            tt(r_dec, rT, dec, ALU.mult).then_inc(s_wkv_T, 1)
            pool.wait_ge(s_pairs_done, 3 + 6)
            nc.gpsimd.tensor_copy(tk(eye, L), C("eye64").unsqueeze(1).to_broadcast([128, NSET, L])).then_inc(s_eye_set, 1)
            pool.wait_ge(s_zb_sig, 1)
            step(tt(rw_z, rw_z, z_sig, ALU.mult))
            pool.wait_ge(s_bon_ready, 1)
            step(tt(tk(bonus, S), tk(bonus, S), Pn("ln_x_b_2", 4, S), ALU.add))
            step(tt(bonus, bonus, rw_z, ALU.mult))
            tt(tk(rw_z, S), tk(rw_z, S), Pn("ln_x_w_2", 4, S), ALU.mult).then_inc(s_bon_ready, 1)

        @block.vector
        def _(dve):
            v = nc.vector
            done = [0]

            def step(ins):
                done[0] += 1
                ins.then_inc(s_dve_chain, 1)
                dve.wait_ge(s_dve_chain, done[0])

            def rstd(n):
                dve.wait_ge(s_norm_std, n + 1)
                v.reciprocal(stat[:, 32 + 2 * n:34 + 2 * n], stat[:, 16 + 2 * n:18 + 2 * n]).then_inc(s_norm_rstd, 1)
                dve.wait_ge(s_norm_rstd, n + 1)

            def half_rstd(n, h):
                dve.wait_ge(s_norm_std, 2 * n - 3 + h)
                v.reciprocal(stat[:, 32 + 2 * n + h:33 + 2 * n + h], stat[:, 16 + 2 * n + h:17 + 2 * n + h]).then_inc(s_norm_rstd, 1)
                dve.wait_ge(s_norm_rstd, 2 * n - 3 + h)

            def norm_rows(n):
                half_rstd(n, 0)
                v.tensor_scalar(HN[:, 0, :], X[:, 0, :], stat[:, 32 + 2 * n:33 + 2 * n], None, ALU.mult).then_inc(s_norm_rows, 1)
                half_rstd(n, 1)

            def scale_half(n, dst, src):
                v.tensor_scalar(dst, src, stat[:, 32 + 2 * n:33 + 2 * n], None, ALU.mult).then_inc(s_norm_rows, 1)

            def evac_T(m, bank, dst, gain):
                dve.wait_ge(s_norm_tr, 2 * m - 1)
                if gain:
                    t = v.tensor_tensor(dst[:, 0:4, :], banks(bank, 2, S), Pn(gain, 4, S), ALU.mult)
                else:
                    t = v.tensor_copy(dst[:, 0:4, :], banks(bank, 2, S))
                t.then_inc(s_norm_T, 1)

            def rows_half(bank, h):
                return PS[:, bank + 2 * h:bank + 2 * h + 2, :].rearrange("p b n -> p (b n)")

            def add_residual(bank, h):
                v.tensor_tensor(X[:, h, :], rows_half(bank, h), X[:, h, :], ALU.add).then_inc(s_x_new, 1)

            def split_w(n):
                dve.wait_ge(s_w_high, n + 1)
                v.tensor_tensor(W_rest[n % 2][:, :], slot(n % PRE_SLOTS), W_high[n % 2][:, :].bitcast(f32), ALU.subtract)\
                    .then_inc(s_w_rest, 1)

            def split_T(m, high, rest, gain):
                hi, lo = tk(high[:, :].bitcast(f32), S), tk(rest[:, :], S)
                for b in range(4):
                    dve.wait_ge(s_t_high, 4 * m + b + 1)
                    if gain:
                        for k in (2 * b, 2 * b + 1):
                            t = v.scalar_tensor_tensor(lo[:, k, :], banks(0, 4, S)[:, k, :], P(gain, k), hi[:, k, :],
                                                       ALU.mult, ALU.subtract)
                    else:
                        t = v.tensor_tensor(lo[:, 2 * b:2 * b + 2, :], banks(b, 1, S), hi[:, 2 * b:2 * b + 2, :], ALU.subtract)
                    t.then_inc(s_t_rest, 1)

            def split_units(lo, hi):
                for u in range(lo, hi):
                    n, half = unit_chunk(u)
                    dve.wait_ge(s_w_high, NPRE + u + 1)
                    v.tensor_tensor(W2_rest[u % 2][:, :], slot(post_slot(n)[0], D * half, D * half + D),
                                    W2_high[u % 2][:, :].bitcast(f32), ALU.subtract).then_inc(s_w_rest, 1)

            rstd(0)
            scale_half(0, HN[:, 0, :], X[:, 0, :])
            dve.wait_ge(s_params_T, 1)
            v.tensor_copy(par[:, :], PS[:, 7, 0:128]).then_inc(s_params_cols, 1)
            dve.wait_ge(s_params_cols, 1)
            split_w(0)
            split_T(0, HTH, HTL, "g_mix")
            split_w(1)
            v.tensor_scalar(mu_keep[:, :], par[:, P_AT["mu_shift_2"]:P_AT["mu_shift_2"] + 16], -1.0, 1.0, ALU.mult, ALU.add)\
                .then_inc(s_params_cols, 1)
            rstd(1)
            scale_half(1, mem_rows[:, 0, :], mem_rows[:, 0, :])
            split_w(2)
            split_w(3)
            split_T(1, memH, memL, "g_mem_kv")
            split_w(4)
            dve.wait_ge(s_ring_used, C_VU)
            v.tensor_copy(qkT[:, 4:8, :], banks(6, 2, S)).then_inc(s_qkv_evac, 1)
            for n in range(5, 9):
                split_w(n)
            dve.wait_ge(s_ring_used, C_K)
            v.tensor_copy(u_T, banks(2, 2, S)).then_inc(s_vu_evac, 1)
            causal = C("causal").unsqueeze(1).to_broadcast([128, 4, 128])
            neg = C("neg_diag").unsqueeze(1).to_broadcast([128, 4, 128])
            diag = (slice(0, 128), slice(256, 384))
            dve.wait_ge(s_z_done, 1)
            v.tensor_copy(Z[:, 0:4, :], PS[:, 4:8, 0:384]).then_inc(s_z_copied, 1)
            split_w(9)

            def softplus(g):
                z, sp = Z[:, 4 * g:4 * g + 4, :], SP[:, 4 * g:4 * g + 4, :]
                dve.wait_ge(s_z_copied, 2)
                dve.wait_ge(s_z_ln, g + 1)
                step(v.scalar_tensor_tensor(sp, z, 0.0, sp, ALU.max, ALU.add))
                for c in diag:
                    t = v.tensor_tensor(sp[:, :, c], sp[:, :, c], causal, ALU.mult)
                t.then_inc(s_sp_ready, 1)
                for c in diag:
                    t = v.tensor_tensor(z[:, :, c], z[:, :, c], neg, ALU.add)
                step(t)

            def less_sums(g):
                z = Z[:, 4 * g:4 * g + 4, :]
                dve.wait_ge(s_rev_done, g + 1)
                v.tensor_tensor(z, z, PS[:, 0:4, 0:384], ALU.subtract).then_inc(s_arg_ready, 1)

            split_w(10)
            softplus(0)
            split_w(11)
            softplus(1)
            less_sums(0)
            split_w(12)
            dve.wait_ge(s_ring_used, C_V)
            v.tensor_copy(mkT[:, 4:8, :], banks(6, 2, S)).then_inc(s_qkv_evac, 1)
            less_sums(1)
            split_w(13)
            split_w(14)
            dve.wait_ge(s_pool_done, 1)
            dve.wait_ge(s_small_loaded, 16 * 6)
            for h in range(TH):
                v.tensor_tensor(HN[:, h, 512:], PS[:, 2 + h, :], scale_bc[:, :], ALU.mult).then_inc(s_pool_scaled, 1)
            dve.wait_ge(s_mix_std, 1)
            v.reciprocal(stat[:, 56:60], stat[:, 52:56]).then_inc(s_mix_rstd, 1)
            dve.wait_ge(s_mix_rstd, 1)
            for h in range(TH):
                t = v.tensor_scalar(HN[:, h, 512:], HN[:, h, 512:], stat[:, 58 + h:59 + h], None, ALU.mult)
            t.then_inc(s_norm_rows, 1)
            split_w(15)
            split_w(16)
            dve.wait_ge(s_ring_used, C_OUT)
            v.tensor_copy(mv_rows[:, 1, :].rearrange("p (b n) -> p b n", b=2), PS[:, 6:8, :]).then_inc(s_qkv_evac, 1)
            split_T(2, HTH, HTL, "g_sb_out")
            for n in range(17, 21):
                split_w(n)
            dve.wait_ge(s_ring_used, C_MQ)
            for h in range(TH):
                add_residual(4, h)
            norm_rows(3)
            split_T(3, HTH, HTL, "g_mem_q")
            for n in range(21, 25):
                split_w(n)
            dve.wait_ge(s_ring_used, C_MO)
            v.tensor_scalar(mqT[:, 4:8, :], banks(6, 2, S), 256 ** -0.5, None, ALU.mult).then_inc(s_memq_evac, 1)
            for g in range(2):
                dve.wait_ge(s_score_done, g + 1)
                step(v.reduce_max(mstat[:, 4 * g:4 * g + 4], banks(2 * g, 2, S), AX))
                v.tensor_scalar(mstat[:, 8 + 4 * g:12 + 4 * g], mstat[:, 4 * g:4 * g + 4], -1.0, None, ALU.mult)\
                    .then_inc(s_score_max, 1)
            for g in range(2):
                dve.wait_ge(s_p_exp, 4 * (g + 1))
                step(v.reciprocal(mstat[:, 24 + 4 * g:28 + 4 * g], mstat[:, 16 + 4 * g:20 + 4 * g]))
                v.tensor_tensor(prob[:, 4 * g:4 * g + 4, :], prob[:, 4 * g:4 * g + 4, :],
                                mstat[:, 24 + 4 * g:28 + 4 * g].unsqueeze(2).to_broadcast([128, 4, S]), ALU.mult)\
                    .then_inc(s_p_ready, 1)
            split_w(25)
            dve.wait_ge(s_tr_p, 2)
            v.tensor_copy(probT[:, 4:8, :], banks(6, 2, S)).then_inc(s_pT_evac, 1)
            split_T(4, HTH, HTL, None)
            for n in (26, 27):
                split_w(n)
            dve.wait_ge(s_part_done, 1)
            add_residual(4, 0)
            dve.wait_ge(s_ring_used, NPRE)
            add_residual(4, 1)
            norm_rows(4)
            evac_T(5, 4, HT, "g_ffn")
            dve.wait_ge(s_logits_done, 1)
            step(v.tensor_copy(lg[:, :, :], PS[:, 0, 0:64].rearrange("p (h e) -> p h e", h=TH)))
            for h in range(TH):
                t = v.max(top8[:, h, :], lg[:, h, :])
            step(t)
            for h in range(TH):
                v.tensor_scalar(stat[:, 60 + h:61 + h], top8[:, h, 0:1], -1.0, None, ALU.mult)
                t = v.max_index(idx8[:, h, :], top8[:, h, :], lg[:, h, :])
            t.then_inc(s_top_ready, 1)
            dve.wait_ge(s_top_ready, 1)
            step(v.tensor_copy(idxf[:, :, :], idx8[:, :, :]))
            for h in range(TH):
                t = v.tensor_tensor(hot[:, h, :, :], C("iota32").unsqueeze(1).to_broadcast([128, 4, N_EXP]),
                                    idxf[:, h, 0:4].unsqueeze(2).to_broadcast([128, 4, N_EXP]), ALU.is_equal)
            step(t)
            v.tensor_reduce(mask[:, :, :], hot[:, :, :, :].rearrange("p h k e -> p h e k"), AX, ALU.add)\
                .then_inc(s_mask_ready, 1)
            dve.wait_ge(s_top_exp, 1)
            dve.wait_ge(s_mask_ready, 1)
            step(v.tensor_tensor(lg[:, :, :], lg[:, :, :], mask[:, :, :], ALU.mult))
            step(v.tensor_reduce(stat[:, 62:64], lg[:, :, :], AX, ALU.add))
            step(v.reciprocal(stat[:, 64:66], stat[:, 62:64]))
            v.tensor_tensor(gate[:, :, 0:N_EXP], lg[:, :, :], stat[:, 64:66].unsqueeze(2).to_broadcast([128, TH, N_EXP]),
                            ALU.mult).then_inc(s_gates_ready, 1)
            dve.wait_ge(s_rank_done, 1)
            step(v.scalar_tensor_tensor(slot_of[:, :, 0:N_EXP], PS[:, 1, 0:64].rearrange("p (h e) -> p h e", h=TH), 1.0,
                                        mask[:, :, :], ALU.add, ALU.mult))
            step(v.tensor_scalar(slot_of[:, :, 0:N_EXP], slot_of[:, :, 0:N_EXP], -1.0, None, ALU.add))
            dve.wait_ge(s_ov_sc, 1)

            def set_pick(col):
                for h in range(TH):
                    t = v.tensor_scalar(pick[:, h, :], C("iota")[:, 0:CAP], col(h), None, ALU.is_equal)
                return t

            def set_gpick(col, e):
                for h in range(TH):
                    t = v.tensor_scalar(gpick[:, h, :], C("iota"), col(h), gate[:, h, bass.ds(e, 1)], ALU.is_equal,
                                        ALU.mult)
                return t

            def copy_xT():
                return v.tensor_tensor(xT_e, banks(0, 1, CAP), Pn("g_ffn", KT, CAP), ALU.mult)

            def clip_gate():
                return v.tensor_scalar(g7, PS[:, 2, :], 7.0, None, ALU.min)

            def clip_up():
                return v.tensor_scalar(u7, PS[:, 3, :], 7.0, -7.0, ALU.min, ALU.max)

            def up_gate():
                return v.scalar_tensor_tensor(gu, u7, 1.0, g7, ALU.add, ALU.mult)

            def activate():
                return v.tensor_tensor(act_e, gu, sig, ALU.mult)

            set_pick(lambda h: slot_of[:, h, 0:1]).then_inc(s_pe_ready, 1)
            step(v.reduce_max(stat[0:1, 66:67], PS[0:1, 1, 64:96], AX))
            v.tensor_scalar(flag[0:1, 0:1], stat[0:1, 66:67], float(CAP), None, ALU.is_gt).then_inc(s_flag_ready, 1)
            dve.wait_ge(s_gates_ready, 1)
            for h in range(TH):
                t = v.tensor_scalar(gpick[:, h, :], C("iota"), slot_of[:, h, 0:1], gate[:, h, 0:1], ALU.is_equal, ALU.mult)
            t.then_inc(s_gp_ready, 1)
            dve.wait_ge(s_gT_done, 1)
            v.tensor_copy(gT[0:N_EXP, :], PS[0:N_EXP, 2, 0:256]).then_inc(s_gT_evac, 1)
            dve.wait_ge(s_gathered, 1)
            copy_xT().then_inc(s_xT_ready, 1)

            with dve.Fori(0, N_EXP) as e:
                dve.wait_ge(s_gathered, e + 1)
                set_pick(lambda h: slot_of[:, h, bass.ds(e + 1, 1)]).then_inc(s_pe_ready, 1)
                dve.wait_ge(s_ring_used, e * PER + (NPRE + 8))
                clip_gate().then_inc(s_sig_in, 1)
                clip_up().then_inc(s_gu_free, 1)
                dve.wait_ge(s_gu_free, e + 2)
                up_gate().then_inc(s_gu_made, 1)
                dve.wait_ge(s_gu_made, e + 1)
                dve.wait_ge(s_sig_out, e + 1)
                activate().then_inc(s_act_ready, 1)
                dve.wait_ge(s_gathered, e + 2)
                copy_xT().then_inc(s_xT_ready, 1)
                dve.wait_ge(s_gpt_done, e + 1)
                set_gpick(lambda h: slot_of[:, h, bass.ds(e + 1, 1)], e + 1).then_inc(s_gp_ready, 1)
            dve.wait_ge(s_flag_ready, 1)
            over = v.value_load(flag[0:1, 0:1], min_val=0, max_val=1)
            with v.If(over > 0):
                NB = N_BLK - 1
                dve.wait_ge(s_scattered, N_EXP)
                with dve.Fori(0, N_EXP) as e:
                    for b in range(NB):
                        dve.wait_ge(s_ov_sc, e * NB + (b + 1))
                        for h in range(TH):
                            t = v.tensor_scalar(ov_slot[:, h:h + 1], slot_of[:, h, bass.ds(e, 1)], -float(CAP * (b + 1)), None,
                                                ALU.add)
                        t.then_inc(s_ov_base, 1)
                        dve.wait_ge(s_ov_base, e * NB + (b + 1))
                        set_pick(lambda h: ov_slot[:, h:h + 1])
                        set_gpick(lambda h: ov_slot[:, h:h + 1], e).then_inc(s_pe_ready, 1)
                        dve.wait_ge(s_gathered, e * NB + (N_EXP + 1 + b + 1))
                        copy_xT().then_inc(s_xT_ready, 1)
                        dve.wait_ge(s_ov_up, e * NB + (b + 1))
                        clip_gate().then_inc(s_sig_in, 1)
                        clip_up().then_inc(s_gu_free, 1)
                        dve.wait_ge(s_gu_free, e * NB + (N_EXP + 1 + b + 1))
                        up_gate().then_inc(s_gu_made, 1)
                        dve.wait_ge(s_gu_made, e * NB + (N_EXP + b + 1))
                        dve.wait_ge(s_sig_out, e * NB + (N_EXP + b + 1))
                        activate().then_inc(s_act_ready, 1)
                dve.wait_ge(s_ov_sc, N_EXP * NB + 1)
            dve.wait_ge(s_scattered, N_EXP)
            for h in range(TH):
                add_residual(4, h)

            dve.wait_ge(s_g_loaded, 32)
            for h in range(TH):
                half_rstd(5, h)
                v.scalar_tensor_tensor(X[:, h, :], X[:, h, :], stat[:, 42 + h:43 + h], g_final, ALU.mult, ALU.mult)\
                    .then_inc(s_norm_rows, 1)
            norm_rows(6)
            split_units(0, 2)
            split_T(5, uTH, uTL, "g_pre_2")
            split_units(2, 3)
            dve.wait_ge(s_ring_used, MOE_END + 1)
            v.tensor_copy(lora, PS[:, 4, 0:256]).then_inc(s_lora_evac, 1)
            dve.wait_ge(s_lora_evac, 1)
            v.tensor_tensor(lora_d[:, 1:], lora[:, 0:S - 1], lora[:, 1:], ALU.subtract)
            step(v.tensor_scalar(lora_d[:, 0:1], lora[:, 0:1], -1.0, None, ALU.mult))
            v.scalar_tensor_tensor(lora, lora_d, P("mu_shift_2", 16), lora, ALU.mult, ALU.add).then_inc(s_lora_mix, 1)
            split_units(3, 18)
            for j in range(16):
                if j == 8:
                    split_units(18, 19)
                if j % 2 == 0:
                    dve.wait_ge(s_rw_kept, j // 2 + 1)
                t = v.scalar_tensor_tensor(rwT[:, j, 1:], banks(0, 8, S)[:, j, 0:S - 1], P("mu_shift_2", j), rwT[:, j, 1:],
                                           ALU.mult, ALU.add)
                if j % 2 == 1:
                    t.then_inc(s_rw_mix, 1)
            split_units(19, 21)
            dve.wait_ge(s_wl_sig, 8)
            step(v.tensor_tensor_scan(cum, C("chunk_reset"), sg, 0.0, ALU.mult, ALU.add))
            v.tensor_tensor(sg, cum, sg, ALU.subtract).then_inc(s_wkv_cum, 1)
            split_units(21, 22)
            step(v.scalar_tensor_tensor(tk(k2, S), tk(rate, S), 1.0, Pn("k_a_2", 4, S), ALU.subtract, ALU.mult))
            dve.wait_ge(s_rw_mix, 8)
            v.scalar_tensor_tensor(k2, k2, 1.0, rw_k, ALU.add, ALU.mult).then_inc(s_k2_ready, 1)
            split_units(22, 26)
            dve.wait_ge(s_ring_used, MOE_END + USED_QK)
            v.tensor_copy(qk2[:, 4:8, :], banks(6, 2, S)).then_inc(s_qkv_evac, 1)
            split_units(26, 27)
            dve.wait_ge(s_head_sums, 2)
            v.tensor_tensor(bonus, PS[:, 2:4, :].rearrange("p b n -> p (b n)"), rw_v, ALU.mult).then_inc(s_bon_ready, 1)
            dve.wait_ge(s_kk_sqrt, 1)
            v.tensor_scalar(kk_inv, kk_inv, 1e-12, None, ALU.max).then_inc(s_kk_max, 1)
            split_units(27, 28)
            dve.wait_ge(s_wkv_exp, 3)
            v.tensor_copy(dec_end[:, :], tk(dec, L)[:, :, L - 1])
            split_units(28, 30)
            dve.wait_ge(s_bias_read, 32)

            def moba_bias(g, u):
                hs = slice(4 * g, 4 * g + 4)
                dve.wait_ge(s_moba_s, g + 1)
                for c, b in ((0, 0), (1, 1), (2, 0)):
                    t = v.tensor_tensor(prob2[:, hs, 128 * c:128 * c + 128], PS[:, 0:4, 128 * c:128 * c + 128],
                                        bias[:, hs, b, :], ALU.add)
                t.then_inc(s_moba_read, 1)
                split_units(u, u + 1)
                dve.wait_ge(s_moba_read, g + 1)
                v.reduce_max(mstat[:, 4 * g:4 * g + 4], prob2[:, hs, 0:128], AX)
                step(v.reduce_max(mstat[:, 8 + 4 * g:12 + 4 * g], prob2[:, hs, 128:384], AX))
                v.tensor_scalar(halves_of(16, g), halves_of(0, g), -1.0, None, ALU.mult).then_inc(s_moba_max, 1)

            def halves_of(lo, g):
                return mstat[:, lo:lo + 16].rearrange("p (i h) -> p i h", i=2)[:, :, 4 * g:4 * g + 4]

            def moba_probs(g):
                hs = slice(4 * g, 4 * g + 4)
                dve.wait_ge(s_moba_exp, 8 * (g + 1))
                step(v.reciprocal(halves_of(48, g), halves_of(32, g)))
                v.tensor_tensor(prob2[:, hs, 0:128], prob2[:, hs, 0:128],
                                mstat[:, 48 + 4 * g:52 + 4 * g].unsqueeze(2).to_broadcast([128, 4, 128]), ALU.mult)
                v.tensor_tensor(prob2[:, hs, 128:384], prob2[:, hs, 128:384],
                                mstat[:, 56 + 4 * g:60 + 4 * g].unsqueeze(2).to_broadcast([128, 4, 256]), ALU.mult)\
                    .then_inc(s_moba_p, 1)

            def moba_evac(g):
                dve.wait_ge(s_moba_tr, g + 1)
                t = v.tensor_copy(prob2T[:, 4 * g + 2:4 * g + 4, :], PS[:, 6:8, 0:384])
                if g:
                    t = v.tensor_copy(pT[:, 1, :].rearrange("p (h t) -> p h t", h=2), PS[:, 6:8, 384:512])
                t.then_inc(s_moba_pT, 1)

            moba_bias(0, 30)
            split_units(31, 32)
            moba_bias(1, 32)
            dve.wait_ge(s_ring_used, MOE_END + USED_VZ)
            v.tensor_copy(v2, PS[:, 4:6, :]).then_inc(s_a_evac, 1)
            dve.wait_ge(s_za_sig, 1)
            v.tensor_tensor(za, banks(6, 2, S), tk(z_sig, S), ALU.mult).then_inc(s_a_evac, 1)
            def invert(lo, hi):
                dve.wait_ge(s_kk_max, 1)
                for j in range(lo, hi):
                    t = v.reciprocal(tk(kk_inv, S)[:, j, :], tk(kk_inv, S)[:, j, :])
                return t

            moba_probs(0)
            moba_probs(1)
            invert(0, 2)
            moba_evac(0)
            step(invert(2, 4))
            moba_evac(1)
            step(v.tensor_tensor(kk, kk, kk_inv, ALU.mult))
            v.scalar_tensor_tensor(aT, kk, -1.0, dec_prev, ALU.mult, ALU.mult)
            dve.wait_ge(s_wkv_T, 1)
            v.tensor_tensor(bT, rate, kk, ALU.mult).then_inc(s_wkv_T, 1)

            def flat(bank):
                return PS[:, bank:bank + 2, :].rearrange("p b n -> p (b n)")

            def half(x, hf):
                return tk(x, L)[:, NSET // 2 * hf:NSET // 2 * hf + NSET // 2, :]

            def masked(name):
                return C(name).unsqueeze(1).to_broadcast([128, NSET // 2, L])

            def wide(bank):
                return PS[:, bank:bank + 2, :].rearrange("p b (n a t) -> p a (b n) t", a=2, t=L)

            dve.wait_ge(s_moba_o, 1)
            v.tensor_tensor(ya, banks(4, 2, S), za, ALU.mult).then_inc(s_ya_ready, 1)
            for i, (dst, bank) in enumerate(((v_tok, 6), (b_tok, 4), (k_tok, 6))):
                dve.wait_ge(s_pairs_done, i + 1)
                v.tensor_copy(dst, flat(bank)).then_inc(s_rows_evac, 1)
            for hf in range(2):
                dve.wait_ge(s_pairs_done, 3 + hf + 1)
                v.tensor_tensor(half(a0, hf), banks(4 + hf, 1, L), masked("low_diag"), ALU.mult).then_inc(s_mat_evac, 1)
            dve.wait_ge(s_mat_evac, 2)
            for hf in range(2):
                v.tensor_tensor(half(F, hf), half(a0, hf), masked("eye64"), ALU.add)
                dve.wait_ge(s_pairs_done, 3 + 2 + hf + 1)
                ps = wide(6 - 2 * hf)
                v.tensor_tensor(half(b0, hf), ps[:, 0], masked("up_diag"), ALU.mult).then_inc(s_mat_evac, 1)
                v.tensor_tensor(half(offT, hf), ps[:, 0], masked("up_off"), ALU.mult).then_inc(s_mat_evac, 1)
                v.tensor_tensor(half(rbT, hf), ps[:, 1], masked("up_incl"), ALU.mult).then_inc(s_mat_evac, 1)
            for hf in range(2):
                dve.wait_ge(s_pairs_done, 3 + 4 + hf + 1)
                ps = wide(6 - 2 * hf)
                v.tensor_tensor(half(akT, hf), ps[:, 0], masked("up_strict"), ALU.mult)
                v.tensor_tensor(half(rkT, hf), ps[:, 1], masked("up_incl"), ALU.mult).then_inc(s_sol_ready, 1)
            for i, (x, y, res) in enumerate(SOLVE):
                for hf in range(2):
                    dve.wait_ge(s_sol_done, 2 * i + hf + 1)
                    bank = 6 - 2 * hf
                    for q, (dst, plus) in enumerate(res):
                        ps = wide(bank)[:, q] if len(res) == 2 else banks(bank, 1, L)
                        if plus is None:
                            t = v.tensor_copy(half(dst, hf), ps)
                        else:
                            t = v.tensor_tensor(half(dst, hf), ps, half(plus, hf), ALU.add)
                    t.then_inc(s_sol_evac, 1)
            for c in range(NCH):
                for g in range(2):
                    dve.wait_ge(s_rec_x, 2 * c + g + 1)
                    v.tensor_copy(rec_rhs[:, 2 * g:2 * g + 2, :], tk(PS[:, 4 + g, 0:128], L)).then_inc(s_rec_xe, 1)
                for g in range(2):
                    dve.wait_ge(s_rec_sa, 2 * c + g + 1)
                    v.tensor_copy(rec_sa[:, 2 * g:2 * g + 2, :], tk(PS[:, 4 + g, 128:256], L)).then_inc(s_rec_sae, 1)
                for g in range(2):
                    if c < NCH - 1:
                        js = slice(2 * g, 2 * g + 2)
                        end = dec_end[:, :].rearrange("p (j c) -> p j c", c=NCH)[:, js, c].unsqueeze(2).to_broadcast([128, 2, HD])
                        new, old, ps = state[(c + 1) % 2][:, js, :], state[c % 2][:, js, :], tk(PS[:, 4 + g, 256:384], L)
                        dve.wait_ge(s_rec_s, 2 * c + g + 1)
                        if c:
                            step(v.tensor_tensor(new, ps, old, ALU.add))
                            v.tensor_tensor(new, new, end, ALU.mult).then_inc(s_rec_state, 1)
                        else:
                            v.tensor_tensor(new, ps, end, ALU.mult).then_inc(s_rec_state, 1)
            dve.wait_ge(s_y_psum, NCH)
            v.tensor_copy(yT, flat(6)).then_inc(s_yT_evac, 1)
            dve.wait_ge(s_gate_evac, 2)
            dve.wait_ge(s_ring_used, MOE_END + USED_PA)
            v.tensor_tensor(gate_a, gate_a, banks(0, 4, S), ALU.mult).then_inc(s_pa_used, 1)
            dve.wait_ge(s_yT_evac, 1)
            dve.wait_ge(s_gn_sums, 1)
            step(v.scalar_tensor_tensor(yT, flat(4), -1.0 / HD, yT, ALU.mult, ALU.add))
            v.tensor_tensor(ysq, yT, yT, ALU.mult).then_inc(s_gn_sq, 1)
            dve.wait_ge(s_bon_ready, 2)
            step(v.tensor_tensor(yT, yT, rw_z, ALU.mult))
            dve.wait_ge(s_gn_std, 1)
            for j in range(4):
                y, d = yb[:, j, :], tk(ystd, S)[:, j, :]
                step(v.reciprocal(d, d))
                step(v.tensor_tensor(y, y, d, ALU.mult))
                v.tensor_tensor(y, y, tk(bonus, S)[:, j, :], ALU.add).then_inc(s_yb_ready, 1)
            split_units(33, 35)
            dve.wait_ge(s_pa_used, 1)

            def merge_rest(b):
                ks = slice(2 * b, 2 * b + 2)
                dve.wait_ge(s_t_high, 24 + b + 1)
                v.tensor_tensor(tk(uTL[:, :], S)[:, ks, :], merged[:, ks, :], tk(uTH[:, :].bitcast(f32), S)[:, ks, :],
                                ALU.subtract).then_inc(s_t_rest, 1)

            for b in range(4):
                ks = slice(2 * b, 2 * b + 2)
                if b < 3:
                    dve.wait_ge(s_part_done, P_B_DONE + b + 1)
                else:
                    dve.wait_ge(s_ring_used, MOE_END + USED_PB)
                step(v.tensor_tensor(gate_b[:, ks, :], gate_b[:, ks, :], banks(b, 1, S), ALU.mult))
                v.tensor_tensor(merged[:, ks, :], gate_a[:, ks, :], gate_b[:, ks, :], ALU.add).then_inc(s_merged_ready, 1)
                if b:
                    merge_rest(b - 1)
            merge_rest(3)
            split_units(35, 42)
            for h in range(TH):
                dve.wait_ge(s_norm_sq, 13 + h)
                step(v.tensor_tensor(HN[:, h, :], rows_half(4, h), g_post, ALU.mult))
                half_rstd(7, h)
                v.scalar_tensor_tensor(X[:, h, :], HN[:, h, :], stat[:, 46 + h:47 + h], X[:, h, :], ALU.mult, ALU.add)\
                    .then_inc(s_h2_ready, 1)
            split_units(42, 43)
            split_T(7, uTH, uTL, None)
            split_units(43, U_END)
            for h in range(TH):
                dve.wait_ge(s_pg_sig, h + 1)
                dve.wait_ge(s_h2_ready, 2)
                dve.wait_ge(s_e_evac, 1)
                step(v.tensor_tensor(HN[:, h, :], pg_sig[:, h, :], e_rows[:, h, :], ALU.mult))
                v.tensor_tensor(HN[:, h, :], HN[:, h, :], X[:, h, :], ALU.add).then_inc(s_out_ready, 1)



_INS = ["x", "mem", "w_in", "w_pool", "pool_scale", "w_out", "w_mem_q", "w_mem_kv", "w_mem_o", "w_router", "b_router",
        "w_expert_in", "b_expert_in", "w_expert_out", "b_expert_out", "g_final", "p_2", "w_in_2", "rel_bias_2",
        "w_up_2", "a_up_2", "p_a_2", "p_b_2", "w_out_2", "g_post_2", "w_ple_up_2", "w_ple_gate_2"]


def kernel(**inputs):
    import numpy as _np
    import concourse.bacc as _bacc
    from concourse import mybir as _mybir
    from concourse.bass_utils import run_bass_kernel_spmd as _run

    nc = _bacc.Bacc("TRN2", target_bir_lowering=False, num_devices=1)
    given = {n: _np.ascontiguousarray(inputs[n]) for n in _INS}
    given["params"] = _np.concatenate([_np.asarray(inputs[n]).reshape(-1, 128) for n, _ in PARAMS]
                                      + [_np.zeros((128 - P_ROWS, 128), _np.float32)], axis=0)
    given["consts"] = constants()
    arrays, args = {}, {}
    for name, v in given.items():
        arrays[f"in_{name}_dram"] = v
        args[name] = nc.dram_tensor(f"in_{name}_dram", v.shape, _mybir.dt.from_np(v.dtype), kind="ExternalInput").ap()
    out = nc.dram_tensor("out_0_dram", (1, S, D), _mybir.dt.float32, kind="ExternalOutput").ap()
    two_blocks(nc, args, out)
    r = _run(nc, [arrays], core_ids=[0])
    return r.results[0]["out_0_dram"]
```
